# Optimizing a Trainium2 kernel written in Bass

```python
import math
import jax, jax.numpy as jnp
from jax import lax
import numpy as np

D_MODEL = 1024
BATCH = 1
SEQ = 256
DEPTH = 1
DEC_BATCH = 1
DEC_SEQ = 512
PAST_LEN = 128

GRID_W = 64
N_Q_HEADS = 8
N_KV_HEADS = 2
HEAD_DIM = 64
ATTN_W = N_Q_HEADS * HEAD_DIM
KV_W = N_KV_HEADS * HEAD_DIM
ROPE_THETA = 10000.0
Q_BLOCK = 128
SSD_HEADS = 8
SSD_HEAD_DIM = 64
D_INNER = SSD_HEADS * SSD_HEAD_DIM
SSD_GROUPS = 2
D_STATE = 128
D_CONV = 5
CHUNK = 128
CONV_CH = D_INNER + 2 * SSD_GROUPS * D_STATE
MIX_W = ATTN_W + D_INNER
_K0 = ATTN_W
_V0 = _K0 + KV_W
_Z0 = _V0 + KV_W
_XBC0 = _Z0 + D_INNER
_DT0 = _XBC0 + CONV_CH
IN_COLS = _DT0 + 2 * SSD_HEADS
N_EXPERTS = 16
CAPACITY_FACTOR = 2
D_EXPERT = 1024
PLE_DIM = 256
DN_ALPHA = (2.0 * DEPTH) ** 0.25
DN_BETA = (8.0 * DEPTH) ** -0.25
NORM_EPS = 1e-6
LN_EPS = 1e-5

kernel_name = "hymba_gqa_ssd_expert_choice_encoder"

def _rms_norm(x, w):
    xf = x.astype(jnp.float32)
    y = xf * lax.rsqrt(jnp.mean(xf * xf, axis=-1, keepdims=True) + NORM_EPS)
    return (y * w.astype(jnp.float32)).astype(x.dtype)

def _layer_norm(x, g, b):
    xf = x.astype(jnp.float32)
    xc = xf - jnp.mean(xf, axis=-1, keepdims=True)
    y = xc * lax.rsqrt(jnp.mean(xc * xc, axis=-1, keepdims=True) + LN_EPS)
    return (y * g.astype(jnp.float32) + b.astype(jnp.float32)).astype(x.dtype)

def _axial_rope_tables(seq_len):
    rows = seq_len // GRID_W
    row_id = jnp.broadcast_to(jnp.arange(rows)[:, None], (rows, GRID_W)).reshape(seq_len)
    col_id = jnp.broadcast_to(jnp.arange(GRID_W)[None, :], (rows, GRID_W)).reshape(seq_len)
    pos = jnp.stack([row_id, col_id], axis=-1).astype(jnp.float32)
    n_freq = HEAD_DIM // 4
    inv_freq = ROPE_THETA ** (-jnp.arange(n_freq, dtype=jnp.float32) / n_freq)
    ang = pos[:, :, None] * inv_freq
    return jnp.cos(ang), jnp.sin(ang)

def _apply_axial_rope(x, cos, sin):
    b, s, h, d = x.shape
    xr = x.astype(jnp.float32).reshape(b, s, h, 2, 2, d // 4)
    x1, x2 = xr[..., 0, :], xr[..., 1, :]
    c = cos[None, :, None]
    sn = sin[None, :, None]
    out = jnp.stack([x1 * c - x2 * sn, x1 * sn + x2 * c], axis=-2)
    return out.reshape(b, s, h, d).astype(x.dtype)

def _attention(q, k, v):
    b, s, _, hd = q.shape
    grp = N_Q_HEADS // N_KV_HEADS
    nb = s // Q_BLOCK
    qb = (q * (hd ** -0.5)).reshape(b, nb, Q_BLOCK, N_KV_HEADS, grp, hd).transpose(1, 0, 2, 3, 4, 5)

    def attend_block(q_blk):
        sc = jnp.einsum("bqkgd,bskd->bkgqs", q_blk, k).astype(jnp.float32)
        pr = jax.nn.softmax(sc, axis=-1).astype(v.dtype)
        return jnp.einsum("bkgqs,bskd->bqkgd", pr, v)

    o = lax.map(attend_block, qb)
    return o.transpose(1, 0, 2, 3, 4, 5).reshape(b, s, N_Q_HEADS * hd)

def _dwconv_centred(u, w, bias):
    y = lax.conv_general_dilated(
        u, w[:, None, :].astype(u.dtype), window_strides=(1,),
        padding=((D_CONV // 2, D_CONV // 2),),
        dimension_numbers=("NWC", "WIO", "NWC"),
        feature_group_count=u.shape[-1])
    return y + bias.astype(u.dtype)

def _ssd_chunked(xdt, a, bm, cm):
    b, L, H, P = xdt.shape
    G, N = bm.shape[2], bm.shape[3]
    R = H // G
    c = L // CHUNK
    x = xdt.reshape(b, c, CHUNK, G, R, P)
    a = a.reshape(b, c, CHUNK, G, R).transpose(0, 3, 4, 1, 2)
    bc = bm.reshape(b, c, CHUNK, G, N)
    cc = cm.reshape(b, c, CHUNK, G, N)
    a_cum = jnp.cumsum(a, axis=-1)
    lower = jnp.tril(jnp.ones((CHUNK, CHUNK), dtype=bool))
    seg = a_cum[..., :, None] - a_cum[..., None, :]
    decay_in = jnp.exp(jnp.where(lower, seg, -jnp.inf))
    cb = jnp.einsum("bclgn,bcsgn->bgcls", cc, bc)
    y_diag = jnp.einsum("bgcls,bgrcls,bcsgrp->bclgrp", cb, decay_in, x)
    decay_states = jnp.exp(a_cum[..., -1:] - a_cum)
    states = jnp.einsum("bclgn,bgrcl,bclgrp->bcgrpn", bc, decay_states, x)
    chunk_decay = jnp.exp(a_cum[..., -1])

    def step(h, inp):
        st, dec = inp
        return h * dec[..., None, None] + st, h

    h0 = jnp.zeros((b, G, R, P, N), dtype=x.dtype)
    _, prev = lax.scan(step, h0, (states.transpose(1, 0, 2, 3, 4, 5), chunk_decay.transpose(3, 0, 1, 2)))
    y_off = jnp.einsum("bclgn,cbgrpn,bgrcl->bclgrp", cc, prev, jnp.exp(a_cum))
    return (y_diag + y_off).reshape(b, L, H, P)

def _flip_seq(t):
    return jnp.flip(t, axis=1)

def _ssd_mixer(z, xbc, dt_raw, conv_w, conv_b, dt_bias, a_log, d_skip, norm_w):
    b, s, _ = z.shape
    xbc = jax.nn.silu(_dwconv_centred(xbc, conv_w, conv_b)).astype(jnp.float32)
    xs = xbc[..., :D_INNER].reshape(b, s, SSD_HEADS, SSD_HEAD_DIM)
    bm = xbc[..., D_INNER:D_INNER + SSD_GROUPS * D_STATE].reshape(b, s, SSD_GROUPS, D_STATE)
    cm = xbc[..., D_INNER + SSD_GROUPS * D_STATE:].reshape(b, s, SSD_GROUPS, D_STATE)
    dt = jax.nn.softplus(dt_raw.astype(jnp.float32).reshape(b, s, 2, SSD_HEADS) + dt_bias.astype(jnp.float32))
    a = dt * (-jnp.exp(a_log.astype(jnp.float32)))
    y_fwd = _ssd_chunked(xs * dt[:, :, 0, :, None], a[:, :, 0], bm, cm)
    y_bwd = _flip_seq(_ssd_chunked(_flip_seq(xs * dt[:, :, 1, :, None]), _flip_seq(a[:, :, 1]),
                                   _flip_seq(bm), _flip_seq(cm)))
    y = y_fwd + y_bwd + d_skip.astype(jnp.float32)[:, None] * xs
    y = y.reshape(b, s, D_INNER) * jax.nn.silu(z.astype(jnp.float32))
    y = y.reshape(b, s, SSD_GROUPS, D_INNER // SSD_GROUPS)
    y = y * lax.rsqrt(jnp.mean(y * y, axis=-1, keepdims=True) + NORM_EPS)
    y = y.reshape(b, s, D_INNER) * norm_w.astype(jnp.float32)
    return y.astype(z.dtype)

def _expert_choice(h, w_router, w_gate, w_up, w_down):
    n_tok, d = h.shape
    cap = CAPACITY_FACTOR * n_tok // N_EXPERTS
    aff = jax.nn.softmax((h @ w_router).astype(jnp.float32), axis=-1)
    gate, idx = lax.top_k(aff.T, cap)
    xe = h[idx]
    hid = jax.nn.silu(jnp.einsum("ecd,edf->ecf", xe, w_gate)) * jnp.einsum("ecd,edf->ecf", xe, w_up)
    ye = jnp.einsum("ecf,efd->ecd", hid, w_down) * gate[..., None].astype(h.dtype)
    return jnp.zeros_like(h).at[idx.reshape(-1)].add(ye.reshape(-1, d))

def _layer(x, p, w_in, q_norm_w, k_norm_w, conv_w, conv_b, dt_bias, a_log, d_skip, ssd_norm_w,
           w_out, ln1_g, ln1_b, w_router, w_e_gate, w_e_up, w_e_down, w_ple_gate, b_ple_gate,
           w_ple, ln2_g, ln2_b):
    b, s, d = x.shape
    proj = x @ w_in
    q = proj[..., :_K0].reshape(b, s, N_Q_HEADS, HEAD_DIM)
    k = proj[..., _K0:_V0].reshape(b, s, N_KV_HEADS, HEAD_DIM)
    v = proj[..., _V0:_Z0].reshape(b, s, N_KV_HEADS, HEAD_DIM)
    z = proj[..., _Z0:_XBC0]
    xbc = proj[..., _XBC0:_DT0]
    dt_raw = proj[..., _DT0:]
    cos, sin = _axial_rope_tables(s)
    q = _apply_axial_rope(_rms_norm(q, q_norm_w), cos, sin)
    k = _apply_axial_rope(_rms_norm(k, k_norm_w), cos, sin)
    attn_out = _attention(q, k, v)
    ssd_out = _ssd_mixer(z, xbc, dt_raw, conv_w, conv_b, dt_bias, a_log, d_skip, ssd_norm_w)
    mix = jnp.concatenate([attn_out, ssd_out], axis=-1) @ w_out
    x = _layer_norm(DN_ALPHA * x + mix, ln1_g, ln1_b)
    moe = _expert_choice(x.reshape(b * s, d), w_router, w_e_gate, w_e_up, w_e_down).reshape(b, s, d)
    ple = jax.nn.sigmoid(x @ w_ple_gate + b_ple_gate) * (p @ w_ple)
    return _layer_norm(DN_ALPHA * x + moe + ple, ln2_g, ln2_b)

def _trunk(x, p, ln_in_g, ln_in_b, w_in, q_norm_w, k_norm_w, conv_w, conv_b, dt_bias, a_log,
           d_skip, ssd_norm_w, w_out, ln1_g, ln1_b, w_router, w_e_gate, w_e_up, w_e_down,
           w_ple_gate, b_ple_gate, w_ple, ln2_g, ln2_b):
    x = _layer_norm(x, ln_in_g, ln_in_b)
    for l in range(DEPTH):
        x = _layer(x, p[l], w_in[l], q_norm_w[l], k_norm_w[l], conv_w[l], conv_b[l], dt_bias[l],
                   a_log[l], d_skip[l], ssd_norm_w[l], w_out[l], ln1_g[l], ln1_b[l], w_router[l],
                   w_e_gate[l], w_e_up[l], w_e_down[l], w_ple_gate[l], b_ple_gate[l], w_ple[l],
                   ln2_g[l], ln2_b[l])
    return x

def setup_inputs(seed: int = 0) -> dict:
    key = jax.random.key(seed)
    ks = jax.random.split(key, 32)
    f32 = jnp.float32

    def nrm(k, shape, scale):
        return jax.random.normal(k, shape, f32) * scale

    def gain(k, shape):
        return 1.0 + 0.02 * jax.random.normal(k, shape, f32)

    u = jax.random.uniform(ks[12], (DEPTH, 2, SSD_HEADS), f32)
    dt0 = jnp.exp(u * (math.log(0.1) - math.log(0.001)) + math.log(0.001))
    dt_bias = dt0 + jnp.log(-jnp.expm1(-dt0))
    a_log = jnp.log(jax.random.uniform(ks[13], (DEPTH, 2, SSD_HEADS), f32, 1.0, 16.0))
    return {
        "x_prompt": jax.random.normal(ks[0], (BATCH, SEQ, D_MODEL), f32),
        "x_sample": jax.random.normal(ks[1], (DEC_BATCH, DEC_SEQ, D_MODEL), f32),
        "p_prompt": jax.random.normal(ks[2], (DEPTH, BATCH, SEQ, PLE_DIM), f32),
        "p_sample": jax.random.normal(ks[3], (DEPTH, DEC_BATCH, DEC_SEQ, PLE_DIM), f32),
        "ln_in_g": gain(ks[4], (D_MODEL,)),
        "ln_in_b": nrm(ks[5], (D_MODEL,), 0.02),
        "w_in": nrm(ks[6], (DEPTH, D_MODEL, IN_COLS), D_MODEL ** -0.5),
        "q_norm_w": gain(ks[7], (DEPTH, HEAD_DIM)),
        "k_norm_w": gain(ks[8], (DEPTH, HEAD_DIM)),
        "conv_w": nrm(ks[9], (DEPTH, D_CONV, CONV_CH), D_CONV ** -0.5),
        "conv_b": nrm(ks[10], (DEPTH, CONV_CH), 0.02),
        "dt_bias": dt_bias,
        "a_log": a_log,
        "d_skip": gain(ks[11], (DEPTH, SSD_HEADS)),
        "ssd_norm_w": gain(ks[14], (DEPTH, D_INNER)),
        "w_out": nrm(ks[15], (DEPTH, MIX_W, D_MODEL), DN_BETA * MIX_W ** -0.5),
        "ln1_g": gain(ks[16], (DEPTH, D_MODEL)),
        "ln1_b": nrm(ks[17], (DEPTH, D_MODEL), 0.02),
        "w_router": nrm(ks[18], (DEPTH, D_MODEL, N_EXPERTS), D_MODEL ** -0.5),
        "w_e_gate": nrm(ks[19], (DEPTH, N_EXPERTS, D_MODEL, D_EXPERT), D_MODEL ** -0.5),
        "w_e_up": nrm(ks[20], (DEPTH, N_EXPERTS, D_MODEL, D_EXPERT), D_MODEL ** -0.5),
        "w_e_down": nrm(ks[21], (DEPTH, N_EXPERTS, D_EXPERT, D_MODEL), DN_BETA * D_EXPERT ** -0.5),
        "w_ple_gate": nrm(ks[22], (DEPTH, D_MODEL, D_MODEL), D_MODEL ** -0.5),
        "b_ple_gate": nrm(ks[23], (DEPTH, D_MODEL), 0.02),
        "w_ple": nrm(ks[24], (DEPTH, PLE_DIM, D_MODEL), DN_BETA * PLE_DIM ** -0.5),
        "ln2_g": gain(ks[25], (DEPTH, D_MODEL)),
        "ln2_b": nrm(ks[26], (DEPTH, D_MODEL), 0.02),
    }

def reference(x_prompt, x_sample, p_prompt, p_sample, ln_in_g, ln_in_b, w_in, q_norm_w, k_norm_w,
              conv_w, conv_b, dt_bias, a_log, d_skip, ssd_norm_w, w_out, ln1_g, ln1_b, w_router,
              w_e_gate, w_e_up, w_e_down, w_ple_gate, b_ple_gate, w_ple, ln2_g, ln2_b):
    y_prompt = _trunk(x_prompt, p_prompt, ln_in_g, ln_in_b, w_in, q_norm_w, k_norm_w, conv_w, conv_b,
                      dt_bias, a_log, d_skip, ssd_norm_w, w_out, ln1_g, ln1_b, w_router, w_e_gate,
                      w_e_up, w_e_down, w_ple_gate, b_ple_gate, w_ple, ln2_g, ln2_b)
    y_sample = _trunk(x_sample, p_sample, ln_in_g, ln_in_b, w_in, q_norm_w, k_norm_w, conv_w, conv_b,
                      dt_bias, a_log, d_skip, ssd_norm_w, w_out, ln1_g, ln1_b, w_router, w_e_gate,
                      w_e_up, w_e_down, w_ple_gate, b_ple_gate, w_ple, ln2_g, ln2_b)
    return (y_prompt, y_sample)


_drawn_inputs = setup_inputs


def setup_inputs(seed=0):
    import zlib

    import numpy as np

    out = dict(_drawn_inputs(seed))
    spreads = {}
    factors = {'q_norm_w': 8.0,
     'k_norm_w': 22.292,
     'conv_b': 5.029,
     'd_skip': 27.526,
     'ssd_norm_w': 19.154,
     'ln1_b': 2.88,
     'b_ple_gate': 125.252,
     'ln2_g': 22.101,
     'ln2_b': 22.052,
     'ln1_g': 2.738}
    for name, (base, spread) in spreads.items():
        noise = np.random.default_rng([zlib.crc32(name.encode()), seed]).standard_normal(out[name].shape)
        drawn = base * np.exp(spread * noise) if base else spread * noise
        out[name] = __import__('jax').numpy.asarray(drawn.astype(out[name].dtype))
    for name, factor in factors.items():
        out[name] = (out[name] * factor).astype(out[name].dtype)
    return out
```

```python
from contextlib import ExitStack

import numpy as np

import concourse.bass as bass
from concourse import mybir

ALU = mybir.AluOpType
ACT = mybir.ActivationFunctionType
F32 = mybir.dt.float32
BF16 = mybir.dt.bfloat16
U32 = mybir.dt.uint32
I32 = mybir.dt.int32
X = mybir.AxisListType.X

P = 128
D = 1024
KD = D // P
HD = 64
NQ, NKV = 8, 2
NH = 8
GROUPS, HPG = 2, 4
NSTATE = 128
TAPS = 5
CONV = 1024
KC = CONV // P
NE = 16
PLE = 256
GRID_W = 64
THETA = 10000.0
NORM_EPS, LN_EPS = 1e-6, 1e-5
ALPHA = 2.0 ** 0.25
K0, V0, Z0, XBC0, DT0, IN_COLS = 512, 640, 768, 1280, 2304, 2320
NEG = -1e30


def shape_constants(lengths):
    i = np.arange(P)
    ident = np.eye(P)
    upto = (i[:, None] <= i[None, :]) * 1.0
    onward = (i[:, None] >= i[None, :]) * 1.0
    mask_f = np.where(upto > 0, 0.0, NEG)
    mask_b = np.where(onward > 0, 0.0, NEG)
    inv = THETA ** (-np.arange(HD // 4) / (HD // 4))
    cs = []
    for n in lengths:
        pos = np.stack([np.arange(n) // GRID_W, np.arange(n) % GRID_W], -1)
        ang = (pos[:, :, None] * inv).reshape(n // P, P, HD // 2)
        cs.append(np.stack([np.cos(ang), np.sin(ang)], 2))
    cs = np.concatenate(cs).transpose(1, 0, 2, 3).reshape(P, -1)
    return np.concatenate([ident, upto, onward, mask_f, mask_b, cs], 1).astype(np.float32)


def hymba_layer(nc, A, consts, out_prompt, out_sample):
    TP = A["x_prompt"].shape[1] // P
    TS = A["x_sample"].shape[1] // P
    NT = TP + TS
    T = NT * P
    SEQS = [(0, TP), (TP, TS)]
    CAPP, CAPS = TP * P * 2 // NE, TS * P * 2 // NE
    CAP = CAPP + CAPS
    PADW = TP * P + TS * P + 6
    CW = PADW - 4

    def conv_col(t):
        return t * P if t < TP else t * P + 2

    ctx = ExitStack()
    with ctx:
        def sb(name, shape, dt=F32):
            return ctx.enter_context(nc.sbuf_tensor(name, shape, dt))

        def sem(name):
            return ctx.enter_context(nc.semaphore(name))

        ring = sb("ring", [P, 3, KD * 512])
        late = sb("late", [P, KC * (PADW + CW)])
        xa = sb("xa", [P, NT, D])
        xT = sb("xT", [P, KD, T])
        mix = sb("mix", [P, NT, D])
        kvd = sb("kvd", [P, NT, 272])
        cst = sb("cst", [P, 5 * P + NT * 64])
        gA, bA = sb("gA", [P, D]), sb("bA", [P, D])
        gB, bB = sb("gB", [P, D]), sb("bB", [P, D])
        ssdw = sb("ssdw", [P, 512])
        qkw = sb("qkw", [P, 2, HD])
        hpar = sb("hpar", [P, 3, 16])
        maskb = sb("maskb", [P, 2, P], BF16)
        identb = sb("identb", [P, P], BF16)
        ones = sb("ones", [P, P])
        wr = sb("wr", [P, KD, NE])
        cw = sb("cw", [P, KC, TAPS + 1])
        stats = sb("stats", [P, 2, 12])
        mv = sb("mv", [P, NT, 2])
        sd = sb("sd", [P, 2, NT])
        qks = sb("qks", [P, 3, 10])
        dtw = sb("dtw", [P, 9, NT * 16])
        att = sb("att", [P, 4, NT * NQ])
        gss = sb("gss", [P, 3, NT * GROUPS])
        rt = sb("rt", [P, 1, NT * NE])
        rs6 = sb("rs6", [P, 3, NT])
        topv = sb("topv", [NE, CAP])
        topi = sb("topi", [NE, CAP], U32)
        gateT = sb("gateT", [CAP, NE])
        idxT = sb("idxT", [CAP, NE], I32)
        idx_now = sb("idx_now", [CAP, 2], I32)
        qksq = sb("qksq", [P, 640])
        ps = ctx.enter_context(nc.psum_tensor("ps", [P, 8, 512], F32))

        x1_rows = nc.dram_tensor("x1_rows", (T, D), F32, kind="Internal").ap()
        acc_rows = nc.dram_tensor("acc_rows", (T, D), F32, kind="Internal").ap()

        ident = cst[:, 0:P]
        ysum = qksq[:, 0:512].rearrange("p (b c) -> p b c", b=2)
        topf = cst[0:NE, 3 * P:3 * P + CAP]
        upto, onward = cst[:, P:2 * P], cst[:, 2 * P:3 * P]
        masks = cst[:, 3 * P:5 * P]
        rope = cst[:, 5 * P:].rearrange("p (t c a f) -> p t c a f", t=NT, c=2, a=2)
        u_pad = late[:, 0:KC * PADW].rearrange("p (m c) -> p m c", m=KC)
        conv = late[:, KC * PADW:].rearrange("p (m c) -> p m c", m=KC)
        cw_rows = late[0:TAPS + 1, KC * PADW + 6 * CW:KC * PADW + 6 * CW + CONV]
        xtok = late[:, 0:NT * 512].rearrange("p (t c) -> p t c", t=NT)
        btok = late[:, NT * 512:NT * 768].rearrange("p (t c) -> p t c", t=NT)
        slot = [ring[:, j, :] for j in range(3)] + [late[:, j * 4096:(j + 1) * 4096] for j in range(3)]
        slotk = [s.rearrange("p (k c) -> p k c", k=KD) for s in slot]
        qT = xT[:, 0:4, :]
        kT = xT[:, 4, :]
        s0, s1 = ring[:, 0, :], ring[:, 1, :]
        prob = s0[:, 0:1536].rearrange("p (b c) -> p b c", b=3)
        probT = s0[:, 1536:2560].rearrange("p (b c) -> p b c", b=2)
        dec = s0[:, 0:2048].rearrange("p (b d h l) -> p b d h l", b=2, d=2, h=HPG)
        msum = s0[:, 2048:3072].rearrange("p (b h l) -> p b h l", b=2, h=HPG)
        cbT = s0[:, 3072:3328].rearrange("p (b l) -> p b l", b=2)
        ysq = s0[:, 3328:3584]
        xsc = s0[:, 3584:4096].rearrange("p (d c) -> p d c", d=2)
        NPREV = sum(n - 1 for _, n in SEQS)
        state = s1[:, 0:4 * NPREV * 256].rearrange("p (d g n c) -> p d g n c", d=2, g=2, n=NPREV)
        mixf = mix[:, :, :].rearrange("p t c -> p (t c)")
        pT = mixf[:, 0:1536].rearrange("p (k c) -> p k c", k=2)
        sig = mixf[:, 1536:3584].rearrange("p (b c) -> p b c", b=2)
        affw = mixf[0:NE, 3584:3584 + 2 * T].rearrange("p (b c) -> p b c", b=2)
        kvf = kvd[:, :, :].rearrange("p t c -> p (t c)")
        ptok = kvf[:, 0:NT * PLE].rearrange("p (t c) -> p t c", t=NT)
        xe = kvf[0:CAP, 0:D]
        xaf = xa[:, :, :].rearrange("p t c -> p (t c)")
        xeT = xaf[:, 0:KD * CAP].rearrange("p (k c) -> p k c", k=KD)
        hidT = xaf[:, 1024:1024 + KD * CAP].rearrange("p (k c) -> p k c", k=KD)
        hid = xaf[0:CAP, 2048:3072]
        ye = xaf[0:CAP, 3072:4096]
        fin = xT[:, :, :].rearrange("p k c -> p (k c)").rearrange("p (t c) -> p t c", t=NT)

        s_const = sem("s_const")
        s_param = sem("s_param")
        s_x = [sem(f"s_xin{t}") for t in range(NT)]
        s_slot = [sem(f"s_slot{j}") for j in range(6)]
        s_ple_in = sem("s_ple_in")
        s_dve = sem("s_dve")
        s_act = sem("s_act")
        s_pool = sem("s_pool")
        s_prep = sem("s_prep")
        s_var = sem("s_var")
        s_std = sem("s_std")
        s_xa = sem("s_xa")
        s_tr = sem("s_tr")
        s_xT = sem("s_xT")
        s_cw = sem("s_cw")
        s_proj = sem("s_proj")
        s_projo = sem("s_projo")
        s_rope = sem("s_rope")
        s_conv = sem("s_conv")
        s_silu = sem("s_silu")
        s_qkT = sem("s_qkT")
        s_xB = sem("s_xB")
        s_dt1 = sem("s_dt1")
        s_dt2 = sem("s_dt2")
        s_a = sem("s_a")
        s_cum = sem("s_cum")
        s_cums = sem("s_cums")
        s_ecum = sem("s_ecum")
        s_sc = sem("s_sc")
        s_max = sem("s_max")
        s_exp = sem("s_exp")
        s_pt = sem("s_pt")
        s_pts = sem("s_pts")
        s_pv = sem("s_pv")
        s_ao = sem("s_ao")
        s_ws = sem("s_ws")
        s_st = sem("s_st")
        s_sts = sem("s_sts")
        s_dec = sem("s_dec")
        s_edec = sem("s_edec")
        s_cb = sem("s_cb")
        s_cbs = sem("s_cbs")
        s_tfb = sem("s_tfb")
        s_m = sem("s_m")
        s_y = sem("s_y")
        s_yo = sem("s_yo")
        s_ssd = sem("s_ssd")
        s_mixT = sem("s_mixT")
        s_o = sem("s_o")
        s_x1 = sem("s_x1")
        s_x1T = sem("s_x1T")
        s_rowst = sem("s_rowst")
        s_lg = sem("s_lg")
        s_lge = sem("s_lge")
        s_lgd = sem("s_lgd")
        s_affT = sem("s_affT")
        s_top = sem("s_top")
        s_topT = sem("s_topT")
        s_idx = sem("s_idx")
        s_pT = sem("s_pT")
        s_pg = sem("s_pg")
        s_sig = sem("s_sig")
        s_base = sem("s_base")
        s_acc = [sem(f"s_acc{i}") for i in range(2)]
        s_gath = sem("s_gath")
        s_idg = sem("s_idg")
        s_xeT_p = sem("s_xeT_p")
        s_xeT = sem("s_xeT")
        s_gu = sem("s_gu")
        s_hs = sem("s_hs")
        s_hid = sem("s_hid")
        s_hT_p = sem("s_hT_p")
        s_hT = sem("s_hT")
        s_dn = sem("s_dn")
        s_ye = sem("s_ye")
        s_scat = sem("s_scat")
        s_fin = [sem(f"s_fin_{t}") for t in range(NT)]
        s_ln2 = sem("s_ln2")
        s_bple = sem("s_bple")
        s_y2 = sem("s_y2")
        s_out = sem("s_out")

        tok_groups = [(kind, t) for t in range(NT) for kind in ("q", "kv")]
        xbc_groups = [("xbc", m, s) for m in range(KC) for s in range(2)]
        z_groups = [("z", t) for t in range(NT)]
        groups = tok_groups + xbc_groups + z_groups
        gidx = {g: n for n, g in enumerate(groups)}
        COLS = {"q": (0, K0), "kv": (K0, 256), "z": (0, 512)}
        tr_units = [(s_xT, t + 1) for t in range(NT)] + [(s_cw, 1)] \
            + [(s_qkT, t + 1) for t in range(NT)] + [(s_xB, t + 1) for t in range(NT)]
        att_units = [(t, j + 4 * hh) for t in range(NT) for j in range(4) for hh in range(2)]
        NU = len(att_units)
        seq_of = {t: (a, n) for a, n in SEQS for t in range(a, a + n)}
        ssd_units = [(t, g) for t in range(NT) for g in range(GROUPS)]
        upd = []
        n0 = 0
        prev_at = {}
        for a, n in SEQS:
            for i in range(n - 1):
                prev_at[0, a + 1 + i] = n0 + i
                prev_at[1, a + n - 2 - i] = n0 + i
                for g in range(GROUPS):
                    upd.append((0, a + i, g, n0 + i, i == 0))
                    upd.append((1, a + n - 1 - i, g, n0 + i, i == 0))
            n0 += n - 1

        DT, ANEG, ACUM, NACUM, EA, WDEC, CD, W1, W2 = range(9)

        def d16(r):
            return dtw[:, r, :].rearrange("p (t c) -> p t c", t=NT)

        block = ctx.enter_context(nc.Block())

        class Chain:

            def __init__(self, eng, s):
                self.eng, self.s, self.n = eng, s, 0

            def step(self, ins):
                self.n += 1
                ins.then_inc(self.s, 1)

            def settle(self):
                self.eng.wait_ge(self.s, self.n)

            def link(self, ins):
                self.step(ins)
                self.settle()

        @block.sync
        def _(sp):
            win = A["w_in"][0].rearrange("(k p) c -> p k c", p=P)
            wout = A["w_out"][0].rearrange("(k p) c -> p k c", p=P)
            wpg = A["w_ple_gate"][0].rearrange("(k p) c -> p k c", p=P)

            def xtile(name, i):
                return A[name][0][i * P:(i + 1) * P, :]

            def bc(ap):
                return ap.partition_broadcast(P)

            sp.dma_start(xa[:, 0, :], xtile("x_prompt", 0)).then_inc(s_x[0], 16)
            small = [(cst[:], consts), (gA[:], bc(A["ln_in_g"])), (bA[:], bc(A["ln_in_b"]))]
            for dst, src in small:
                sp.dma_start(dst, src).then_inc(s_const, 16)
            sp.dma_start(slotk[0], win[:, :, 0:K0]).then_inc(s_slot[0], 16)
            for t in range(1, NT):
                src = xtile("x_prompt", t) if t < TP else xtile("x_sample", t - TP)
                sp.dma_start(xa[:, t, :], src).then_inc(s_x[t], 16)
            sp.dma_start(slot[1][:, 0:KD * 256].rearrange("p (k c) -> p k c", k=KD),
                         win[:, :, K0:Z0]).then_inc(s_slot[1], 16)
            sp.dma_start(slot[1][:, KD * 256:KD * 272].rearrange("p (k c) -> p k c", k=KD),
                         win[:, :, DT0:IN_COLS]).then_inc(s_slot[1], 16)
            sp.dma_start(slotk[2], win[:, :, XBC0:XBC0 + 512]).then_inc(s_slot[2], 16)
            small2 = [(gB[:], bc(A["ln1_g"][0])), (bB[:], bc(A["ln1_b"][0])),
                      (ssdw[:], bc(A["ssd_norm_w"][0])),
                      (qkw[:, 0, :], bc(A["q_norm_w"][0])), (qkw[:, 1, :], bc(A["k_norm_w"][0])),
                      (hpar[:, 0, :], bc(A["dt_bias"][0].rearrange("d h -> (d h)"))),
                      (hpar[:, 1, :], bc(A["a_log"][0].rearrange("d h -> (d h)"))),
                      (hpar[:, 2, 0:NH], bc(A["d_skip"][0])),
                      (wr[:], A["w_router"][0].rearrange("(k p) e -> p k e", p=P)),
                      (cw_rows[0:TAPS, :], A["conv_w"][0]), (cw_rows[TAPS:TAPS + 1, :], A["conv_b"])]
            for dst, src in small2:
                sp.dma_start(dst, src).then_inc(s_param, 16)
            sp.wait_ge(s_proj, gidx["q", NT - 1] + 1)
            sp.dma_start(slotk[0], win[:, :, XBC0 + 512:DT0]).then_inc(s_slot[0], 16)
            sp.wait_ge(s_proj, gidx["kv", NT - 1] + 1)
            sp.dma_start(slotk[1], win[:, :, Z0:XBC0]).then_inc(s_slot[1], 16)
            sp.wait_ge(s_proj, gidx["xbc", 3, 1] + 1)
            sp.dma_start(slotk[2], wout[:, :, 0:512]).then_inc(s_slot[2], 16)
            sp.wait_ge(s_pv, NU)
            sp.wait_ge(s_a, 1)
            pt = [(ptok[:, 0:TP, :], A["p_prompt"][0, 0]), (ptok[:, TP:NT, :], A["p_sample"][0, 0])]
            for dst, src in pt:
                sp.dma_start(dst, src.rearrange("(t p) c -> p t c", p=P)).then_inc(s_ple_in, 16)
            sp.wait_ge(s_ssd, NT)
            sp.dma_start(slotk[0], wout[:, :, 512:D]).then_inc(s_slot[0], 16)
            sp.dma_start(slotk[1], wpg[:, :, 0:512]).then_inc(s_slot[1], 16)
            sp.dma_start(gA[0:1, :], A["b_ple_gate"]).then_inc(s_bple, 16)

            wg = A["w_e_gate"][0].rearrange("e (k p) f -> e p k f", p=P)
            wu = A["w_e_up"][0].rearrange("e (k p) f -> e p k f", p=P)
            wd = A["w_e_down"][0].rearrange("e (k p) f -> e p k f", p=P)

            def load(j, w, e, h):
                sp.dma_start(slotk[j], w[e, :, :, h * 512:(h + 1) * 512]).then_inc(s_slot[j], 16)

            load(3, wg, 0, 0)
            load(4, wu, 0, 0)
            load(5, wg, 0, 1)
            sp.wait_ge(s_o, NT)
            sp.dma_start(slotk[2], wpg[:, :, 512:D]).then_inc(s_slot[2], 16)
            sp.dma_start(slot[0][:, 0:2048].rearrange("p (k c) -> p k c", k=2),
                         A["w_ple"][0].rearrange("(k p) c -> p k c", p=P)).then_inc(s_slot[0], 16)
            sp.wait_ge(s_pg, 2 * NT)
            load(0, wu, 0, 1)
            load(1, wd, 0, 0)
            load(2, wd, 0, 1)
            sp.dma_start(gA[:], bc(A["ln2_g"][0])).then_inc(s_ln2, 16)
            sp.dma_start(bA[:], bc(A["ln2_b"][0])).then_inc(s_ln2, 16)
            with sp.Fori(1, NE) as e:
                sp.wait_ge(s_gu, 2 * e - 1)
                load(3, wg, e, 0)
                load(4, wu, e, 0)
                sp.wait_ge(s_gu, 2 * e)
                load(5, wg, e, 1)
                load(0, wu, e, 1)
                sp.wait_ge(s_dn, 2 * e - 1)
                load(1, wd, e, 0)
                sp.wait_ge(s_dn, 2 * e)
                load(2, wd, e, 1)
            sp.wait_ge(s_scat, 16 * NE)
            for t in range(NT):
                sp.dma_start(fin[:, t, :], acc_rows[t * P:(t + 1) * P, :]).then_inc(s_fin[t], 16)
            for t in range(NT):
                sp.wait_ge(s_y2, t + 1)
                dst = out_prompt[0] if t < TP else out_sample[0]
                i = t if t < TP else t - TP
                sp.dma_start(dst[i * P:(i + 1) * P, :], fin[:, t, :]).then_inc(s_out, 16)
            sp.wait_ge(s_out, 16 * NT)
            sp.wait_ge(s_rowst, 16 * NT)
            for s in s_acc:
                sp.wait_ge(s, 16 * (NT // 2))

        @block.gpsimd
        def _(pool):
            ch = Chain(pool, s_pool)
            nc.gpsimd.memset(ones[:], 1.0)
            for c0, w in ((0, 2), (2 + TP * P, 2), (4 + T, 2)):
                nc.gpsimd.memset(u_pad[:, :, c0:c0 + w], 0.0)
            pool.wait_ge(s_const, 16 * 3)
            nc.gpsimd.tensor_copy(maskb[:], masks.rearrange("p (d l) -> p d l", d=2))
            nc.gpsimd.tensor_copy(identb[:], ident).then_inc(s_prep, 1)
            pool.wait_ge(s_ecum, 3)
            pool.wait_ge(s_cums, 2)
            pool.wait_ge(s_xB, NT)
            pool.wait_ge(s_pv, NU)
            for n, (d, t, g, i, first) in enumerate(upd):
                if n >= 2:
                    pool.wait_ge(s_st, n - 1)
                o = xsc[:, n % 2, :].rearrange("p (h c) -> p h c", h=HPG)
                xin = xtok[:, t, g * 256:(g + 1) * 256].rearrange("p (h c) -> p h c", h=HPG)
                w = d16(WDEC)[:, t, d * NH + g * HPG:d * NH + (g + 1) * HPG]
                nc.gpsimd.tensor_tensor(o, xin, w.unsqueeze(2).broadcast_to([P, HPG, HD]),
                                        ALU.mult).then_inc(s_ws, 1)
            for n, (t, g) in enumerate(ssd_units):
                pool.wait_ge(s_tfb, n + 1)
                if n >= 2:
                    pool.wait_ge(s_y, n - 1)
                nc.gpsimd.tensor_tensor(msum[:, n % 2], dec[:, n % 2, 0], dec[:, n % 2, 1],
                                        ALU.add).then_inc(s_m, 1)
            for t in range(NT):
                pool.wait_ge(s_x1, t + 1)
                pool.dma_start(x1_rows[t * P:(t + 1) * P, :], xa[:, t, :]).then_inc(s_rowst, 16)

            def gather():
                pool.indirect_dma_start(xe, None, x1_rows,
                                        bass.IndirectOffsetOnAxis(ap=idx_now[:, 0:1], axis=0)
                                        ).then_inc(s_gath, 16)

            pool.wait_ge(s_rowst, 16 * NT)
            pool.wait_ge(s_idx, 2)
            pool.wait_ge(s_pT, 3)
            ch.link(nc.gpsimd.tensor_copy(idx_now[:, 0:1], idxT[:, 0:1]))
            gather()
            for t in range(NT):
                pool.wait_ge(s_base, 2 * (t + 1))
                pool.dma_start(acc_rows[t * P:(t + 1) * P, :], sig[:, t % 2, :]).then_inc(s_acc[t % 2], 16)
            for s in s_acc:
                pool.wait_ge(s, 16 * (NT // 2))

            def scatter():
                pool.indirect_dma_start(acc_rows, bass.IndirectOffsetOnAxis(ap=idx_now[:, 1:2], axis=0),
                                        ye, None, compute_op=ALU.add).then_inc(s_scat, 16)

            def pick(col, e):
                return nc.gpsimd.tensor_copy(idx_now[:, col:col + 1], idxT[:, bass.ds(e, 1)])

            pool.wait_ge(s_xeT_p, 1)
            ch.link(pick(0, 1))
            gather()
            with pool.Fori(1, NE - 1) as f:
                pool.wait_ge(s_xeT_p, f + 1)
                pick(0, f + 1)
                pick(1, f - 1).then_inc(s_idg, 1)
                pool.wait_ge(s_const, 16 * 3)
                pool.wait_ge(s_idg, f)
                gather()
                pool.wait_ge(s_const, 16 * 3)
                pool.wait_ge(s_ye, f)
                scatter()
                pool.wait_ge(s_scat, 16 * f)
            for e in (NE - 2, NE - 1):
                ch.link(pick(1, e))
                pool.wait_ge(s_ye, e + 1)
                scatter()
                pool.wait_ge(s_scat, 16 * (e + 1))

        @block.scalar
        def _(act):
            ch = Chain(act, s_act)
            nvar = [0]

            def root():
                nvar[0] += 1
                act.wait_ge(s_var, nvar[0])

            def copy(o, i):
                return nc.scalar.activation(o, i, ACT.Copy)

            def x_std(t):
                root()
                nc.scalar.activation(sd[:, 0, t:t + 1], sd[:, 0, t:t + 1], ACT.Sqrt).then_inc(s_std, 1)

            x_std(0)
            x_std(1)
            n = 0
            for g in groups:
                if g[0] == "q" and g[1] + 2 < NT:
                    x_std(g[1] + 2)
                act.wait_ge(s_proj, n + 1)
                bank = ps[:, 4 + n % 4, :]
                if g[0] == "q":
                    copy(mix[:, g[1], 0:512].rearrange("p (j i c) -> p i j c", i=2, j=4),
                         bank.rearrange("p (i j c) -> p i j c", i=2, j=4)).then_inc(s_projo, 1)
                elif g[0] == "kv":
                    copy(kvd[:, g[1], :], bank[:, 0:272]).then_inc(s_projo, 1)
                elif g[0] == "xbc":
                    a, w = SEQS[g[2]]
                    c0 = 2 + a * P + 2 * g[2]
                    copy(u_pad[:, g[1], c0:c0 + w * P], bank[:, 0:w * P]).then_inc(s_projo, 1)
                    if g[2] == 1 and g[1] < NT:
                        root()
                        nc.scalar.activation(qks[:, 1, :], qks[:, 0, :], ACT.Sqrt).then_inc(s_std, 1)
                else:
                    copy(mix[:, g[1], 512:D], bank).then_inc(s_projo, 1)
                n += 1
            act.wait_ge(s_projo, n)
            for m in range(KC):
                act.wait_ge(s_conv, m + 1)
                nc.scalar.activation(conv[:, m, :], conv[:, m, :], ACT.Silu).then_inc(s_silu, 1)
            for t in range(NT):
                nc.scalar.activation(mix[:, t, 512:D], mix[:, t, 512:D], ACT.Silu).then_inc(s_silu, 1)
            for t in range(NT):
                u = NT + 1 + t
                act.wait_ge(s_tr, u + 1)
                b = 2 * (u % 2)
                copy(qT[:, :, t * P:(t + 1) * P], ps[:, b, :].rearrange("p (j c) -> p j c", j=4))
                copy(kT[:, t * P:(t + 1) * P], ps[:, b + 1, 0:P]).then_inc(s_qkT, 1)
            for t in range(NT):
                u = 2 * NT + 1 + t
                act.wait_ge(s_tr, u + 1)
                b = 2 * (u % 2)
                copy(xtok[:, t, :], ps[:, b, :])
                copy(btok[:, t, :], ps[:, b + 1, 0:256]).then_inc(s_xB, 1)
            act.wait_ge(s_dt1, 1)
            nc.scalar.activation(dtw[:, W1, :], dtw[:, W1, :], ACT.Exp)
            nc.scalar.activation(hpar[:, 1, :], hpar[:, 1, :], ACT.Exp).then_inc(s_dt2, 1)
            act.wait_ge(s_dt1, 2)
            nc.scalar.activation(dtw[:, ACUM, :], dtw[:, W2, :], ACT.Ln).then_inc(s_dt2, 1)
            act.wait_ge(s_cums, 1)
            nc.scalar.activation(dtw[:, EA, :], dtw[:, ACUM, :], ACT.Exp).then_inc(s_ecum, 1)
            nc.scalar.activation(dtw[:, WDEC, :], dtw[:, W1, :], ACT.Exp).then_inc(s_ecum, 1)
            nc.scalar.activation(dtw[:, CD, :], dtw[:, CD, :], ACT.Exp).then_inc(s_ecum, 1)
            for u, (t, h) in enumerate(att_units):
                L = seq_of[t][1] * P
                act.wait_ge(s_max, u + 1)
                if u >= 3:
                    act.wait_ge(s_pt, u - 2)
                nc.scalar.activation(prob[:, u % 3, 0:L], ps[:, u % 3, 0:L], ACT.Exp,
                                     bias=att[:, 0, u:u + 1], scale=HD ** -0.5,
                                     accum_out=att[:, 1, u:u + 1]).then_inc(s_exp, 1)
            for n, (t, g) in enumerate(ssd_units):
                act.wait_ge(s_dec, n + 1)
                act.wait_ge(s_pv, NU)
                if n >= 2:
                    act.wait_ge(s_m, n - 1)
                for d in range(2):
                    for h in range(HPG):
                        c = d * NH + g * HPG + h
                        last = nc.scalar.activation(dec[:, n % 2, d, h], ps[:, 2 * (n % 2) + d, h * P:(h + 1) * P],
                                                    ACT.Exp, bias=d16(NACUM)[:, t, c:c + 1])
                last.then_inc(s_edec, 1)
            root()
            nc.scalar.activation(gss[:, 1, :], gss[:, 1, :], ACT.Sqrt).then_inc(s_std, 1)
            for t in range(NT):
                act.wait_ge(s_tr, 3 * NT + 1 + t + 1)
                b = 2 * (t % 2)
                for half in range(2):
                    last = copy(xT[:, 4 * half:4 * half + 4, t * P:(t + 1) * P],
                                ps[:, b + half, :].rearrange("p (k c) -> p k c", k=4))
                last.then_inc(s_mixT, 1)
            for t in range(NT):
                root()
                nc.scalar.activation(sd[:, 0, t:t + 1], sd[:, 0, t:t + 1], ACT.Sqrt).then_inc(s_std, 1)
                act.wait_ge(s_tr, 4 * NT + 1 + t + 1)
                b = 2 * (t % 2)
                for half in range(2):
                    last = copy(xT[:, 4 * half:4 * half + 4, t * P:(t + 1) * P],
                                ps[:, b + half, :].rearrange("p (k c) -> p k c", k=4))
                last.then_inc(s_x1T, 1)
            act.wait_ge(s_lgd, 1)
            nc.scalar.activation(rt[:, 0, :], rt[:, 0, :], ACT.Exp).then_inc(s_lge, 1)
            for k in range(3):
                act.wait_ge(s_tr, 5 * NT + 1 + k + 1)
                copy(pT[:, :, 2 * k * P:2 * (k + 1) * P],
                     ps[:, k, :].rearrange("p (k c) -> p k c", k=2)).then_inc(s_pT, 1)
            for u in range(2 * NT):
                t, h = u // 2, u % 2
                act.wait_ge(s_pg, u + 1)
                if t >= 2:
                    act.wait_ge(s_acc[t % 2], 16 * (t // 2))
                nc.scalar.activation(sig[:, t % 2, h * 512:(h + 1) * 512], ps[:, 2 * h, :],
                                     ACT.Sigmoid).then_inc(s_sig, 1)

            def silu_half(e, h):
                act.wait_ge(s_gu, 2 * e + h + 1)
                nc.scalar.activation(hid[:, h * 512:(h + 1) * 512], ps[0:CAP, 2 * h, :],
                                     ACT.Silu).then_inc(s_hs, 1)

            def hidT_out(e):
                act.wait_ge(s_hT_p, e + 1)
                for half in range(2):
                    last = copy(hidT[:, 4 * half:4 * half + 4, :],
                                ps[:, 6 + half, 0:4 * CAP].rearrange("p (k c) -> p k c", k=4))
                last.then_inc(s_hT, 1)

            act.wait_ge(s_base, 2 * NT)
            silu_half(0, 0)
            silu_half(0, 1)
            with act.Fori(1, NE) as e:
                act.wait_ge(s_hT_p, e)
                for half in range(2):
                    last = copy(hidT[:, 4 * half:4 * half + 4, :],
                                ps[:, 6 + half, 0:4 * CAP].rearrange("p (k c) -> p k c", k=4))
                last.then_inc(s_hT, 1)
                silu_half(e, 0)
                silu_half(e, 1)
            hidT_out(NE - 1)
            for t in range(NT):
                root()
                nc.scalar.activation(sd[:, 0, t:t + 1], sd[:, 0, t:t + 1], ACT.Sqrt).then_inc(s_std, 1)

        @block.vector
        def _(dve):
            ch = Chain(dve, s_dve)
            nroot = [0]

            def ln_stats(t, src, eps):
                for half in range(2):
                    ch.step(nc.vector.bn_stats(stats[:, t % 2, 6 * half:6 * half + 6],
                                               src[:, half * 512:(half + 1) * 512]))
                ch.settle()
                ch.link(nc.vector.bn_aggr(mv[:, t, :], stats[:, t % 2, :]))
                nc.vector.tensor_scalar(sd[:, 0, t:t + 1], mv[:, t, 1:2], eps, None, ALU.add).then_inc(s_var, 1)

            def ln_apply(t, x, o, g, b, done):
                nroot[0] += 1
                dve.wait_ge(s_std, nroot[0])
                ch.link(nc.vector.reciprocal(sd[:, 1, t:t + 1], sd[:, 0, t:t + 1]))
                ch.link(nc.vector.tensor_scalar(o, x, mv[:, t, 0:1], sd[:, 1, t:t + 1], ALU.subtract, ALU.mult))
                ch.link(nc.vector.tensor_tensor(o, o, g[:], ALU.mult))
                nc.vector.tensor_tensor(o, o, b[:], ALU.add).then_inc(done, 1)

            def xT_out(t):
                dve.wait_ge(s_tr, t + 1)
                b = 2 * (t % 2)
                for half in range(2):
                    last = nc.vector.tensor_copy(xT[:, 4 * half:4 * half + 4, t * P:(t + 1) * P],
                                                 ps[:, b + half, :].rearrange("p (k c) -> p k c", k=4))
                last.then_inc(s_xT, 1)

            for t in range(NT):
                dve.wait_ge(s_x[t], 16)
                ln_stats(t, xa[:, t, :], LN_EPS)
                if t == 0:
                    dve.wait_ge(s_const, 16 * 3)
                ln_apply(t, xa[:, t, :], xa[:, t, :], gA, bA, s_xa)
                if t:
                    xT_out(t - 1)
            xT_out(NT - 1)
            dve.wait_ge(s_tr, NT + 1)
            b = 2 * (NT % 2)
            nc.vector.tensor_copy(cw[:], ps[:, b, 0:KC * (TAPS + 1)].rearrange("p (m j) -> p m j", m=KC)
                                  ).then_inc(s_cw, 1)
            dve.wait_ge(s_cw, 1)

            def rope_tile(t):
                dve.wait_ge(s_projo, gidx["kv", t] + 1)
                q = mix[:, t, 0:512]
                k = kvd[:, t, 0:P]
                sq = qksq[:]
                ch.step(nc.vector.tensor_tensor(sq[:, 0:512], q, q, ALU.mult))
                ch.link(nc.vector.tensor_tensor(sq[:, 512:640], k, k, ALU.mult))
                ch.link(nc.vector.tensor_reduce(qks[:, 0, :], sq.rearrange("p (h c) -> p h c", c=HD), X, ALU.add))
                nc.vector.tensor_scalar(qks[:, 0, :], qks[:, 0, :], 1.0 / HD, NORM_EPS, ALU.mult,
                                        ALU.add).then_inc(s_var, 1)
                nroot[0] += 1
                dve.wait_ge(s_std, nroot[0])
                ch.link(nc.vector.reciprocal(qks[:, 2, :], qks[:, 1, :]))
                for src, h0, n, w in ((q, 0, NQ, 0), (k, NQ, NKV, 1)):
                    v = src.rearrange("p (h c) -> p h c", c=HD)
                    rs = qks[:, 2, h0:h0 + n].unsqueeze(2).broadcast_to([P, n, HD])
                    ch.link(nc.vector.tensor_tensor(v, v, rs, ALU.mult))
                    wb = qkw[:, w, :].unsqueeze(1).broadcast_to([P, n, HD])
                    ch.link(nc.vector.tensor_tensor(v, v, wb, ALU.mult))
                    halves = src.rearrange("p (h a i f) -> p i h a f", a=2, i=2, f=16)
                    x1, x2 = halves[:, 0], halves[:, 1]
                    c, s = [rope[:, t, i].unsqueeze(1).broadcast_to([P, n, 2, 16]) for i in range(2)]
                    tmp = [sq[:, i * 256:i * 256 + n * 32].rearrange("p (h a f) -> p h a f", a=2, f=16)
                           for i in range(2)]
                    ch.step(nc.vector.tensor_tensor(tmp[0], x2, s, ALU.mult))
                    ch.link(nc.vector.tensor_tensor(tmp[1], x1, s, ALU.mult))
                    ch.step(nc.vector.tensor_tensor(x1, x1, c, ALU.mult))
                    ch.link(nc.vector.tensor_tensor(x2, x2, c, ALU.mult))
                    ch.step(nc.vector.tensor_tensor(x1, x1, tmp[0], ALU.subtract))
                    ch.link(nc.vector.tensor_tensor(x2, x2, tmp[1], ALU.add))
                nc.vector.tensor_copy(rs6[:, 0, t:t + 1], qks[:, 2, 0:1]).then_inc(s_rope, 1)

            def conv_tile(m):
                dve.wait_ge(s_projo, gidx["xbc", m, 1] + 1)
                ch.link(nc.vector.tensor_scalar(conv[:, m, :], u_pad[:, m, 0:CW], cw[:, m, 0:1],
                                                cw[:, m, TAPS:TAPS + 1], ALU.mult, ALU.add))
                for j in range(1, TAPS):
                    ins = nc.vector.scalar_tensor_tensor(conv[:, m, :], u_pad[:, m, j:j + CW], cw[:, m, j:j + 1],
                                                         conv[:, m, :], ALU.mult, ALU.add)
                    if j == TAPS - 1:
                        ins.then_inc(s_conv, 1)
                    else:
                        ch.link(ins)

            dve.wait_ge(s_param, 16 * 11)
            dve.wait_ge(s_prep, 1)
            for m in range(KC):
                if m < NT:
                    rope_tile(m)
                if m:
                    conv_tile(m - 1)
            conv_tile(KC - 1)

            raw = kvd[:, :, 256:272]
            ch.link(nc.vector.tensor_tensor(d16(DT), raw, hpar[:, 0, :].unsqueeze(1).broadcast_to([P, NT, 16]), ALU.add))
            nc.vector.scalar_tensor_tensor(dtw[:, W1, :], dtw[:, DT, :], -1.0, dtw[:, DT, :], ALU.mult,
                                           ALU.min).then_inc(s_dt1, 1)
            dve.wait_ge(s_dt2, 1)
            nc.vector.tensor_scalar(dtw[:, W2, :], dtw[:, W1, :], 1.0, None, ALU.add).then_inc(s_dt1, 1)
            dve.wait_ge(s_dt1, 2)
            ch.link(nc.vector.tensor_scalar(dtw[:, EA, :], dtw[:, W2, :], 1.0, None, ALU.is_equal))
            dve.wait_ge(s_dt2, 2)
            ch.step(nc.vector.tensor_tensor(dtw[:, ACUM, :], dtw[:, ACUM, :], dtw[:, EA, :], ALU.add))
            ch.link(nc.vector.scalar_tensor_tensor(dtw[:, W2, :], dtw[:, W2, :], -1.0, dtw[:, EA, :], ALU.add, ALU.add))
            ch.link(nc.vector.reciprocal(dtw[:, W2, :], dtw[:, W2, :]))
            ch.link(nc.vector.tensor_tensor(dtw[:, W1, :], dtw[:, W1, :], dtw[:, ACUM, :], ALU.mult))
            ch.link(nc.vector.tensor_tensor(dtw[:, W1, :], dtw[:, W1, :], dtw[:, W2, :], ALU.mult))
            ch.link(nc.vector.scalar_tensor_tensor(dtw[:, DT, :], dtw[:, DT, :], 0.0, dtw[:, W1, :], ALU.max, ALU.add))
            nc.vector.scalar_tensor_tensor(d16(ANEG), d16(DT), -1.0,
                                           hpar[:, 1, :].unsqueeze(1).broadcast_to([P, NT, 16]), ALU.mult,
                                           ALU.mult).then_inc(s_a, 1)
            dve.wait_ge(s_cum, 1)
            cum = ps[:, 4, 0:NT * 16].rearrange("p (d t h) -> p t d h", d=2, h=NH)
            tot = ps[:, 5, 0:NT * 16]
            a4 = dtw[:, ACUM, :].rearrange("p (t d h) -> p t d h", d=2, h=NH)
            ch.step(nc.vector.tensor_copy(dtw[:, CD, :], tot))
            ch.link(nc.vector.tensor_copy(a4, cum))
            ch.step(nc.vector.tensor_scalar(dtw[:, NACUM, :], dtw[:, ACUM, :], -1.0, None, ALU.mult))
            nc.vector.tensor_tensor(dtw[:, W1, :], dtw[:, CD, :], dtw[:, ACUM, :], ALU.subtract).then_inc(s_cums, 1)
            dve.wait_ge(s_ecum, 3)
            nc.vector.tensor_tensor(dtw[:, WDEC, :], dtw[:, WDEC, :], dtw[:, DT, :], ALU.mult).then_inc(s_cums, 1)

            def pt_out(u):
                t, h = att_units[u]
                L = seq_of[t][1] * P
                dve.wait_ge(s_pt, u + 1)
                if u >= 2:
                    dve.wait_ge(s_pv, u - 1)
                nc.vector.tensor_copy(probT[:, u % 2, 0:L], ps[:, 3 + u % 2, 0:L]).then_inc(s_pts, 1)

            def att_out(t):
                dve.wait_ge(s_pv, NQ * (t + 1))
                ch.link(nc.vector.reciprocal(att[:, 2, NQ * t:NQ * (t + 1)], att[:, 1, NQ * t:NQ * (t + 1)]))
                for hh in range(2):
                    o = mix[:, t, hh * 256:(hh + 1) * 256].rearrange("p (j c) -> p j c", j=4)
                    i = ps[:, 5 + t % 2, :].rearrange("p (j i c) -> p i j c", j=4, i=2)[:, hh]
                    r = att[:, 2, NQ * t:NQ * (t + 1)].rearrange("p (j i) -> p i j", i=2)[:, hh]
                    last = nc.vector.tensor_tensor(o, i, r.unsqueeze(2).broadcast_to([P, 4, HD]), ALU.mult)
                last.then_inc(s_ao, 1)

            for u in range(NU + 3):
                if u < NU:
                    t, h = att_units[u]
                    L = seq_of[t][1] * P
                    dve.wait_ge(s_sc, u + 1)
                    ch.link(nc.vector.reduce_max(att[:, 3, u:u + 1], ps[:, u % 3, 0:L], X))
                    nc.vector.tensor_scalar(att[:, 0, u:u + 1], att[:, 3, u:u + 1], -(HD ** -0.5), None,
                                            ALU.mult).then_inc(s_max, 1)
                if 2 <= u < NU + 2:
                    pt_out(u - 2)
                if u >= 3 and (u - 3) % NQ == NQ - 1:
                    att_out((u - 3) // NQ)

            for n, (d, t, g, i, first) in enumerate(upd):
                dve.wait_ge(s_st, n + 1)
                new = state[:, d, g, i, :]
                prod = ps[:, 5 + n % 2, 0:256]
                if first:
                    nc.vector.tensor_copy(new, prod).then_inc(s_sts, 1)
                else:
                    dve.wait_ge(s_sts, n - 3)
                    o = new.rearrange("p (h c) -> p h c", h=HPG)
                    old = state[:, d, g, i - 1, :].rearrange("p (h c) -> p h c", h=HPG)
                    w = d16(CD)[:, t, d * NH + g * HPG:d * NH + (g + 1) * HPG]
                    ch.link(nc.vector.tensor_tensor(o, old, w.unsqueeze(2).broadcast_to([P, HPG, HD]), ALU.mult))
                    nc.vector.tensor_tensor(new, new, prod, ALU.add).then_inc(s_sts, 1)

            def weights(n):
                t, g = ssd_units[n]
                dve.wait_ge(s_cb, n + 1)
                if n >= 2:
                    dve.wait_ge(s_tfb, n - 1)
                nc.vector.tensor_copy(cbT[:, n % 2, :], ps[:, 4, (n % 2) * P:(n % 2 + 1) * P]).then_inc(s_cbs, 1)
                dve.wait_ge(s_cbs, n + 1)
                dve.wait_ge(s_edec, n + 1)
                for d in range(2):
                    for h in range(HPG):
                        c = d * NH + g * HPG + h
                        v = dec[:, n % 2, d, h]
                        last = nc.vector.scalar_tensor_tensor(v, v, d16(DT)[:, t, c:c + 1], cbT[:, n % 2, :],
                                                              ALU.mult, ALU.mult)
                last.then_inc(s_tfb, 1)

            def y_out(n):
                t, g = ssd_units[n]
                dve.wait_ge(s_y, n + 1)
                cols = slice(512 + g * 256, 512 + (g + 1) * 256)
                acc = ysum[:, n % 2, :]
                tmp = ysq

                def heads(ap):
                    return ap.rearrange("p (h c) -> p h c", h=HPG)

                dsk = hpar[:, 2, g * HPG:(g + 1) * HPG].unsqueeze(2).broadcast_to([P, HPG, HD])
                ch.link(nc.vector.tensor_tensor(heads(acc), heads(xtok[:, t, g * 256:(g + 1) * 256]), dsk, ALU.mult))
                ch.link(nc.vector.tensor_tensor(acc, acc, ps[:, 6 + n % 2, 0:256], ALU.add))
                for d in range(2):
                    if (d, t) in prev_at:
                        off = ps[:, 5, d * 256:(d + 1) * 256]
                        c = d * NH + g * HPG
                        w = d16(EA)[:, t, c:c + HPG].unsqueeze(2).broadcast_to([P, HPG, HD])
                        ch.link(nc.vector.tensor_tensor(heads(tmp), heads(off), w, ALU.mult))
                        ch.link(nc.vector.tensor_tensor(acc, acc, tmp, ALU.add))
                ch.link(nc.vector.tensor_tensor(mix[:, t, cols], acc, mix[:, t, cols], ALU.mult))
                nc.vector.tensor_tensor_reduce(ysq, mix[:, t, cols], mix[:, t, cols], 1.0, 0.0, ALU.mult,
                                               ALU.add, gss[:, 0, n:n + 1]).then_inc(s_yo, 1)
                dve.wait_ge(s_yo, n + 1)

            dve.wait_ge(s_silu, KC + NT)
            for n in range(len(ssd_units)):
                weights(n)
                if n:
                    y_out(n - 1)
            y_out(len(ssd_units) - 1)
            nc.vector.tensor_scalar(gss[:, 1, :], gss[:, 0, :], 1.0 / 256, NORM_EPS, ALU.mult,
                                    ALU.add).then_inc(s_var, 1)
            nroot[0] += 1
            dve.wait_ge(s_std, nroot[0])
            ch.link(nc.vector.reciprocal(gss[:, 2, :], gss[:, 1, :]))
            for n, (t, g) in enumerate(ssd_units):
                y = mix[:, t, 512 + g * 256:512 + (g + 1) * 256]
                ins = nc.vector.scalar_tensor_tensor(y, y, gss[:, 2, n:n + 1], ssdw[:, g * 256:(g + 1) * 256],
                                                     ALU.mult, ALU.mult)
                if g:
                    ins.then_inc(s_ssd, 1)

            for t in range(NT):
                dve.wait_ge(s_o, t + 1)
                b = 4 + 2 * (t % 2)
                ch.link(nc.vector.scalar_tensor_tensor(xa[:, t, :], xa[:, t, :], ALPHA,
                                                       ps[:, b:b + 2, :].rearrange("p b c -> p (b c)"),
                                                       ALU.mult, ALU.add))
                ln_stats(t, xa[:, t, :], LN_EPS)
                ln_apply(t, xa[:, t, :], xa[:, t, :], gB, bB, s_x1)
            dve.wait_ge(s_lg, 1)
            lg = ps[:, 4, 0:NT * NE].rearrange("p (t e) -> p t e", e=NE)
            r0 = rt[:, 0, :].rearrange("p (t e) -> p t e", e=NE)
            ch.link(nc.vector.reduce_max(rs6[:, 0, :], lg, X))
            nc.vector.tensor_tensor(r0, lg, rs6[:, 0, :].unsqueeze(2).broadcast_to([P, NT, NE]),
                                    ALU.subtract).then_inc(s_lgd, 1)
            dve.wait_ge(s_lge, 1)
            ch.link(nc.vector.reduce_sum(rs6[:, 1, :], r0, X))
            ch.link(nc.vector.reciprocal(rs6[:, 2, :], rs6[:, 1, :]))
            nc.vector.tensor_tensor(r0, r0, rs6[:, 2, :].unsqueeze(2).broadcast_to([P, NT, NE]),
                                    ALU.mult).then_inc(s_lgd, 1)
            dve.wait_ge(s_affT, 1)
            ch.link(nc.vector.tensor_copy(affw[:, 0, :], ps[0:NE, 6:8, :].rearrange("p b c -> p (b c)")[:, 0:T]))
            for (a, n), c0, cap in ((SEQS[0], 0, CAPP), (SEQS[1], CAPP, CAPS)):
                lo, hi = a * P, (a + n) * P
                for r in range(cap // 8):
                    v = topv[:, c0 + 8 * r:c0 + 8 * r + 8]
                    cur, nxt = affw[:, r % 2, lo:hi], affw[:, (r + 1) % 2, lo:hi]
                    ch.link(nc.vector.max(v, cur))
                    ch.step(nc.vector.max_index(topi[:, c0 + 8 * r:c0 + 8 * r + 8], v, cur))
                    ch.link(nc.vector.match_replace(nxt, v, cur, -1.0))
            ch.step(nc.vector.tensor_copy(topf[:, 0:CAPP], topi[:, 0:CAPP]))
            ch.link(nc.vector.tensor_copy(topf[:, CAPP:CAP], topi[:, CAPP:CAP]))
            nc.vector.tensor_scalar(topf[:, CAPP:CAP], topf[:, CAPP:CAP], float(TP * P), None, ALU.add).then_inc(s_top, 1)
            dve.wait_ge(s_topT, 1)
            nc.vector.tensor_copy(idxT[:], ps[0:CAP, 5, 0:NE]).then_inc(s_idx, 1)
            nc.vector.tensor_copy(gateT[:], ps[0:CAP, 5, NE:2 * NE]).then_inc(s_idx, 1)
            for u in range(2 * NT):
                t, h = u // 2, u % 2
                dve.wait_ge(s_sig, u + 1)
                s = sig[:, t % 2, h * 512:(h + 1) * 512]
                ch.link(nc.vector.tensor_tensor(s, s, ps[:, 2 * h + 1, :], ALU.mult))
                nc.vector.scalar_tensor_tensor(s, xa[:, t, h * 512:(h + 1) * 512], ALPHA, s, ALU.mult,
                                               ALU.add).then_inc(s_base, 1)

            def xeT_out(e):
                dve.wait_ge(s_xeT_p, e + 1)
                for half in range(2):
                    last = nc.vector.tensor_copy(xeT[:, 4 * half:4 * half + 4, :],
                                                 ps[:, 6 + half, 0:4 * CAP].rearrange("p (k c) -> p k c", k=4))
                last.then_inc(s_xeT, 1)

            def hid_half(e, h):
                dve.wait_ge(s_hs, 2 * e + h + 1)
                v = hid[:, h * 512:(h + 1) * 512]
                nc.vector.tensor_tensor(v, v, ps[0:CAP, 2 * h + 1, :], ALU.mult).then_inc(s_hid, 1)

            def ye_out(e, gate, first=False):
                if not first:
                    dve.wait_ge(s_scat, 16 * e)
                for h in range(2):
                    dve.wait_ge(s_dn, 2 * e + h + 1)
                    last = nc.vector.tensor_scalar(ye[:, h * 512:(h + 1) * 512], ps[0:CAP, 4 + h, :], gate, None,
                                                   ALU.mult)
                last.then_inc(s_ye, 1)

            dve.wait_ge(s_rowst, 16 * NT)
            dve.wait_ge(s_base, 2 * NT)
            xeT_out(0)
            hid_half(0, 0)
            hid_half(0, 1)
            xeT_out(1)
            hid_half(1, 0)
            hid_half(1, 1)
            xeT_out(2)
            ye_out(0, gateT[:, 0:1], True)
            with dve.Fori(2, NE - 1) as e:
                hid_half(e, 0)
                hid_half(e, 1)
                xeT_out(e + 1)
                ye_out(e - 1, gateT[:, bass.ds(e - 1, 1)])
            hid_half(NE - 1, 0)
            hid_half(NE - 1, 1)
            ye_out(NE - 2, gateT[:, NE - 2:NE - 1])
            ye_out(NE - 1, gateT[:, NE - 1:NE])

            dve.wait_ge(s_ln2, 32)
            for t in range(NT):
                dve.wait_ge(s_fin[t], 16)
                ln_stats(t, fin[:, t, :], LN_EPS)
                ln_apply(t, fin[:, t, :], fin[:, t, :], gA, bA, s_y2)

        @block.tensor
        def _(pe):
            tr = [0]

            def unit(pairs, waits=()):
                n = tr[0]
                if n >= 2 and n < len(tr_units):
                    pe.wait_ge(*tr_units[n - 2])
                b = 2 * (n % 2)
                for half, lst in enumerate(pairs):
                    for col, src in lst:
                        k = src.shape[0]
                        w = 1
                        for s in src.shape[1:]:
                            w *= s
                        last = nc.tensor.transpose(ps[0:w, b + half, col:col + k], src, ident[0:k, 0:k])
                last.then_inc(s_tr, 1)
                tr[0] += 1

            def eight(src):
                return [[(j * P, src[:, (4 * half + j) * P:(4 * half + j + 1) * P]) for j in range(4)]
                        for half in range(2)]

            ng = [0]

            def group(g):
                n = ng[0]
                if n >= 4:
                    pe.wait_ge(s_projo, n - 3)
                bank = ps[:, 4 + n % 4, :]
                kind = g[0]
                if kind == "xbc":
                    m, s = g[1], g[2]
                    a, w = SEQS[s]
                    wsl = slotk[2] if m < 4 else slotk[0]
                    for k in range(KD):
                        last = nc.tensor.matmul(bank[:, 0:w * P], wsl[:, k, (m % 4) * P:(m % 4 + 1) * P],
                                                xT[:, k, a * P:(a + w) * P], start=(k == 0), stop=(k == KD - 1))
                else:
                    t = g[1]
                    lhs = [xT[:, k, t * P:(t + 1) * P] for k in range(KD)]
                    if kind == "kv":
                        wkv = slot[1][:, 0:KD * 256].rearrange("p (k c) -> p k c", k=KD)
                        wdt = slot[1][:, KD * 256:KD * 272].rearrange("p (k c) -> p k c", k=KD)
                        for k in range(KD):
                            nc.tensor.matmul(bank[:, 0:256], lhs[k], wkv[:, k, :], start=(k == 0), stop=(k == KD - 1))
                        for k in range(KD):
                            last = nc.tensor.matmul(bank[:, 256:272], lhs[k], wdt[:, k, :], start=(k == 0),
                                                    stop=(k == KD - 1))
                    else:
                        w = slotk[0] if kind == "q" else slotk[1]
                        for k in range(KD):
                            last = nc.tensor.matmul(bank, lhs[k], w[:, k, :], start=(k == 0), stop=(k == KD - 1))
                last.then_inc(s_proj, 1)
                ng[0] += 1

            pe.wait_ge(s_const, 16 * 3)
            pe.wait_ge(s_xa, 1)
            unit(eight(xa[:, 0, :]))
            for t in range(NT):
                if t + 1 < NT:
                    pe.wait_ge(s_xa, t + 2)
                    unit(eight(xa[:, t + 1, :]))
                pe.wait_ge(s_xT, t + 1)
                if t == 0:
                    pe.wait_ge(s_slot[0], 16)
                group(("q", t))
                if t == 0:
                    pe.wait_ge(s_slot[1], 32)
                group(("kv", t))
            pe.wait_ge(s_param, 16 * 11)
            unit([[(m * (TAPS + 1), cw_rows[:, m * P:(m + 1) * P]) for m in range(KC)]])
            pe.wait_ge(s_slot[2], 16)
            for g in xbc_groups:
                if g == ("xbc", 4, 0):
                    pe.wait_ge(s_slot[0], 32)
                group(g)
            pe.wait_ge(s_slot[1], 48)
            for g in z_groups:
                group(g)
            for t in range(NT):
                pe.wait_ge(s_rope, t + 1)
                unit([[(j * P, mix[:, t, j * P:(j + 1) * P]) for j in range(4)], [(0, kvd[:, t, 0:P])]])
            pe.wait_ge(s_silu, KC)
            for t in range(NT):
                c = conv_col(t)
                unit([[(m * P, conv[:, m, c:c + P]) for m in range(4)],
                      [(m * P, conv[:, 4 + m, c:c + P]) for m in range(2)]])
            pe.wait_ge(s_a, 1)
            pe.wait_ge(s_projo, len(groups))
            an = d16(ANEG)
            nc.tensor.matmul(ps[:, 4, 0:NT * NH], upto, an[:, :, 0:NH], start=True, stop=True)
            nc.tensor.matmul(ps[:, 4, NT * NH:2 * NT * NH], onward, an[:, :, NH:16], start=True, stop=True)
            pe.wait_ge(s_prep, 1)
            nc.tensor.matmul(ps[:, 5, 0:NT * 16], ones[:], dtw[:, ANEG, :], start=True, stop=True).then_inc(s_cum, 1)

            def scores(u):
                t, h = att_units[u]
                a, n = seq_of[t]
                hh = h // 4
                if u >= 3:
                    pe.wait_ge(s_exp, u - 2)
                nc.tensor.matmul(ps[:, u % 3, 0:n * P], qT[hh * 64:(hh + 1) * 64, h % 4, t * P:(t + 1) * P],
                                 kT[hh * 64:(hh + 1) * 64, a * P:(a + n) * P], start=True, stop=True).then_inc(s_sc, 1)

            def turn(u):
                t, h = att_units[u]
                n = seq_of[t][1]
                pe.wait_ge(s_exp, u + 1)
                if u >= 2:
                    pe.wait_ge(s_pts, u - 1)
                for b in range(n):
                    last = nc.tensor.transpose(ps[:, 3 + u % 2, b * P:(b + 1) * P],
                                               prob[:, u % 3, b * P:(b + 1) * P], ident)
                last.then_inc(s_pt, 1)

            def pv(u):
                t, h = att_units[u]
                a, n = seq_of[t]
                kvh = h // 4
                pe.wait_ge(s_pts, u + 1)
                if t >= 2 and u % NQ == 0:
                    pe.wait_ge(s_ao, t - 1)
                c = (u % NQ) * HD
                for b in range(n):
                    last = nc.tensor.matmul(ps[:, 5 + t % 2, c:c + HD], probT[:, u % 2, b * P:(b + 1) * P],
                                            kvd[:, a + b, P + kvh * HD:P + (kvh + 1) * HD],
                                            start=(b == 0), stop=(b == n - 1))
                last.then_inc(s_pv, 1)

            pe.wait_ge(s_qkT, NT)
            pe.wait_ge(s_xB, NT)
            pe.wait_ge(s_cums, 1)
            for i in range(NU + 3):
                if i < NU:
                    scores(i)
                if 2 <= i < NU + 2:
                    turn(i - 2)
                if i >= 3:
                    pv(i - 3)

            pe.wait_ge(s_ao, NT)
            for n, (d, t, g, i, first) in enumerate(upd):
                pe.wait_ge(s_ws, n + 1)
                if n >= 2:
                    pe.wait_ge(s_sts, n - 1)
                nc.tensor.matmul(ps[:, 5 + n % 2, 0:256], btok[:, t, g * P:(g + 1) * P], xsc[:, n % 2, :],
                                 start=True, stop=True).then_inc(s_st, 1)
            pe.wait_ge(s_pts, NU)
            pe.wait_ge(s_sts, len(upd))

            def decay(n):
                t, g = ssd_units[n]
                if n >= 2:
                    pe.wait_ge(s_edec, n - 1)
                for d, tri in ((0, upto), (1, onward)):
                    bank = ps[:, 2 * (n % 2) + d, :]
                    for h in range(HPG):
                        c = d * NH + g * HPG + h
                        nc.tensor.matmul(bank[:, h * P:(h + 1) * P], identb[:], maskb[:, d, :],
                                         start=True, stop=False)
                        last = nc.tensor.matmul(bank[:, h * P:(h + 1) * P],
                                                an[:, t, c:c + 1].broadcast_to([P, P]), tri,
                                                start=False, stop=True)
                last.then_inc(s_dec, 1)
                cc = conv_col(t)
                if n:
                    pe.wait_ge(s_cbs, n)
                nc.tensor.matmul(ps[:, 4, (n % 2) * P:(n % 2 + 1) * P], conv[:, 4 + g, cc:cc + P],
                                 conv[:, 6 + g, cc:cc + P], start=True, stop=True).then_inc(s_cb, 1)

            def y(n):
                t, g = ssd_units[n]
                cc = conv_col(t)
                pe.wait_ge(s_m, n + 1)
                if n:
                    pe.wait_ge(s_yo, n)
                for d in range(2):
                    if (d, t) in prev_at:
                        nc.tensor.matmul(ps[:, 5, d * 256:(d + 1) * 256], conv[:, 6 + g, cc:cc + P],
                                         state[:, d, g, prev_at[d, t], :], start=True, stop=True)
                for h in range(HPG):
                    last = nc.tensor.matmul(ps[:, 6 + n % 2, h * HD:(h + 1) * HD], msum[:, n % 2, h],
                                            xtok[:, t, (g * HPG + h) * HD:(g * HPG + h + 1) * HD],
                                            start=True, stop=True)
                last.then_inc(s_y, 1)

            decay(0)
            for n in range(len(ssd_units)):
                if n + 1 < len(ssd_units):
                    decay(n + 1)
                y(n)

            pe.wait_ge(s_edec, len(ssd_units))
            pe.wait_ge(s_yo, len(ssd_units))
            assert tr[0] == 3 * NT + 1

            def pair(t, src, freed=None):
                if freed:
                    pe.wait_ge(*freed)
                b = 2 * (t % 2)
                for j in range(KD):
                    last = nc.tensor.transpose(ps[:, b + j // 4, (j % 4) * P:(j % 4 + 1) * P],
                                               src[:, j * P:(j + 1) * P], ident)
                last.then_inc(s_tr, 1)

            for t in range(NT):
                pe.wait_ge(s_ssd, t + 1)
                pair(t, mix[:, t, :], (s_mixT, t - 1) if t >= 2 else None)

            def out_proj(t):
                pe.wait_ge(s_mixT, t + 1)
                if t >= 2:
                    pe.wait_ge(s_x1, t - 1)
                for h, w in ((0, slotk[2]), (1, slotk[0])):
                    if t == 0:
                        pe.wait_ge(s_slot[2 - 2 * h], 32 if h == 0 else 48)
                    for k in range(KD):
                        last = nc.tensor.matmul(ps[:, 4 + 2 * (t % 2) + h, :], xT[:, k, t * P:(t + 1) * P],
                                                w[:, k, :], start=(k == 0), stop=(k == KD - 1))
                last.then_inc(s_o, 1)

            def x1_turn(t):
                pe.wait_ge(s_x1, t + 1)
                pair(t, xa[:, t, :], (s_mixT, NT) if t < 2 else (s_x1T, t - 1))

            for t in range(NT):
                out_proj(t)
                if t:
                    x1_turn(t - 1)
            x1_turn(NT - 1)
            for t in range(NT):
                pe.wait_ge(s_x1T, t + 1)
                for k in range(KD):
                    last = nc.tensor.matmul(ps[:, 4, t * NE:(t + 1) * NE], xT[:, k, t * P:(t + 1) * P],
                                            wr[:, k, :], start=(k == 0), stop=(k == KD - 1))
            last.then_inc(s_lg, 1)
            pe.wait_ge(s_ple_in, 32)
            for b in range(3):
                for k in range(2):
                    for i in range(2):
                        last = nc.tensor.transpose(ps[:, b, k * 256 + i * P:k * 256 + (i + 1) * P],
                                                   ptok[:, 2 * b + i, k * P:(k + 1) * P], ident)
                last.then_inc(s_tr, 1)
            pe.wait_ge(s_lgd, 2)
            for t in range(NT):
                last = nc.tensor.transpose(ps[0:NE, 6 + t // 4, (t % 4) * P:(t % 4 + 1) * P],
                                           rt[:, 0, t * NE:(t + 1) * NE], ident)
            last.then_inc(s_affT, 1)

            pe.wait_ge(s_pT, 3)
            pe.wait_ge(s_bple, 16)
            wple = slot[0][:, 0:2048].rearrange("p (k c) -> p k c", k=2)
            for u in range(2 * NT):
                t, h = u // 2, u % 2
                if u == 2:
                    pe.wait_ge(s_top, 1)
                    nc.tensor.transpose(ps[0:CAP, 5, 0:NE], topf[:], ident[0:NE, 0:NE])
                    nc.tensor.transpose(ps[0:CAP, 5, NE:2 * NE], topv[:], ident[0:NE, 0:NE]).then_inc(s_topT, 1)
                if u >= 2:
                    pe.wait_ge(s_base, u - 1)
                if u == 0:
                    pe.wait_ge(s_slot[1], 64)
                    pe.wait_ge(s_slot[0], 64)
                if u == 1:
                    pe.wait_ge(s_slot[2], 48)
                w = slotk[1] if h == 0 else slotk[2]
                nc.tensor.matmul(ps[:, 2 * h, :], ones[0:1, :], gA[0:1, h * 512:(h + 1) * 512], start=True, stop=False)
                for k in range(KD):
                    nc.tensor.matmul(ps[:, 2 * h, :], xT[:, k, t * P:(t + 1) * P], w[:, k, :],
                                     start=False, stop=(k == KD - 1))
                for k in range(2):
                    last = nc.tensor.matmul(ps[:, 2 * h + 1, :], pT[:, k, t * P:(t + 1) * P],
                                            wple[:, k, h * 512:(h + 1) * 512], start=(k == 0), stop=(k == 1))
                last.then_inc(s_pg, 1)

            def turn8(src, done):
                for j in range(KD):
                    last = nc.tensor.transpose(ps[:, 6 + j // 4, (j % 4) * CAP:(j % 4 + 1) * CAP],
                                               src[:, j * P:(j + 1) * P], ident[0:CAP, 0:CAP])
                last.then_inc(done, 1)

            def rows_turn(e, hT=True):
                pe.wait_ge(s_gath, 16 * (e + 1))
                if hT:
                    pe.wait_ge(s_hT, e - 1)
                turn8(xe, s_xeT_p)

            def gate_up(e, h, first=False):
                if h == 0:
                    pe.wait_ge(s_xeT, e + 1)
                if not first:
                    pe.wait_ge(s_hid, 2 * e - 1 + h)
                for i, j in ((0, (3, 5)[h]), (1, (4, 0)[h])):
                    pe.wait_ge(s_slot[j], 16 * (e + 1) + (64 if j == 0 else 0))
                    for k in range(KD):
                        last = nc.tensor.matmul(ps[0:CAP, 2 * h + i, :], xeT[:, k, :], slotk[j][:, k, :],
                                                start=(k == 0), stop=(k == KD - 1))
                last.then_inc(s_gu, 1)

            def hid_turn(e, nxt=True):
                pe.wait_ge(s_hid, 2 * e + 2)
                if nxt:
                    pe.wait_ge(s_xeT, e + 2)
                turn8(hid, s_hT_p)

            def down(e, first=False):
                pe.wait_ge(s_hT, e + 1)
                if not first:
                    pe.wait_ge(s_ye, e)
                for h, j in ((0, 1), (1, 2)):
                    pe.wait_ge(s_slot[j], 16 * (e + 1) + (64 if j == 1 else 48))
                    for k in range(KD):
                        last = nc.tensor.matmul(ps[0:CAP, 4 + h, :], hidT[:, k, :], slotk[j][:, k, :],
                                                start=(k == 0), stop=(k == KD - 1))
                    last.then_inc(s_dn, 1)

            pe.wait_ge(s_base, 2 * NT)
            pe.wait_ge(s_idx, 2)
            rows_turn(0, hT=False)
            gate_up(0, 0, first=True)
            gate_up(0, 1, first=True)
            rows_turn(1, hT=False)
            gate_up(1, 0)
            hid_turn(0)
            gate_up(1, 1)
            rows_turn(2)
            down(0, first=True)
            with pe.Fori(2, NE - 1) as e:
                gate_up(e, 0)
                hid_turn(e - 1)
                gate_up(e, 1)
                rows_turn(e + 1)
                down(e - 1)
            gate_up(NE - 1, 0)
            hid_turn(NE - 2)
            gate_up(NE - 1, 1)
            down(NE - 2)
            hid_turn(NE - 1, nxt=False)
            down(NE - 1)


NAMES = ["x_prompt", "x_sample", "p_prompt", "p_sample", "ln_in_g", "ln_in_b", "w_in", "q_norm_w",
         "k_norm_w", "conv_w", "conv_b", "dt_bias", "a_log", "d_skip", "ssd_norm_w", "w_out", "ln1_g",
         "ln1_b", "w_router", "w_e_gate", "w_e_up", "w_e_down", "w_ple_gate", "b_ple_gate", "w_ple",
         "ln2_g", "ln2_b"]


def kernel(**inputs):
    import concourse.bacc as bacc
    from concourse.bass_utils import run_bass_kernel_spmd

    nc = bacc.Bacc("TRN2", target_bir_lowering=False, num_devices=1)
    arrays, A = {}, {}
    for name in NAMES:
        a = np.ascontiguousarray(inputs[name])
        arrays[f"in_{name}"] = a
        A[name] = nc.dram_tensor(f"in_{name}", a.shape, mybir.dt.from_np(a.dtype), kind="ExternalInput").ap()
    lengths = (inputs["x_prompt"].shape[1], inputs["x_sample"].shape[1])
    c = shape_constants(lengths)
    arrays["shape_constants"] = c
    consts = nc.dram_tensor("shape_constants", c.shape, F32, kind="ExternalInput").ap()
    outs = [nc.dram_tensor(f"out_{i}", (1, n, D), F32, kind="ExternalOutput").ap()
            for i, n in enumerate(lengths)]
    hymba_layer(nc, A, consts, *outs)
    r = run_bass_kernel_spmd(nc, [arrays], core_ids=[0])
    return tuple(r.results[0][f"out_{i}"] for i in range(2))
```

```python
from contextlib import ExitStack

import numpy as np

import concourse.bass as bass
from concourse import mybir

ALU = mybir.AluOpType
ACT = mybir.ActivationFunctionType
F32 = mybir.dt.float32
BF16 = mybir.dt.bfloat16
U32 = mybir.dt.uint32
I32 = mybir.dt.int32
X = mybir.AxisListType.X

P = 128
D = 1024
KD = D // P
HD = 64
NQ, NKV = 8, 2
NH = 8
GROUPS, HPG = 2, 4
NSTATE = 128
TAPS = 5
CONV = 1024
KC = CONV // P
NE = 16
PLE = 256
GRID_W = 64
THETA = 10000.0
NORM_EPS, LN_EPS = 1e-6, 1e-5
ALPHA = 2.0 ** 0.25
K0, V0, Z0, XBC0, DT0, IN_COLS = 512, 640, 768, 1280, 2304, 2320
NEG = -1e30


def shape_constants(lengths):
    i = np.arange(P)
    ident = np.eye(P)
    upto = (i[:, None] <= i[None, :]) * 1.0
    onward = (i[:, None] >= i[None, :]) * 1.0
    mask_f = np.where(upto > 0, 0.0, NEG)
    mask_b = np.where(onward > 0, 0.0, NEG)
    inv = THETA ** (-np.arange(HD // 4) / (HD // 4))
    cs = []
    for n in lengths:
        pos = np.stack([np.arange(n) // GRID_W, np.arange(n) % GRID_W], -1)
        ang = (pos[:, :, None] * inv).reshape(n // P, P, HD // 2)
        cs.append(np.stack([np.cos(ang), np.sin(ang)], 2))
    cs = np.concatenate(cs).transpose(1, 0, 2, 3).reshape(P, -1)
    return np.concatenate([ident, upto, onward, mask_f, mask_b, cs], 1).astype(np.float32)


def hymba_layer(nc, A, consts, out_prompt, out_sample):
    TP = A["x_prompt"].shape[1] // P
    TS = A["x_sample"].shape[1] // P
    NT = TP + TS
    T = NT * P
    SEQS = [(0, TP), (TP, TS)]
    CAPP, CAPS = TP * P * 2 // NE, TS * P * 2 // NE
    CAP = CAPP + CAPS
    PADW = TP * P + TS * P + 6
    CW = PADW - 4

    def conv_col(t):
        return t * P if t < TP else t * P + 2

    ctx = ExitStack()
    with ctx:
        def sb(name, shape, dt=F32):
            return ctx.enter_context(nc.sbuf_tensor(name, shape, dt))

        def sem(name):
            return ctx.enter_context(nc.semaphore(name))

        ring = sb("ring", [P, 3, KD * 512])
        late = sb("late", [P, KC * (PADW + CW)])
        xa = sb("xa", [P, NT, D])
        xT = sb("xT", [P, KD, T])
        mix = sb("mix", [P, NT, D])
        kvd = sb("kvd", [P, NT, 272])
        cst = sb("cst", [P, 5 * P + NT * 64])
        gb_in = sb("gb_in", [P, 2, D])
        gB, bB = sb("gB", [P, D]), sb("bB", [P, D])
        ssdw = sb("ssdw", [P, 512])
        qkw = sb("qkw", [P, 2, HD])
        hpar = sb("hpar", [P, 3, 16])
        maskb = sb("maskb", [P, 2, P], BF16)
        identb = sb("identb", [P, P], BF16)
        ones = sb("ones", [P, P])
        wr = sb("wr", [P, KD, NE])
        cw = sb("cw", [P, KC, TAPS + 1])
        stats = sb("stats", [P, 2, 12])
        mv = sb("mv", [P, NT, 2])
        sd = sb("sd", [P, 2, NT])
        qks = sb("qks", [P, 2, 3, 10])
        dtw = sb("dtw", [P, 9, NT * 16])
        att = sb("att", [P, 3, NT * NQ])
        gss = sb("gss", [P, 3, NT * GROUPS])
        rt = sb("rt", [P, 1, NT * NE])
        rs6 = sb("rs6", [P, 3, NT])
        topv = sb("topv", [NE, CAP])
        topi = sb("topi", [NE, CAP], U32)
        gateT = sb("gateT", [CAP, NE])
        idxT = sb("idxT", [CAP, NE], I32)
        idx_now = sb("idx_now", [CAP, 2], I32)
        qksq = sb("qksq", [P, 640])
        ps = ctx.enter_context(nc.psum_tensor("ps", [P, 8, 512], F32))

        x1_rows = nc.dram_tensor("x1_rows", (T, D), F32, kind="Internal").ap()
        acc_rows = nc.dram_tensor("acc_rows", (T, D), F32, kind="Internal").ap()

        ident = cst[:, 0:P]
        topf = cst[0:NE, 3 * P:3 * P + CAP]
        upto, onward = cst[:, P:2 * P], cst[:, 2 * P:3 * P]
        masks = cst[:, 3 * P:5 * P]
        rope = cst[:, 5 * P:].rearrange("p (t c a f) -> p t c a f", t=NT, c=2, a=2)
        u_pad = late[:, 0:KC * PADW].rearrange("p (m c) -> p m c", m=KC)
        conv = late[:, KC * PADW:].rearrange("p (m c) -> p m c", m=KC)
        cw_rows = late[0:TAPS + 1, KC * PADW + 6 * CW:KC * PADW + 6 * CW + CONV]
        xtok = late[:, 0:NT * 512].rearrange("p (t c) -> p t c", t=NT)
        btok = late[:, NT * 512:NT * 768].rearrange("p (t c) -> p t c", t=NT)
        slot = [ring[:, j, :] for j in range(3)] + [late[:, j * 4096:(j + 1) * 4096] for j in range(3)]
        slotk = [s.rearrange("p (k c) -> p k c", k=KD) for s in slot]
        gA, bA = gb_in[:, 0, :], gb_in[:, 1, :]
        qT = xT[:, 0:4, :]
        kz = xT[:, 4:6, :]
        s0, s1 = ring[:, 0, :], ring[:, 1, :]
        NPREV = sum(n - 1 for _, n in SEQS)
        state = s0[:, 0:4 * NPREV * 256].rearrange("p (d g n c) -> p d g n c", d=2, g=2, n=NPREV)
        prob = s1[:, 0:2048].rearrange("p (b c) -> p b c", b=4)
        dec = s1[:, 2048:3072].rearrange("p (d h l) -> p d h l", d=2, h=HPG)
        msum = s1[:, 3072:3584].rearrange("p (h l) -> p h l", h=HPG)
        offm = s1[:, 3584:4096].rearrange("p (d c) -> p d c", d=2)
        xrows = late[:, KC * PADW:KC * PADW + 4 * CW]
        probT = [xrows[:, 0:2048].rearrange("p (b c) -> p b c", b=4),
                 gb_in[:, :, :].rearrange("p a c -> p (a c)").rearrange("p (b c) -> p b c", b=4)]
        cbT = xrows[:, 2048:2176]
        yadd = xrows[:, 2176:2432]
        ysum = xrows[:, 2432:2688]
        ysq = xrows[:, 2688:2944]
        xsc = qksq[:, 0:512].rearrange("p (d c) -> p d c", d=2)
        rot = gb_in[:, 0, 0:512].rearrange("p (b c) -> p b c", b=2)
        mixf = mix[:, :, :].rearrange("p t c -> p (t c)")
        sig = mixf[:, 0:2048].rearrange("p (b c) -> p b c", b=4)
        affw = mixf[0:NE, 2048:2048 + 2 * T].rearrange("p (b c) -> p b c", b=2)
        xe = mixf[0:CAP, 5 * D:6 * D]
        kvf = kvd[:, :, :].rearrange("p t c -> p (t c)")
        ptok = kvf[:, 0:NT * PLE].rearrange("p (t c) -> p t c", t=NT)
        pT = kvf[:, 0:NT * PLE].rearrange("p (k c) -> p k c", k=2)
        wple = gb_in
        bple = [qksq[0:1, 0:512], dtw[0:1, 0:6, :].rearrange("p r c -> p (r c)")[:, 0:512]]
        xaf = xa[:, :, :].rearrange("p t c -> p (t c)")
        xeT = xaf[:, 0:KD * CAP].rearrange("p (k c) -> p k c", k=KD)
        hidT = xaf[:, 1024:1024 + KD * CAP].rearrange("p (k c) -> p k c", k=KD)
        hid = xaf[0:CAP, 2048:3072]
        ye = xaf[0:CAP, 3072:4096]
        fin = xT[:, :, :].rearrange("p k c -> p (k c)").rearrange("p (t c) -> p t c", t=NT)

        s_const = sem("s_const")
        s_tab = sem("s_tab")
        s_param = sem("s_param")
        s_xin = [sem(f"s_xin{t}") for t in range(NT)]
        s_slot = [sem(f"s_slot{j}") for j in range(6)]
        s_ple_in = sem("s_ple_in")
        s_dve = sem("s_dve")
        s_act = sem("s_act")
        s_pool = sem("s_pool")
        s_prep = sem("s_prep")
        s_var = sem("s_var")
        s_std = sem("s_std")
        s_xa = sem("s_xa")
        s_tr = sem("s_tr")
        s_xT = sem("s_xT")
        s_cw = sem("s_cw")
        s_proj = sem("s_proj")
        s_projo = sem("s_projo")
        s_rr = sem("s_rr")
        s_rope = sem("s_rope")
        s_kz = sem("s_kz")
        s_conv = sem("s_conv")
        s_silu = sem("s_silu")
        s_qkT = sem("s_qkT")
        s_xB = sem("s_xB")
        s_dt1 = sem("s_dt1")
        s_dt2 = sem("s_dt2")
        s_a = sem("s_a")
        s_cum = sem("s_cum")
        s_cums = sem("s_cums")
        s_ecum = sem("s_ecum")
        s_sc = sem("s_sc")
        s_max = sem("s_max")
        s_exp = sem("s_exp")
        s_rc = sem("s_rc")
        s_pn = sem("s_pn")
        s_pt = sem("s_pt")
        s_pts = sem("s_pts")
        s_pv = sem("s_pv")
        s_ao = sem("s_ao")
        s_ws = sem("s_ws")
        s_st = sem("s_st")
        s_sts = sem("s_sts")
        s_dec = sem("s_dec")
        s_edec = sem("s_edec")
        s_off = sem("s_off")
        s_offm = sem("s_offm")
        s_t = sem("s_t")
        s_cb = sem("s_cb")
        s_cbs = sem("s_cbs")
        s_tfb = sem("s_tfb")
        s_m = sem("s_m")
        s_y = sem("s_y")
        s_yo = sem("s_yo")
        s_yz = sem("s_yz")
        s_gs = sem("s_gs")
        s_ssd = sem("s_ssd")
        s_mixT = sem("s_mixT")
        s_o = sem("s_o")
        s_res = sem("s_res")
        s_x1 = sem("s_x1")
        s_x1T = sem("s_x1T")
        s_rowst = sem("s_rowst")
        s_lg = sem("s_lg")
        s_lge = sem("s_lge")
        s_lgd = sem("s_lgd")
        s_affT = sem("s_affT")
        s_top = sem("s_top")
        s_topT = sem("s_topT")
        s_idx = sem("s_idx")
        s_pT = sem("s_pT")
        s_pg = sem("s_pg")
        s_sig = sem("s_sig")
        s_base = sem("s_base")
        s_acc = [sem(f"s_acc{i}") for i in range(4)]
        s_wple = sem("s_wple")
        s_gath = sem("s_gath")
        s_idg = sem("s_idg")
        s_xeT_p = sem("s_xeT_p")
        s_xeT = sem("s_xeT")
        s_gu = sem("s_gu")
        s_hs = sem("s_hs")
        s_hid = sem("s_hid")
        s_hT_p = sem("s_hT_p")
        s_hT = sem("s_hT")
        s_dn = sem("s_dn")
        s_ye = sem("s_ye")
        s_scat = sem("s_scat")
        s_fin = [sem(f"s_fin_{t}") for t in range(NT)]
        s_ln2 = sem("s_ln2")
        s_bple = sem("s_bple")
        s_y2 = sem("s_y2")
        s_out = sem("s_out")

        tok_groups = [(kind, t) for t in range(NT) for kind in ("q", "kv")]
        xbc_groups = [("xbc", m, s) for m in range(KC) for s in range(2)]
        z_groups = [("z", t) for t in range(NT)]
        groups = tok_groups + xbc_groups + z_groups
        gidx = {g: n for n, g in enumerate(groups)}
        COLS = {"q": (0, K0), "kv": (K0, 256), "z": (0, 512)}
        tr_units = [(s_xT, t + 1) for t in range(NT)] + [(s_cw, 1)] \
            + [(s_xB, t + 1) for t in range(NT)] + [(s_qkT, t + 1) for t in range(NT)]
        U_XB, U_QK = NT + 1, 2 * NT + 1
        att_units = [(t, 4 * i + j) for t in range(NT) for i in range(NKV) for j in range(4)]
        NU = len(att_units)
        NG = NU // 4
        seq_of = {t: (a, n) for a, n in SEQS for t in range(a, a + n)}
        ssd_units = [(t, g) for t in range(NT) for g in range(GROUPS)]
        assert len(ssd_units) == NG
        EARLY = 8
        ple_units = [(h, t) for h in range(2) for t in range(NT)]
        upd = []
        n0 = 0
        prev_at = {}
        for a, n in SEQS:
            for i in range(n - 1):
                prev_at[0, a + 1 + i] = n0 + i
                prev_at[1, a + n - 2 - i] = n0 + i
                for g in range(GROUPS):
                    upd.append((0, a + i, g, n0 + i, i == 0))
                    upd.append((1, a + n - 1 - i, g, n0 + i, i == 0))
            n0 += n - 1

        DT, ANEG, ACUM, NACUM, EA, WDEC, CD, W1, W2 = range(9)

        def d16(r):
            return dtw[:, r, :].rearrange("p (t c) -> p t c", t=NT)

        block = ctx.enter_context(nc.Block())

        class Chain:

            def __init__(self, eng, s):
                self.eng, self.s, self.n = eng, s, 0

            def step(self, ins):
                self.n += 1
                ins.then_inc(self.s, 1)

            def settle(self):
                self.eng.wait_ge(self.s, self.n)

            def link(self, ins):
                self.step(ins)
                self.settle()

        @block.sync
        def _(sp):
            win = A["w_in"][0].rearrange("(k p) c -> p k c", p=P)
            wout = A["w_out"][0].rearrange("(k p) c -> p k c", p=P)
            wpg = A["w_ple_gate"][0].rearrange("(k p) c -> p k c", p=P)

            def xtile(name, i):
                return A[name][0][i * P:(i + 1) * P, :]

            def bc(ap):
                return ap.partition_broadcast(P)

            def load_x(t):
                src = xtile("x_prompt", t) if t < TP else xtile("x_sample", t - TP)
                sp.dma_start(xa[:, t, :], src).then_inc(s_xin[t], 16)

            load_x(0)
            sp.dma_start(cst[:, 0:P], consts[:, 0:P]).then_inc(s_const, 16)
            sp.dma_start(gA, bc(A["ln_in_g"])).then_inc(s_const, 16)
            sp.dma_start(bA, bc(A["ln_in_b"])).then_inc(s_const, 16)
            load_x(1)
            sp.dma_start(slotk[0], win[:, :, 0:K0]).then_inc(s_slot[0], 16)
            load_x(2)
            sp.dma_start(slot[1][:, 0:KD * 256].rearrange("p (k c) -> p k c", k=KD),
                         win[:, :, K0:Z0]).then_inc(s_slot[1], 16)
            sp.dma_start(slot[1][:, KD * 256:KD * 272].rearrange("p (k c) -> p k c", k=KD),
                         win[:, :, DT0:IN_COLS]).then_inc(s_slot[1], 16)
            sp.dma_start(cst[:, P:], consts[:, P:]).then_inc(s_tab, 16)
            for t in range(3, NT):
                load_x(t)
            sp.dma_start(slotk[2], win[:, :, XBC0:XBC0 + 512]).then_inc(s_slot[2], 16)
            small2 = [(gB[:], bc(A["ln1_g"][0])), (bB[:], bc(A["ln1_b"][0])),
                      (ssdw[:], bc(A["ssd_norm_w"][0])),
                      (qkw[:, 0, :], bc(A["q_norm_w"][0])), (qkw[:, 1, :], bc(A["k_norm_w"][0])),
                      (hpar[:, 0, :], bc(A["dt_bias"][0].rearrange("d h -> (d h)"))),
                      (hpar[:, 1, :], bc(A["a_log"][0].rearrange("d h -> (d h)"))),
                      (hpar[:, 2, 0:NH], bc(A["d_skip"][0])),
                      (wr[:], A["w_router"][0].rearrange("(k p) e -> p k e", p=P)),
                      (cw_rows[0:TAPS, :], A["conv_w"][0]), (cw_rows[TAPS:TAPS + 1, :], A["conv_b"])]
            for dst, src in small2:
                sp.dma_start(dst, src).then_inc(s_param, 16)
            sp.wait_ge(s_proj, gidx["q", NT - 1] + 1)
            sp.dma_start(slotk[0], win[:, :, XBC0 + 512:DT0]).then_inc(s_slot[0], 16)
            sp.wait_ge(s_proj, gidx["kv", NT - 1] + 1)
            sp.dma_start(slotk[1], win[:, :, Z0:XBC0]).then_inc(s_slot[1], 16)
            sp.wait_ge(s_proj, gidx["xbc", 3, 1] + 1)

            def load_wout(j, h):
                c = slice(h * 512, (h + 1) * 512)
                for i in range(2):
                    rows = A["w_out"][0][i * 256:(i + 1) * 256, c].rearrange("(k p) c -> p k c", p=HD)
                    sp.dma_start(slotk[j][i * HD:(i + 1) * HD, 0:4, :], rows).then_inc(s_slot[j], 16)
                sp.dma_start(slotk[j][:, 4:8, :], wout[:, 4:8, c]).then_inc(s_slot[j], 16)

            load_wout(2, 0)
            sp.wait_ge(s_ao, NG)
            sp.wait_ge(s_yo, NG)
            load_wout(0, 1)
            pt = [(ptok[:, 0:TP, :], A["p_prompt"][0, 0]), (ptok[:, TP:NT, :], A["p_sample"][0, 0])]
            for dst, src in pt:
                sp.dma_start(dst, src.rearrange("(t p) c -> p t c", p=P)).then_inc(s_ple_in, 16)
            sp.dma_start(slotk[1], wpg[:, :, 0:512]).then_inc(s_slot[1], 16)
            sp.dma_start(wple[:], A["w_ple"][0].rearrange("(k p) c -> p k c", p=P)).then_inc(s_wple, 16)
            for h in range(2):
                sp.dma_start(bple[h], A["b_ple_gate"][:, h * 512:(h + 1) * 512]).then_inc(s_bple, 16)

            wg = A["w_e_gate"][0].rearrange("e (k p) f -> e p k f", p=P)
            wu = A["w_e_up"][0].rearrange("e (k p) f -> e p k f", p=P)
            wd = A["w_e_down"][0].rearrange("e (k p) f -> e p k f", p=P)

            def load(j, w, e, h):
                sp.dma_start(slotk[j], w[e, :, :, h * 512:(h + 1) * 512]).then_inc(s_slot[j], 16)

            sp.wait_ge(s_gs, NG)
            load(3, wg, 0, 0)
            load(4, wu, 0, 0)
            load(5, wg, 0, 1)
            sp.wait_ge(s_o, NT)
            sp.dma_start(slotk[2], wpg[:, :, 512:D]).then_inc(s_slot[2], 16)
            load(0, wu, 0, 1)
            sp.wait_ge(s_pg, NT)
            load(1, wd, 0, 0)
            sp.wait_ge(s_pg, 2 * NT)
            load(2, wd, 0, 1)
            sp.dma_start(gA, bc(A["ln2_g"][0])).then_inc(s_ln2, 16)
            sp.dma_start(bA, bc(A["ln2_b"][0])).then_inc(s_ln2, 16)

            def load_gate_up(e):
                sp.wait_ge(s_gu, 2 * e - 1)
                load(3, wg, e, 0)
                load(4, wu, e, 0)
                sp.wait_ge(s_gu, 2 * e)
                load(5, wg, e, 1)
                load(0, wu, e, 1)

            def load_down(e):
                sp.wait_ge(s_dn, 2 * e - 1)
                load(1, wd, e, 0)
                sp.wait_ge(s_dn, 2 * e)
                load(2, wd, e, 1)

            load_gate_up(1)
            with sp.Fori(1, NE - 1) as e:
                load_gate_up(e + 1)
                load_down(e)
            load_down(NE - 1)
            sp.wait_ge(s_scat, 16 * NE)
            for t in range(NT):
                sp.dma_start(fin[:, t, :], acc_rows[t * P:(t + 1) * P, :]).then_inc(s_fin[t], 16)
            for t in range(NT):
                sp.wait_ge(s_y2, t + 1)
                dst = out_prompt[0] if t < TP else out_sample[0]
                i = t if t < TP else t - TP
                sp.dma_start(dst[i * P:(i + 1) * P, :], fin[:, t, :]).then_inc(s_out, 16)
            sp.wait_ge(s_out, 16 * NT)
            sp.wait_ge(s_rowst, 16 * NT)
            for s in s_acc:
                sp.wait_ge(s, 16 * (2 * NT // 4))

        @block.gpsimd
        def _(pool):
            ch = Chain(pool, s_pool)
            nc.gpsimd.memset(ones[:], 1.0)
            for c0, w in ((0, 2), (2 + TP * P, 2), (4 + T, 2)):
                nc.gpsimd.memset(u_pad[:, :, c0:c0 + w], 0.0)
            pool.wait_ge(s_const, 16 * 3)
            pool.wait_ge(s_tab, 16)
            nc.gpsimd.tensor_copy(maskb[:], masks.rearrange("p (d l) -> p d l", d=2))
            nc.gpsimd.tensor_copy(identb[:], ident).then_inc(s_prep, 1)
            pool.wait_ge(s_xa, NT)
            for t in range(NT):
                pool.wait_ge(s_rr, t + 1)
                for src, h0, n, w in ((mix[:, t, 0:512], 0, NQ, 0), (kvd[:, t, 0:P], NQ, NKV, 1)):
                    v = src.rearrange("p (h c) -> p h c", c=HD)
                    rs = qks[:, t % 2, 2, h0:h0 + n].unsqueeze(2).broadcast_to([P, n, HD])
                    ch.link(nc.gpsimd.tensor_tensor(v, v, rs, ALU.mult))
                    wb = qkw[:, w, :].unsqueeze(1).broadcast_to([P, n, HD])
                    ch.link(nc.gpsimd.tensor_tensor(v, v, wb, ALU.mult))
                    halves = src.rearrange("p (h a i f) -> p i h a f", a=2, i=2, f=16)
                    x1, x2 = halves[:, 0], halves[:, 1]
                    c, sn = [rope[:, t, i].unsqueeze(1).broadcast_to([P, n, 2, 16]) for i in range(2)]
                    tmp = [rot[:, i, 0:n * 32].rearrange("p (h a f) -> p h a f", a=2, f=16) for i in range(2)]
                    ch.step(nc.gpsimd.tensor_tensor(tmp[0], x2, sn, ALU.mult))
                    ch.link(nc.gpsimd.tensor_tensor(tmp[1], x1, sn, ALU.mult))
                    ch.step(nc.gpsimd.tensor_tensor(x1, x1, c, ALU.mult))
                    ch.link(nc.gpsimd.tensor_tensor(x2, x2, c, ALU.mult))
                    ch.step(nc.gpsimd.tensor_tensor(x1, x1, tmp[0], ALU.subtract))
                    last = nc.gpsimd.tensor_tensor(x2, x2, tmp[1], ALU.add)
                    if w == 0:
                        ch.link(last)
                last.then_inc(s_rope, 1)
                pool.wait_ge(s_rope, t + 1)
            pool.wait_ge(s_cums, 2)
            pool.wait_ge(s_xB, NT)
            for n, (d, t, g, i, first) in enumerate(upd):
                if n >= 2:
                    pool.wait_ge(s_st, n - 1)
                o = xsc[:, n % 2, :].rearrange("p (h c) -> p h c", h=HPG)
                xin = xtok[:, t, g * 256:(g + 1) * 256].rearrange("p (h c) -> p h c", h=HPG)
                w = d16(WDEC)[:, t, d * NH + g * HPG:d * NH + (g + 1) * HPG]
                nc.gpsimd.tensor_tensor(o, xin, w.unsqueeze(2).broadcast_to([P, HPG, HD]),
                                        ALU.mult).then_inc(s_ws, 1)
            pool.wait_ge(s_proj, len(groups))
            nc.gpsimd.memset(kz, 0.0).then_inc(s_kz, 1)

            def heads(ap):
                return ap.rearrange("p (h c) -> p h c", h=HPG)

            def normalise(u):
                L = seq_of[att_units[u][0]][1] * P
                pool.wait_ge(s_rc, u + 1)
                nc.gpsimd.tensor_scalar(prob[:, u % 4, 0:L], prob[:, u % 4, 0:L], att[:, 2, u:u + 1], None,
                                        ALU.mult).then_inc(s_pn, 1)

            def ssd_sums(n):
                t, g = ssd_units[n]
                pool.wait_ge(s_tfb, n + 1)
                if n:
                    pool.wait_ge(s_y, n)
                nc.gpsimd.tensor_tensor(msum, dec[:, 0], dec[:, 1], ALU.add).then_inc(s_m, 1)
                if n:
                    pool.wait_ge(s_yo, n)
                pool.wait_ge(s_offm, n + 1)
                dsk = hpar[:, 2, g * HPG:(g + 1) * HPG].unsqueeze(2).broadcast_to([P, HPG, HD])
                ch.link(nc.gpsimd.tensor_tensor(heads(yadd), heads(xtok[:, t, g * 256:(g + 1) * 256]), dsk, ALU.mult))
                dirs = [d for d in range(2) if (d, t) in prev_at]
                for d in dirs:
                    last = nc.gpsimd.tensor_tensor(yadd, yadd, offm[:, d, :], ALU.add)
                    if d != dirs[-1]:
                        ch.link(last)
                last.then_inc(s_t, 1)

            def gate(n):
                t, g = ssd_units[n]
                pool.wait_ge(s_yo, n + 1)
                z = mix[:, t, 512 + g * 256:512 + (g + 1) * 256]
                nc.gpsimd.tensor_tensor(z, ysum, z, ALU.mult).then_inc(s_yz, 1)

            pool.wait_ge(s_param, 16 * 11)
            for i in range(NU + 1):
                if i:
                    normalise(i - 1)
                if i % 4 == 2:
                    ssd_sums(i // 4)
                if i % 4 == 0 and i:
                    gate(i // 4 - 1)
            for t in range(NT):
                pool.wait_ge(s_x1, t + 1)
                pool.dma_start(x1_rows[t * P:(t + 1) * P, :], xa[:, t, :]).then_inc(s_rowst, 16)

            def gather():
                pool.indirect_dma_start(xe, None, x1_rows,
                                        bass.IndirectOffsetOnAxis(ap=idx_now[:, 0:1], axis=0)
                                        ).then_inc(s_gath, 16)

            for u, (h, t) in enumerate(ple_units):
                pool.wait_ge(s_base, u + 1)
                pool.dma_start(acc_rows[t * P:(t + 1) * P, h * 512:(h + 1) * 512],
                               sig[:, u % 4, :]).then_inc(s_acc[u % 4], 16)
                if u == 7:
                    pool.wait_ge(s_rowst, 16 * NT)
                    pool.wait_ge(s_idx, 2)
                    ch.link(nc.gpsimd.tensor_copy(idx_now[:, 0:1], idxT[:, 0:1]))
                    gather()
            for s in s_acc:
                pool.wait_ge(s, 16 * (2 * NT // 4))

            def scatter():
                pool.indirect_dma_start(acc_rows, bass.IndirectOffsetOnAxis(ap=idx_now[:, 1:2], axis=0),
                                        ye, None, compute_op=ALU.add).then_inc(s_scat, 16)

            def pick(col, e):
                return nc.gpsimd.tensor_copy(idx_now[:, col:col + 1], idxT[:, bass.ds(e, 1)])

            pool.wait_ge(s_xeT_p, 1)
            ch.link(pick(0, 1))
            gather()
            with pool.Fori(1, NE - 1) as f:
                pool.wait_ge(s_xeT_p, f + 1)
                pick(0, f + 1)
                pick(1, f - 1).then_inc(s_idg, 1)
                pool.wait_ge(s_const, 16 * 3)
                pool.wait_ge(s_idg, f)
                gather()
                pool.wait_ge(s_const, 16 * 3)
                pool.wait_ge(s_ye, f)
                scatter()
                pool.wait_ge(s_scat, 16 * f)
            for e in (NE - 2, NE - 1):
                ch.link(pick(1, e))
                pool.wait_ge(s_ye, e + 1)
                scatter()
                pool.wait_ge(s_scat, 16 * (e + 1))

        @block.scalar
        def _(act):
            ch = Chain(act, s_act)
            nvar = [0]

            def root():
                nvar[0] += 1
                act.wait_ge(s_var, nvar[0])

            def copy(o, i):
                return nc.scalar.activation(o, i, ACT.Copy)

            def x_std(t):
                root()
                nc.scalar.activation(sd[:, 0, t:t + 1], sd[:, 0, t:t + 1], ACT.Sqrt).then_inc(s_std, 1)

            x_std(0)
            x_std(1)
            n = 0
            for g in groups:
                if g[0] == "q" and g[1] + 2 < NT:
                    x_std(g[1] + 2)
                act.wait_ge(s_proj, n + 1)
                bank = ps[:, 4 + n % 4, :]
                if g[0] == "q":
                    copy(mix[:, g[1], 0:512].rearrange("p (j i c) -> p i j c", i=2, j=4),
                         bank.rearrange("p (i j c) -> p i j c", i=2, j=4)).then_inc(s_projo, 1)
                elif g[0] == "kv":
                    copy(kvd[:, g[1], :], bank[:, 0:272]).then_inc(s_projo, 1)
                elif g[0] == "xbc":
                    a, w = SEQS[g[2]]
                    c0 = 2 + a * P + 2 * g[2]
                    copy(u_pad[:, g[1], c0:c0 + w * P], bank[:, 0:w * P]).then_inc(s_projo, 1)
                    if g[2] == 1 and g[1] < NT:
                        root()
                        nc.scalar.activation(qks[:, g[1] % 2, 1, :], qks[:, g[1] % 2, 0, :],
                                             ACT.Sqrt).then_inc(s_std, 1)
                    if g[1:] == (NT, 1):
                        act.wait_ge(s_dt1, 1)
                        nc.scalar.activation(dtw[:, W1, :], dtw[:, W1, :], ACT.Exp)
                        nc.scalar.activation(hpar[:, 1, :], hpar[:, 1, :], ACT.Exp).then_inc(s_dt2, 1)
                        act.wait_ge(s_dt1, 2)
                        nc.scalar.activation(dtw[:, ACUM, :], dtw[:, W2, :], ACT.Ln).then_inc(s_dt2, 1)
                else:
                    if g[1] == 0:
                        for m in range(KC):
                            act.wait_ge(s_conv, m + 1)
                            nc.scalar.activation(conv[:, m, :], conv[:, m, :], ACT.Silu).then_inc(s_silu, 1)
                        act.wait_ge(s_proj, n + 1)
                    nc.scalar.activation(mix[:, g[1], 512:D], ps[:, 4 + n % 2, :], ACT.Silu).then_inc(s_projo, 1)
                    if g[1] == 0:
                        act.wait_ge(s_cums, 1)
                        nc.scalar.activation(dtw[:, EA, :], dtw[:, ACUM, :], ACT.Exp)
                        nc.scalar.activation(dtw[:, WDEC, :], dtw[:, W1, :], ACT.Exp)
                        nc.scalar.activation(dtw[:, CD, :], dtw[:, CD, :], ACT.Exp).then_inc(s_ecum, 1)
                    elif g[1] <= 3:
                        for t in (2 * g[1] - 2, 2 * g[1] - 1):
                            u = U_XB + t
                            act.wait_ge(s_tr, u + 1)
                            b = 2 * (u % 2)
                            copy(xtok[:, t, :], ps[:, b, :])
                            copy(btok[:, t, :], ps[:, b + 1, 0:256]).then_inc(s_xB, 1)
                n += 1
            act.wait_ge(s_kz, 1)
            for t in range(NT):
                u = U_QK + t
                act.wait_ge(s_tr, u + 1)
                b = 2 * (u % 2)
                tc = slice(t * P, (t + 1) * P)
                copy(qT[:, :, tc], ps[:, b, :].rearrange("p (j c) -> p j c", j=4))
                for i in range(NKV):
                    last = copy(kz[i * HD:(i + 1) * HD, i, tc], ps[i * HD:(i + 1) * HD, b + 1, 0:P])
                last.then_inc(s_qkT, 1)

            def probabilities(u):
                L = seq_of[att_units[u][0]][1] * P
                act.wait_ge(s_max, u + 1)
                if u >= 4:
                    act.wait_ge(s_pt, u - 3)
                nc.scalar.activation(prob[:, u % 4, 0:L], ps[:, u % 3, 0:L], ACT.Exp,
                                     bias=att[:, 0, u:u + 1], scale=HD ** -0.5,
                                     accum_out=att[:, 1, u:u + 1]).then_inc(s_exp, 1)

            def decays(n, d):
                t, g = ssd_units[n]
                act.wait_ge(s_dec, n + 1)
                if n:
                    act.wait_ge(s_m, n)
                for h in range(HPG):
                    c = d * NH + g * HPG + h
                    last = nc.scalar.activation(dec[:, d, h], ps[:, 5 + d, h * P:(h + 1) * P],
                                                ACT.Exp, bias=d16(NACUM)[:, t, c:c + 1])
                last.then_inc(s_edec, 1)

            def squares(n):
                t, g = ssd_units[n]
                act.wait_ge(s_yz, n + 1)
                if n:
                    act.wait_ge(s_gs, n)
                nc.scalar.activation(ysq, mix[:, t, 512 + g * 256:512 + (g + 1) * 256], ACT.Square,
                                     accum_out=gss[:, 0, n:n + 1]).then_inc(s_gs, 1)

            def group_root(a, b):
                root()
                nc.scalar.activation(gss[:, 1, a:b], gss[:, 1, a:b], ACT.Sqrt).then_inc(s_std, 1)

            for i in range(NU + 1):
                if i < NU:
                    probabilities(i)
                    if i % 4 < 2:
                        decays(i // 4, i % 4)
                if i % 4 == 2 and i > 4:
                    squares(i // 4 - 1)
                if i == 4 * EARLY + 6:
                    group_root(0, EARLY)
            squares(NG - 1)
            group_root(EARLY, NG)

            def mix_turned(t):
                act.wait_ge(s_tr, 3 * NT + 1 + t + 1)
                copy(xT[:, 4:8, t * P:(t + 1) * P],
                     ps[:, t % 4, :].rearrange("p (k c) -> p k c", k=4)).then_inc(s_mixT, 1)

            for t in range(NT):
                mix_turned(t)
            act.wait_ge(s_tr, 4 * NT + 2)
            for b in range(3):
                last = copy(pT[:, :, 2 * b * P:2 * (b + 1) * P],
                            ps[:, b, :].rearrange("p (k c) -> p k c", k=2))
            last.then_inc(s_pT, 1)

            def sigmoid(u):
                act.wait_ge(s_pg, u + 1)
                if u >= 4:
                    act.wait_ge(s_acc[u % 4], 16 * (u // 4))
                nc.scalar.activation(sig[:, u % 4, :], ps[:, 2 * (u % 2), :], ACT.Sigmoid).then_inc(s_sig, 1)

            for t in range(NT):
                root()
                nc.scalar.activation(sd[:, 0, t:t + 1], sd[:, 0, t:t + 1], ACT.Sqrt).then_inc(s_std, 1)
                act.wait_ge(s_tr, 4 * NT + 2 + t + 1)
                b = 2 * (t % 2)
                for half in range(2):
                    last = copy(xT[:, 4 * half:4 * half + 4, t * P:(t + 1) * P],
                                ps[:, b + half, :].rearrange("p (k c) -> p k c", k=4))
                last.then_inc(s_x1T, 1)
            sigmoid(0)
            act.wait_ge(s_lgd, 1)
            nc.scalar.activation(rt[:, 0, :], rt[:, 0, :], ACT.Exp).then_inc(s_lge, 1)
            for u in range(1, 2 * NT):
                sigmoid(u)

            def silu_half(e, h):
                act.wait_ge(s_gu, 2 * e + h + 1)
                nc.scalar.activation(hid[:, h * 512:(h + 1) * 512], ps[0:CAP, 2 * h, :],
                                     ACT.Silu).then_inc(s_hs, 1)

            def hidT_out(e):
                act.wait_ge(s_hT_p, e + 1)
                for half in range(2):
                    last = copy(hidT[:, 4 * half:4 * half + 4, :],
                                ps[:, 6 + half, 0:4 * CAP].rearrange("p (k c) -> p k c", k=4))
                last.then_inc(s_hT, 1)

            act.wait_ge(s_base, 2 * NT)
            silu_half(0, 0)
            silu_half(0, 1)
            with act.Fori(1, NE) as e:
                act.wait_ge(s_hT_p, e)
                for half in range(2):
                    last = copy(hidT[:, 4 * half:4 * half + 4, :],
                                ps[:, 6 + half, 0:4 * CAP].rearrange("p (k c) -> p k c", k=4))
                last.then_inc(s_hT, 1)
                silu_half(e, 0)
                silu_half(e, 1)
            hidT_out(NE - 1)
            for t in range(NT):
                root()
                nc.scalar.activation(sd[:, 0, t:t + 1], sd[:, 0, t:t + 1], ACT.Sqrt).then_inc(s_std, 1)

        @block.vector
        def _(dve):
            ch = Chain(dve, s_dve)
            nroot = [0]

            def ln_stats(t, src, eps):
                for half in range(2):
                    ch.step(nc.vector.bn_stats(stats[:, t % 2, 6 * half:6 * half + 6],
                                               src[:, half * 512:(half + 1) * 512]))
                ch.settle()
                ch.link(nc.vector.bn_aggr(mv[:, t, :], stats[:, t % 2, :]))
                nc.vector.tensor_scalar(sd[:, 0, t:t + 1], mv[:, t, 1:2], eps, None, ALU.add).then_inc(s_var, 1)

            def ln_apply(t, x, o, g, b, done):
                nroot[0] += 1
                dve.wait_ge(s_std, nroot[0])
                ch.link(nc.vector.reciprocal(sd[:, 1, t:t + 1], sd[:, 0, t:t + 1]))
                ch.link(nc.vector.tensor_scalar(o, x, mv[:, t, 0:1], sd[:, 1, t:t + 1], ALU.subtract, ALU.mult))
                ch.link(nc.vector.tensor_tensor(o, o, g[:], ALU.mult))
                nc.vector.tensor_tensor(o, o, b[:], ALU.add).then_inc(done, 1)

            def xT_out(t):
                dve.wait_ge(s_tr, t + 1)
                b = 2 * (t % 2)
                for half in range(2):
                    last = nc.vector.tensor_copy(xT[:, 4 * half:4 * half + 4, t * P:(t + 1) * P],
                                                 ps[:, b + half, :].rearrange("p (k c) -> p k c", k=4))
                last.then_inc(s_xT, 1)

            for t in range(NT):
                dve.wait_ge(s_xin[t], 16)
                ln_stats(t, xa[:, t, :], LN_EPS)
                dve.wait_ge(s_const, 16 * 3)
                ln_apply(t, xa[:, t, :], xa[:, t, :], gA, bA, s_xa)
                if t:
                    xT_out(t - 1)
            xT_out(NT - 1)
            dve.wait_ge(s_tr, NT + 1)
            b = 2 * (NT % 2)
            nc.vector.tensor_copy(cw[:], ps[:, b, 0:KC * (TAPS + 1)].rearrange("p (m j) -> p m j", m=KC)
                                  ).then_inc(s_cw, 1)
            dve.wait_ge(s_cw, 1)

            def qk_rms(t):
                dve.wait_ge(s_projo, gidx["kv", t] + 1)
                q = mix[:, t, 0:512]
                k = kvd[:, t, 0:P]
                sq = qksq[:]
                ch.step(nc.vector.tensor_tensor(sq[:, 0:512], q, q, ALU.mult))
                ch.link(nc.vector.tensor_tensor(sq[:, 512:640], k, k, ALU.mult))
                if t >= 2:
                    dve.wait_ge(s_rope, t - 1)
                ch.link(nc.vector.tensor_reduce(qks[:, t % 2, 0, :], sq.rearrange("p (h c) -> p h c", c=HD), X, ALU.add))
                nc.vector.tensor_scalar(qks[:, t % 2, 0, :], qks[:, t % 2, 0, :], 1.0 / HD, NORM_EPS, ALU.mult,
                                        ALU.add).then_inc(s_var, 1)
                nroot[0] += 1
                dve.wait_ge(s_std, nroot[0])
                nc.vector.reciprocal(qks[:, t % 2, 2, :], qks[:, t % 2, 1, :]).then_inc(s_rr, 1)

            def conv_tile(m):
                dve.wait_ge(s_projo, gidx["xbc", m, 1] + 1)
                ch.link(nc.vector.tensor_scalar(conv[:, m, :], u_pad[:, m, 0:CW], cw[:, m, 0:1],
                                                cw[:, m, TAPS:TAPS + 1], ALU.mult, ALU.add))
                for j in range(1, TAPS):
                    ins = nc.vector.scalar_tensor_tensor(conv[:, m, :], u_pad[:, m, j:j + CW], cw[:, m, j:j + 1],
                                                         conv[:, m, :], ALU.mult, ALU.add)
                    if j == TAPS - 1:
                        ins.then_inc(s_conv, 1)
                    else:
                        ch.link(ins)

            dve.wait_ge(s_param, 16 * 11)
            dve.wait_ge(s_prep, 1)
            def dt_first():
                raw = kvd[:, :, 256:272]
                ch.link(nc.vector.tensor_tensor(d16(DT), raw, hpar[:, 0, :].unsqueeze(1).broadcast_to([P, NT, 16]),
                                                ALU.add))
                nc.vector.scalar_tensor_tensor(dtw[:, W1, :], dtw[:, DT, :], -1.0, dtw[:, DT, :], ALU.mult,
                                               ALU.min).then_inc(s_dt1, 1)
                dve.wait_ge(s_dt2, 1)
                nc.vector.tensor_scalar(dtw[:, W2, :], dtw[:, W1, :], 1.0, None, ALU.add).then_inc(s_dt1, 1)
                dve.wait_ge(s_dt1, 2)

            for m in range(KC):
                if m < NT:
                    qk_rms(m)
                if m == NT:
                    dt_first()
                if m:
                    conv_tile(m - 1)
            ch.link(nc.vector.tensor_scalar(dtw[:, EA, :], dtw[:, W2, :], 1.0, None, ALU.is_equal))
            dve.wait_ge(s_dt2, 2)
            ch.step(nc.vector.tensor_tensor(dtw[:, ACUM, :], dtw[:, ACUM, :], dtw[:, EA, :], ALU.add))
            ch.link(nc.vector.scalar_tensor_tensor(dtw[:, W2, :], dtw[:, W2, :], -1.0, dtw[:, EA, :], ALU.add, ALU.add))
            ch.link(nc.vector.reciprocal(dtw[:, W2, :], dtw[:, W2, :]))
            ch.link(nc.vector.tensor_tensor(dtw[:, W1, :], dtw[:, W1, :], dtw[:, ACUM, :], ALU.mult))
            ch.link(nc.vector.tensor_tensor(dtw[:, W1, :], dtw[:, W1, :], dtw[:, W2, :], ALU.mult))
            ch.link(nc.vector.scalar_tensor_tensor(dtw[:, DT, :], dtw[:, DT, :], 0.0, dtw[:, W1, :], ALU.max, ALU.add))
            nc.vector.scalar_tensor_tensor(d16(ANEG), d16(DT), -1.0,
                                           hpar[:, 1, :].unsqueeze(1).broadcast_to([P, NT, 16]), ALU.mult,
                                           ALU.mult).then_inc(s_a, 1)
            conv_tile(KC - 1)
            dve.wait_ge(s_cum, 1)
            cum = ps[:, 6, 0:NT * 16].rearrange("p (d t h) -> p t d h", d=2, h=NH)
            tot = ps[:, 7, 0:NT * 16]
            a4 = dtw[:, ACUM, :].rearrange("p (t d h) -> p t d h", d=2, h=NH)
            ch.step(nc.vector.tensor_copy(dtw[:, CD, :], tot))
            ch.link(nc.vector.tensor_copy(a4, cum))
            ch.step(nc.vector.tensor_scalar(dtw[:, NACUM, :], dtw[:, ACUM, :], -1.0, None, ALU.mult))
            nc.vector.tensor_tensor(dtw[:, W1, :], dtw[:, CD, :], dtw[:, ACUM, :], ALU.subtract).then_inc(s_cums, 1)
            dve.wait_ge(s_ecum, 1)
            nc.vector.tensor_tensor(dtw[:, WDEC, :], dtw[:, WDEC, :], dtw[:, DT, :], ALU.mult).then_inc(s_cums, 1)

            for n, (d, t, g, i, first) in enumerate(upd):
                dve.wait_ge(s_st, n + 1)
                new = state[:, d, g, i, :]
                prod = ps[:, 6 + n % 2, 0:256]
                if first:
                    nc.vector.tensor_copy(new, prod).then_inc(s_sts, 1)
                else:
                    dve.wait_ge(s_sts, n - 3)
                    o = new.rearrange("p (h c) -> p h c", h=HPG)
                    old = state[:, d, g, i - 1, :].rearrange("p (h c) -> p h c", h=HPG)
                    w = d16(CD)[:, t, d * NH + g * HPG:d * NH + (g + 1) * HPG]
                    ch.link(nc.vector.tensor_tensor(o, old, w.unsqueeze(2).broadcast_to([P, HPG, HD]), ALU.mult))
                    nc.vector.tensor_tensor(new, new, prod, ALU.add).then_inc(s_sts, 1)

            def row_max(u):
                L = seq_of[att_units[u][0]][1] * P
                dve.wait_ge(s_sc, u + 1)
                ch.link(nc.vector.reduce_max(att[:, 2, u:u + 1], ps[:, u % 3, 0:L], X))
                nc.vector.tensor_scalar(att[:, 0, u:u + 1], att[:, 2, u:u + 1], -(HD ** -0.5), None,
                                        ALU.mult).then_inc(s_max, 1)

            def pt_out(u):
                n = seq_of[att_units[u][0]][1]
                dve.wait_ge(s_pt, u + 1)
                if u >= 8:
                    dve.wait_ge(s_pv, u // 4 - 1)
                nc.vector.tensor_copy(probT[u // 4 % 2][:, 0:n, (u % 4) * P:(u % 4 + 1) * P],
                                      ps[:, 3, 0:n * P].rearrange("p (b c) -> p b c", c=P)).then_inc(s_pts, 1)

            def att_out(G):
                t, i = G // NKV, G % NKV
                dve.wait_ge(s_pv, G + 1)
                nc.vector.tensor_copy(mix[i * HD:(i + 1) * HD, t, 0:512],
                                      ps[i * HD:(i + 1) * HD, 4, :]).then_inc(s_ao, 1)

            def weights(n):
                t, g = ssd_units[n]
                dve.wait_ge(s_cb, n + 1)
                if n:
                    dve.wait_ge(s_tfb, n)
                nc.vector.tensor_copy(cbT, ps[:, 7, 0:P]).then_inc(s_cbs, 1)
                dve.wait_ge(s_cbs, n + 1)
                dve.wait_ge(s_edec, 2 * n + 2)
                for d in range(2):
                    for h in range(HPG):
                        c = d * NH + g * HPG + h
                        v = dec[:, d, h]
                        last = nc.vector.scalar_tensor_tensor(v, v, d16(DT)[:, t, c:c + 1], cbT,
                                                              ALU.mult, ALU.mult)
                last.then_inc(s_tfb, 1)
                dve.wait_ge(s_off, n + 1)
                if n:
                    dve.wait_ge(s_t, n)
                for d in range(2):
                    if (d, t) in prev_at:
                        c = d * NH + g * HPG
                        w = d16(EA)[:, t, c:c + HPG].unsqueeze(2).broadcast_to([P, HPG, HD])
                        last = nc.vector.tensor_tensor(
                            offm[:, d, :].rearrange("p (h c) -> p h c", h=HPG),
                            ps[:, 5, d * 256:(d + 1) * 256].rearrange("p (h c) -> p h c", h=HPG), w, ALU.mult)
                last.then_inc(s_offm, 1)

            def y_out(n):
                dve.wait_ge(s_y, n + 1)
                dve.wait_ge(s_t, n + 1)
                if n:
                    dve.wait_ge(s_yz, n)
                nc.vector.tensor_tensor(ysum, yadd, ps[:, 7, 0:256], ALU.add).then_inc(s_yo, 1)

            def group_var(a, b):
                dve.wait_ge(s_gs, b)
                nc.vector.tensor_scalar(gss[:, 1, a:b], gss[:, 0, a:b], 1.0 / 256, NORM_EPS, ALU.mult,
                                        ALU.add).then_inc(s_var, 1)

            def group_scale(a, b):
                nroot[0] += 1
                dve.wait_ge(s_std, nroot[0])
                ch.link(nc.vector.reciprocal(gss[:, 2, a:b], gss[:, 1, a:b]))

            def group_norm(n):
                t, g = ssd_units[n]
                y = mix[:, t, 512 + g * 256:512 + (g + 1) * 256]
                nc.vector.scalar_tensor_tensor(y, y, gss[:, 2, n:n + 1], ssdw[:, g * 256:(g + 1) * 256],
                                               ALU.mult, ALU.mult).then_inc(s_ssd, 1)

            for i in range(NU + 5):
                if i < NU:
                    row_max(i)
                if 1 <= i <= NU:
                    u = i - 1
                    dve.wait_ge(s_exp, u + 1)
                    nc.vector.reciprocal(att[:, 2, u:u + 1], att[:, 1, u:u + 1]).then_inc(s_rc, 1)
                if 3 <= i < NU + 3:
                    pt_out(i - 3)
                if i % 4 == 0 and i >= 8:
                    att_out(i // 4 - 2)
                if i % 4 == 0 and 4 <= i <= NU:
                    y_out(i // 4 - 1)
                if i % 4 == 2 and i < NU:
                    weights(i // 4)
                if i == 4 * EARLY + 5:
                    group_var(0, EARLY)
                if i == 4 * EARLY + 7:
                    group_scale(0, EARLY)
                if 4 * EARLY + 7 < i <= 5 * EARLY + 7:
                    group_norm(i - 4 * EARLY - 8)
            group_var(EARLY, NG)
            group_scale(EARLY, NG)
            for n in range(EARLY, NG):
                group_norm(n)

            for t in range(NT):
                dve.wait_ge(s_o, t + 1)
                b = 4 + 2 * (t % 2)
                nc.vector.scalar_tensor_tensor(xa[:, t, :], xa[:, t, :], ALPHA,
                                               ps[:, b:b + 2, :].rearrange("p b c -> p (b c)"),
                                               ALU.mult, ALU.add).then_inc(s_res, 1)
                dve.wait_ge(s_res, t + 1)
                ln_stats(t, xa[:, t, :], LN_EPS)
                ln_apply(t, xa[:, t, :], xa[:, t, :], gB, bB, s_x1)
            def base(u):
                h, t = ple_units[u]
                dve.wait_ge(s_sig, u + 1)
                b = sig[:, u % 4, :]
                ch.link(nc.vector.tensor_tensor(b, b, ps[:, 2 * (u % 2) + 1, :], ALU.mult))
                nc.vector.scalar_tensor_tensor(b, xa[:, t, h * 512:(h + 1) * 512], ALPHA, b, ALU.mult,
                                               ALU.add).then_inc(s_base, 1)

            base(0)
            dve.wait_ge(s_lg, 1)
            lg = ps[:, 4, 0:NT * NE].rearrange("p (t e) -> p t e", e=NE)
            r0 = rt[:, 0, :].rearrange("p (t e) -> p t e", e=NE)
            ch.link(nc.vector.reduce_max(rs6[:, 0, :], lg, X))
            nc.vector.tensor_tensor(r0, lg, rs6[:, 0, :].unsqueeze(2).broadcast_to([P, NT, NE]),
                                    ALU.subtract).then_inc(s_lgd, 1)
            dve.wait_ge(s_lge, 1)
            ch.link(nc.vector.reduce_sum(rs6[:, 1, :], r0, X))
            ch.link(nc.vector.reciprocal(rs6[:, 2, :], rs6[:, 1, :]))
            nc.vector.tensor_tensor(r0, r0, rs6[:, 2, :].unsqueeze(2).broadcast_to([P, NT, NE]),
                                    ALU.mult).then_inc(s_lgd, 1)
            base(1)
            dve.wait_ge(s_affT, 1)
            ch.link(nc.vector.tensor_copy(affw[:, 0, :], ps[0:NE, 6:8, :].rearrange("p b c -> p (b c)")[:, 0:T]))
            rounds = 0
            for (a, n), c0, cap in ((SEQS[0], 0, CAPP), (SEQS[1], CAPP, CAPS)):
                lo, hi = a * P, (a + n) * P
                for k in range(cap // 8):
                    v = topv[:, c0 + 8 * k:c0 + 8 * k + 8]
                    cur, nxt = affw[:, k % 2, lo:hi], affw[:, (k + 1) % 2, lo:hi]
                    ch.link(nc.vector.max(v, cur))
                    ch.step(nc.vector.max_index(topi[:, c0 + 8 * k:c0 + 8 * k + 8], v, cur))
                    ch.link(nc.vector.match_replace(nxt, v, cur, -1.0))
                    rounds += 1
                    if rounds % 4 == 0:
                        base(1 + rounds // 4)
            ch.step(nc.vector.tensor_copy(topf[:, 0:CAPP], topi[:, 0:CAPP]))
            ch.link(nc.vector.tensor_copy(topf[:, CAPP:CAP], topi[:, CAPP:CAP]))
            nc.vector.tensor_scalar(topf[:, CAPP:CAP], topf[:, CAPP:CAP], float(TP * P), None, ALU.add).then_inc(s_top, 1)
            base(5)
            base(6)
            dve.wait_ge(s_topT, 1)
            nc.vector.tensor_copy(idxT[:], ps[0:CAP, 5, 0:NE]).then_inc(s_idx, 1)
            nc.vector.tensor_copy(gateT[:], ps[0:CAP, 5, NE:2 * NE]).then_inc(s_idx, 1)
            for u in range(7, 2 * NT):
                base(u)

            def xeT_out(e):
                dve.wait_ge(s_xeT_p, e + 1)
                for half in range(2):
                    last = nc.vector.tensor_copy(xeT[:, 4 * half:4 * half + 4, :],
                                                 ps[:, 6 + half, 0:4 * CAP].rearrange("p (k c) -> p k c", k=4))
                last.then_inc(s_xeT, 1)

            def hid_half(e, h):
                dve.wait_ge(s_hs, 2 * e + h + 1)
                v = hid[:, h * 512:(h + 1) * 512]
                nc.vector.tensor_tensor(v, v, ps[0:CAP, 2 * h + 1, :], ALU.mult).then_inc(s_hid, 1)

            def ye_out(e, gate, first=False):
                if not first:
                    dve.wait_ge(s_scat, 16 * e)
                for h in range(2):
                    dve.wait_ge(s_dn, 2 * e + h + 1)
                    last = nc.vector.tensor_scalar(ye[:, h * 512:(h + 1) * 512], ps[0:CAP, 4 + h, :], gate, None,
                                                   ALU.mult)
                last.then_inc(s_ye, 1)

            dve.wait_ge(s_rowst, 16 * NT)
            dve.wait_ge(s_base, 2 * NT)
            xeT_out(0)
            hid_half(0, 0)
            hid_half(0, 1)
            xeT_out(1)
            hid_half(1, 0)
            hid_half(1, 1)
            xeT_out(2)
            ye_out(0, gateT[:, 0:1], True)
            with dve.Fori(2, NE - 1) as e:
                hid_half(e, 0)
                hid_half(e, 1)
                xeT_out(e + 1)
                ye_out(e - 1, gateT[:, bass.ds(e - 1, 1)])
            hid_half(NE - 1, 0)
            hid_half(NE - 1, 1)
            ye_out(NE - 2, gateT[:, NE - 2:NE - 1])
            ye_out(NE - 1, gateT[:, NE - 1:NE])

            dve.wait_ge(s_ln2, 32)
            for t in range(NT):
                dve.wait_ge(s_fin[t], 16)
                ln_stats(t, fin[:, t, :], LN_EPS)
                ln_apply(t, fin[:, t, :], fin[:, t, :], gA, bA, s_y2)

        @block.tensor
        def _(pe):
            tr = [0]

            def unit(pairs, waits=()):
                n = tr[0]
                if n >= 2 and n < len(tr_units):
                    pe.wait_ge(*tr_units[n - 2])
                b = 2 * (n % 2)
                for half, lst in enumerate(pairs):
                    for col, src in lst:
                        k = src.shape[0]
                        w = 1
                        for s in src.shape[1:]:
                            w *= s
                        last = nc.tensor.transpose(ps[0:w, b + half, col:col + k], src, ident[0:k, 0:k])
                last.then_inc(s_tr, 1)
                tr[0] += 1

            def eight(src):
                return [[(j * P, src[:, (4 * half + j) * P:(4 * half + j + 1) * P]) for j in range(4)]
                        for half in range(2)]

            ng = [0]

            def group(g):
                n = ng[0]
                if n >= 4:
                    pe.wait_ge(s_projo, n - 1 if g[0] == "z" else n - 3)
                kind = g[0]
                bank = ps[:, 4 + (n % 2 if kind == "z" else n % 4), :]
                if kind == "xbc":
                    m, s = g[1], g[2]
                    a, w = SEQS[s]
                    wsl = slotk[2] if m < 4 else slotk[0]
                    for k in range(KD):
                        last = nc.tensor.matmul(bank[:, 0:w * P], wsl[:, k, (m % 4) * P:(m % 4 + 1) * P],
                                                xT[:, k, a * P:(a + w) * P], start=(k == 0), stop=(k == KD - 1))
                else:
                    t = g[1]
                    lhs = [xT[:, k, t * P:(t + 1) * P] for k in range(KD)]
                    if kind == "kv":
                        wkv = slot[1][:, 0:KD * 256].rearrange("p (k c) -> p k c", k=KD)
                        wdt = slot[1][:, KD * 256:KD * 272].rearrange("p (k c) -> p k c", k=KD)
                        for k in range(KD):
                            nc.tensor.matmul(bank[:, 0:256], lhs[k], wkv[:, k, :], start=(k == 0), stop=(k == KD - 1))
                        for k in range(KD):
                            last = nc.tensor.matmul(bank[:, 256:272], lhs[k], wdt[:, k, :], start=(k == 0),
                                                    stop=(k == KD - 1))
                    else:
                        w = slotk[0] if kind == "q" else slotk[1]
                        for k in range(KD):
                            last = nc.tensor.matmul(bank, lhs[k], w[:, k, :], start=(k == 0), stop=(k == KD - 1))
                last.then_inc(s_proj, 1)
                ng[0] += 1

            pe.wait_ge(s_const, 16 * 3)
            pe.wait_ge(s_xa, 1)
            unit(eight(xa[:, 0, :]))
            for t in range(NT):
                if t + 1 < NT:
                    pe.wait_ge(s_xa, t + 2)
                    unit(eight(xa[:, t + 1, :]))
                pe.wait_ge(s_xT, t + 1)
                if t == 0:
                    pe.wait_ge(s_slot[0], 16)
                group(("q", t))
                if t == 0:
                    pe.wait_ge(s_slot[1], 32)
                group(("kv", t))
            pe.wait_ge(s_param, 16 * 11)
            unit([[(m * (TAPS + 1), cw_rows[:, m * P:(m + 1) * P]) for m in range(KC)]])
            pe.wait_ge(s_slot[2], 16)
            for g in xbc_groups:
                if g == ("xbc", 4, 0):
                    pe.wait_ge(s_slot[0], 32)
                group(g)
            an = d16(ANEG)

            def cumulate():
                pe.wait_ge(s_a, 1)
                pe.wait_ge(s_projo, gidx["z", 0])
                pe.wait_ge(s_tab, 16)
                nc.tensor.matmul(ps[:, 6, 0:NT * NH], upto, an[:, :, 0:NH], start=True, stop=True)
                nc.tensor.matmul(ps[:, 6, NT * NH:2 * NT * NH], onward, an[:, :, NH:16], start=True, stop=True)
                pe.wait_ge(s_prep, 1)
                nc.tensor.matmul(ps[:, 7, 0:NT * 16], ones[:], dtw[:, ANEG, :], start=True,
                                 stop=True).then_inc(s_cum, 1)

            def x_token_major(t):
                c = conv_col(t)
                pe.wait_ge(s_silu, KC)
                unit([[(m * P, conv[:, m, c:c + P]) for m in range(4)],
                      [(m * P, conv[:, 4 + m, c:c + P]) for m in range(2)]])

            def chunk_state(n):
                d, t, g, i, first = upd[n]
                pe.wait_ge(s_ws, n + 1)
                pe.wait_ge(s_xB, NT)
                if n >= 2:
                    pe.wait_ge(s_sts, n - 1)
                else:
                    pe.wait_ge(s_cums, 1)
                nc.tensor.matmul(ps[:, 6 + n % 2, 0:256], btok[:, t, g * P:(g + 1) * P], xsc[:, n % 2, :],
                                 start=True, stop=True).then_inc(s_st, 1)

            pe.wait_ge(s_slot[1], 48)
            for t, g in enumerate(z_groups):
                group(g)
                if t == 0:
                    cumulate()
                elif t <= 3:
                    x_token_major(2 * t - 2)
                    x_token_major(2 * t - 1)
                else:
                    for n in range(len(upd) // 2):
                        chunk_state((t - 4) * len(upd) // 2 + n)
            for t in range(NT):
                pe.wait_ge(s_rope, t + 1)
                unit([[(j * P, mix[:, t, j * P:(j + 1) * P]) for j in range(4)], [(0, kvd[:, t, 0:P])]])

            def scores(u):
                t, h = att_units[u]
                a, n = seq_of[t]
                if u >= 3:
                    pe.wait_ge(s_exp, u - 2)
                nc.tensor.matmul(ps[:, u % 3, 0:n * P], qT[:, h % 4, t * P:(t + 1) * P],
                                 kz[:, h // 4, a * P:(a + n) * P], start=True, stop=True).then_inc(s_sc, 1)

            def turn(u):
                n = seq_of[att_units[u][0]][1]
                pe.wait_ge(s_pn, u + 1)
                if u:
                    pe.wait_ge(s_pts, u)
                for b in range(n):
                    last = nc.tensor.transpose(ps[:, 3, b * P:(b + 1) * P], prob[:, u % 4, b * P:(b + 1) * P], ident)
                last.then_inc(s_pt, 1)

            def pv(G):
                a, n = seq_of[G // NKV]
                pe.wait_ge(s_pts, 4 * G + 4)
                if G:
                    pe.wait_ge(s_ao, G)
                for b in range(n):
                    last = nc.tensor.matmul(ps[:, 4, :], kvd[:, a + b, P:2 * P], probT[G % 2][:, b, :],
                                            start=(b == 0), stop=(b == n - 1))
                last.then_inc(s_pv, 1)

            def decay(n):
                t, g = ssd_units[n]
                if n:
                    pe.wait_ge(s_offm, n)
                    pe.wait_ge(s_edec, 2 * n)
                for d, tri in ((0, upto), (1, onward)):
                    bank = ps[:, 5 + d, :]
                    for h in range(HPG):
                        c = d * NH + g * HPG + h
                        nc.tensor.matmul(bank[:, h * P:(h + 1) * P], identb[:], maskb[:, d, :],
                                         start=True, stop=False)
                        last = nc.tensor.matmul(bank[:, h * P:(h + 1) * P],
                                                an[:, t, c:c + 1].broadcast_to([P, P]), tri,
                                                start=False, stop=True)
                last.then_inc(s_dec, 1)

            def products(n):
                t, g = ssd_units[n]
                cc = conv_col(t)
                if n:
                    pe.wait_ge(s_yo, n)
                nc.tensor.matmul(ps[:, 7, 0:P], conv[:, 4 + g, cc:cc + P],
                                 conv[:, 6 + g, cc:cc + P], start=True, stop=True).then_inc(s_cb, 1)
                pe.wait_ge(s_edec, 2 * n + 2)
                for d in range(2):
                    if (d, t) in prev_at:
                        last = nc.tensor.matmul(ps[:, 5, d * 256:(d + 1) * 256], conv[:, 6 + g, cc:cc + P],
                                                state[:, d, g, prev_at[d, t], :], start=True, stop=True)
                last.then_inc(s_off, 1)

            def y(n):
                t, g = ssd_units[n]
                pe.wait_ge(s_m, n + 1)
                for h in range(HPG):
                    last = nc.tensor.matmul(ps[:, 7, h * HD:(h + 1) * HD], msum[:, h],
                                            xtok[:, t, (g * HPG + h) * HD:(g * HPG + h + 1) * HD],
                                            start=True, stop=True)
                last.then_inc(s_y, 1)

            pe.wait_ge(s_qkT, NT)
            pe.wait_ge(s_projo, len(groups))
            pe.wait_ge(s_sts, len(upd))
            for i in range(NU + 4):
                if i < NU:
                    scores(i)
                if i % 4 == 0:
                    if i:
                        if i <= NU:
                            y(i // 4 - 1)
                    if i < NU:
                        decay(i // 4)
                if i % 4 == 2 and i < NU:
                    products(i // 4)
                if 3 <= i < NU + 3:
                    turn(i - 3)
                if i >= 7 and i % 4 == 3:
                    pv((i - 7) // 4)

            assert tr[0] == 3 * NT + 1

            def mix_turn(t):
                pe.wait_ge(s_ssd, 2 * t + 2)
                if t >= 4:
                    pe.wait_ge(s_mixT, t - 3)
                for j in range(4):
                    last = nc.tensor.transpose(ps[:, t % 4, j * P:(j + 1) * P],
                                               mix[:, t, 512 + j * P:512 + (j + 1) * P], ident)
                last.then_inc(s_tr, 1)

            def out_proj(t, h):
                w, j, n = ((slotk[2], 2, 64), (slotk[0], 0, 80))[h]
                if t == 0:
                    pe.wait_ge(s_slot[j], n)
                if t >= 2 and h == 0:
                    pe.wait_ge(s_res, t - 1)
                for k in range(KD):
                    if k == 4:
                        pe.wait_ge(s_mixT, t + 1)
                    lhs = mix[:, t, k * P:(k + 1) * P] if k < 4 else xT[:, k, t * P:(t + 1) * P]
                    last = nc.tensor.matmul(ps[:, 4 + 2 * (t % 2) + h, :], lhs, w[:, k, :],
                                            start=(k == 0), stop=(k == KD - 1))
                if h == 1:
                    last.then_inc(s_o, 1)

            def x1_turn(t):
                pe.wait_ge(s_x1, t + 1)
                if t < 2:
                    pe.wait_ge(s_pT, 1)
                else:
                    pe.wait_ge(s_x1T, t - 1)
                b = 2 * (t % 2)
                for j in range(KD):
                    last = nc.tensor.transpose(ps[:, b + j // 4, (j % 4) * P:(j % 4 + 1) * P],
                                               xa[:, t, j * P:(j + 1) * P], ident)
                last.then_inc(s_tr, 1)

            def ple_unit(u):
                h, t = ple_units[u]
                if u == 0:
                    pe.wait_ge(s_x1T, NT - 1)
                    pe.wait_ge(s_slot[1], 64)
                    pe.wait_ge(s_bple, 32)
                    pe.wait_ge(s_wple, 16)
                if u >= 2:
                    pe.wait_ge(s_base, u - 1)
                if u == NT:
                    pe.wait_ge(s_slot[2], 80)
                w = slotk[1] if h == 0 else slotk[2]
                b = 2 * (u % 2)
                nc.tensor.matmul(ps[:, b, :], ones[0:1, :], bple[h], start=True, stop=False)
                for k in range(KD):
                    nc.tensor.matmul(ps[:, b, :], xT[:, k, t * P:(t + 1) * P], w[:, k, :],
                                     start=False, stop=(k == KD - 1))
                for k in range(2):
                    last = nc.tensor.matmul(ps[:, b + 1, :], pT[:, k, t * P:(t + 1) * P],
                                            wple[:, k, h * 512:(h + 1) * 512], start=(k == 0), stop=(k == 1))
                last.then_inc(s_pg, 1)

            pe.wait_ge(s_pts, NU)
            for t in range(4):
                mix_turn(t)
            pe.wait_ge(s_ao, NG)
            pe.wait_ge(s_yo, NG)
            out_proj(0, 0)
            out_proj(1, 0)
            mix_turn(4)
            mix_turn(5)
            out_proj(0, 1)
            out_proj(1, 1)
            pe.wait_ge(s_ple_in, 32)
            pe.wait_ge(s_mixT, NT)
            for b in range(3):
                for k in range(2):
                    for i in range(2):
                        last = nc.tensor.transpose(ps[:, b, k * 256 + i * P:k * 256 + (i + 1) * P],
                                                   ptok[:, 2 * b + i, k * P:(k + 1) * P], ident)
            last.then_inc(s_tr, 1)
            x1_turn(0)
            for t in range(2, NT):
                out_proj(t, 0)
                out_proj(t, 1)
                x1_turn(t - 1)
            ple_unit(0)
            x1_turn(NT - 1)
            pe.wait_ge(s_x1T, NT)
            for t in range(NT):
                for k in range(KD):
                    last = nc.tensor.matmul(ps[:, 4, t * NE:(t + 1) * NE], xT[:, k, t * P:(t + 1) * P],
                                            wr[:, k, :], start=(k == 0), stop=(k == KD - 1))
            last.then_inc(s_lg, 1)
            ple_unit(1)
            pe.wait_ge(s_lgd, 2)
            for t in range(NT):
                last = nc.tensor.transpose(ps[0:NE, 6 + t // 4, (t % 4) * P:(t % 4 + 1) * P],
                                           rt[:, 0, t * NE:(t + 1) * NE], ident)
            last.then_inc(s_affT, 1)
            for u in range(2, 6):
                ple_unit(u)
            pe.wait_ge(s_top, 1)
            nc.tensor.transpose(ps[0:CAP, 5, 0:NE], topf[:], ident[0:NE, 0:NE])
            nc.tensor.transpose(ps[0:CAP, 5, NE:2 * NE], topv[:], ident[0:NE, 0:NE]).then_inc(s_topT, 1)
            for u in range(6, 2 * NT):
                ple_unit(u)

            def turn8(src, done):
                for j in range(KD):
                    last = nc.tensor.transpose(ps[:, 6 + j // 4, (j % 4) * CAP:(j % 4 + 1) * CAP],
                                               src[:, j * P:(j + 1) * P], ident[0:CAP, 0:CAP])
                last.then_inc(done, 1)

            def rows_turn(e, hT=True):
                pe.wait_ge(s_gath, 16 * (e + 1))
                if hT:
                    pe.wait_ge(s_hT, e - 1)
                turn8(xe, s_xeT_p)

            def gate_up(e, h, first=False):
                if h == 0:
                    pe.wait_ge(s_xeT, e + 1)
                if not first:
                    pe.wait_ge(s_hid, 2 * e - 1 + h)
                for i, j in ((0, (3, 5)[h]), (1, (4, 0)[h])):
                    pe.wait_ge(s_slot[j], 16 * (e + 1) + (80 if j == 0 else 0))
                    for k in range(KD):
                        last = nc.tensor.matmul(ps[0:CAP, 2 * h + i, :], xeT[:, k, :], slotk[j][:, k, :],
                                                start=(k == 0), stop=(k == KD - 1))
                last.then_inc(s_gu, 1)

            def hid_turn(e, nxt=True):
                pe.wait_ge(s_hid, 2 * e + 2)
                if nxt:
                    pe.wait_ge(s_xeT, e + 2)
                turn8(hid, s_hT_p)

            def down(e, first=False):
                pe.wait_ge(s_hT, e + 1)
                if not first:
                    pe.wait_ge(s_ye, e)
                for h, j in ((0, 1), (1, 2)):
                    pe.wait_ge(s_slot[j], 16 * (e + 1) + (64 if j == 1 else 80))
                    for k in range(KD):
                        last = nc.tensor.matmul(ps[0:CAP, 4 + h, :], hidT[:, k, :], slotk[j][:, k, :],
                                                start=(k == 0), stop=(k == KD - 1))
                    last.then_inc(s_dn, 1)

            pe.wait_ge(s_base, 2 * NT)
            pe.wait_ge(s_idx, 2)
            rows_turn(0, hT=False)
            gate_up(0, 0, first=True)
            gate_up(0, 1, first=True)
            rows_turn(1, hT=False)
            gate_up(1, 0)
            hid_turn(0)
            gate_up(1, 1)
            rows_turn(2)
            down(0, first=True)
            with pe.Fori(2, NE - 1) as e:
                gate_up(e, 0)
                hid_turn(e - 1)
                gate_up(e, 1)
                rows_turn(e + 1)
                down(e - 1)
            gate_up(NE - 1, 0)
            hid_turn(NE - 2)
            gate_up(NE - 1, 1)
            down(NE - 2)
            hid_turn(NE - 1, nxt=False)
            down(NE - 1)


NAMES = ["x_prompt", "x_sample", "p_prompt", "p_sample", "ln_in_g", "ln_in_b", "w_in", "q_norm_w",
         "k_norm_w", "conv_w", "conv_b", "dt_bias", "a_log", "d_skip", "ssd_norm_w", "w_out", "ln1_g",
         "ln1_b", "w_router", "w_e_gate", "w_e_up", "w_e_down", "w_ple_gate", "b_ple_gate", "w_ple",
         "ln2_g", "ln2_b"]


def kernel(**inputs):
    import concourse.bacc as bacc
    from concourse.bass_utils import run_bass_kernel_spmd

    nc = bacc.Bacc("TRN2", target_bir_lowering=False, num_devices=1)
    arrays, A = {}, {}
    for name in NAMES:
        a = np.ascontiguousarray(inputs[name])
        arrays[f"in_{name}"] = a
        A[name] = nc.dram_tensor(f"in_{name}", a.shape, mybir.dt.from_np(a.dtype), kind="ExternalInput").ap()
    lengths = (inputs["x_prompt"].shape[1], inputs["x_sample"].shape[1])
    c = shape_constants(lengths)
    arrays["shape_constants"] = c
    consts = nc.dram_tensor("shape_constants", c.shape, F32, kind="ExternalInput").ap()
    outs = [nc.dram_tensor(f"out_{i}", (1, n, D), F32, kind="ExternalOutput").ap()
            for i, n in enumerate(lengths)]
    hymba_layer(nc, A, consts, *outs)
    r = run_bass_kernel_spmd(nc, [arrays], core_ids=[0])
    return tuple(r.results[0][f"out_{i}"] for i in range(2))
```

```python
from contextlib import ExitStack

import numpy as np

import concourse.bass as bass
from concourse import mybir

ALU = mybir.AluOpType
ACT = mybir.ActivationFunctionType
F32 = mybir.dt.float32
F32R = mybir.dt.float32r
U32 = mybir.dt.uint32
I32 = mybir.dt.int32
X = mybir.AxisListType.X

P = 128
D = 1024
KD = D // P
HD = 64
NQ, NKV = 8, 2
NH = 8
GROUPS, HPG = 2, 4
NSTATE = 128
TAPS = 5
CONV = 1024
KC = CONV // P
NE = 16
PLE = 256
GRID_W = 64
THETA = 10000.0
NORM_EPS, LN_EPS = 1e-6, 1e-5
ALPHA = 2.0 ** 0.25
K0, V0, Z0, XBC0, DT0, IN_COLS = 512, 640, 768, 1280, 2304, 2320
NB = 6


def shape_constants(lengths):
    i = np.arange(P)
    ident = np.eye(P)
    upto = (i[:, None] <= i[None, :]) * 1.0
    onward = (i[:, None] >= i[None, :]) * 1.0
    inv = THETA ** (-np.arange(HD // 4) / (HD // 4))
    cs = []
    for n in lengths:
        pos = np.stack([np.arange(n) // GRID_W, np.arange(n) % GRID_W], -1)
        ang = (pos[:, :, None] * inv).reshape(n // P, P, HD // 2)
        cs.append(np.stack([np.cos(ang), np.sin(ang)], 2))
    cs = np.concatenate(cs).transpose(1, 0, 2, 3).reshape(P, -1)
    return np.concatenate([ident, upto, onward, cs], 1).astype(np.float32)


def hymba_layer(nc, A, consts, out_prompt, out_sample):
    TP = A["x_prompt"].shape[1] // P
    TS = A["x_sample"].shape[1] // P
    NT = TP + TS
    T = NT * P
    SEQS = [(0, TP), (TP, TS)]
    CAPP, CAPS = TP * P * 2 // NE, TS * P * 2 // NE
    CAP = CAPP + CAPS
    PADW = TP * P + TS * P + 6
    CW = PADW - 4

    def conv_col(t):
        return t * P if t < TP else t * P + 2

    ctx = ExitStack()
    with ctx:
        def sb(name, shape, dt=F32):
            return ctx.enter_context(nc.sbuf_tensor(name, shape, dt))

        def sem(name):
            return ctx.enter_context(nc.semaphore(name))

        at = {}

        def sb_at(name, shape):
            t = sb(name, shape)
            at[name] = nc.sbuf_base - 4 * int(np.prod(shape[1:]))
            return t

        def over(name, base, skip, shape):
            return nc.alloc_sbuf_tensor_at(name, shape, F32R, offset=at[base] + 4 * skip).ap()

        ring = sb_at("ring", [P, 3, KD * 512])
        late = sb_at("late", [P, KC * (PADW + CW)])
        xa = sb_at("xa", [P, NT, D])
        xT = sb_at("xT", [P, KD, T])
        mix = sb_at("mix", [P, NT, D])
        kvd = sb("kvd", [P, NT, 272])
        cst = sb("cst", [P, 3 * P + NT * 64])
        gb_in = sb_at("gb_in", [P, 2, D])
        gB, bB = sb("gB", [P, D]), sb("bB", [P, D])
        ssdw = sb("ssdw", [P, 512])
        qkw = sb("qkw", [P, 2, HD])
        hpar = sb("hpar", [P, 3, 16])
        ones = sb("ones", [P, P])
        wr = sb("wr", [P, KD, NE])
        cw = sb("cw", [P, KC, TAPS + 1])
        stats = sb("stats", [P, 2, 12])
        mv = sb("mv", [P, NT, 2])
        sd = sb("sd", [P, 2, NT])
        qks = sb("qks", [P, 2, 3, 10])
        dtw = sb("dtw", [P, 8, NT * 16])
        att = sb("att", [P, 3, NT * NQ])
        gss = sb("gss", [P, 3, NT * GROUPS])
        rt = sb("rt", [P, 1, NT * NE])
        rs6 = sb("rs6", [P, 3, NT])
        topv = sb("topv", [NE, CAP])
        topi = sb("topi", [NE, CAP], U32)
        gateT = sb("gateT", [CAP, NE])
        idxT = sb("idxT", [CAP, NE], I32)
        idx_now = sb("idx_now", [CAP, 2], I32)
        qksq = sb("qksq", [P, 640])
        ps = ctx.enter_context(nc.psum_tensor("ps", [P, 8, 512], F32))

        x1_rows = nc.dram_tensor("x1_rows", (T, D), F32, kind="Internal").ap()
        acc_rows = nc.dram_tensor("acc_rows", (T, D), F32, kind="Internal").ap()

        ident = cst[:, 0:P]
        topf = cst[0:NE, P:P + CAP]
        upto, onward = cst[:, P:2 * P], cst[:, 2 * P:3 * P]
        tri = cst[:, P:3 * P].rearrange("p (d l) -> p d l", d=2)
        rope = cst[:, 3 * P:].rearrange("p (t c a f) -> p t c a f", t=NT, c=2, a=2)
        u_pad = late[:, 0:KC * PADW].rearrange("p (m c) -> p m c", m=KC)
        conv = late[:, KC * PADW:].rearrange("p (m c) -> p m c", m=KC)
        cw_rows = late[0:TAPS + 1, KC * PADW + 6 * CW:KC * PADW + 6 * CW + CONV]
        xtok = late[:, 0:NT * 512].rearrange("p (t c) -> p t c", t=NT)
        btok = late[:, NT * 512:NT * 768].rearrange("p (t c) -> p t c", t=NT)
        slot = [ring[:, j, :] for j in range(3)] + [late[:, j * 4096:(j + 1) * 4096] for j in range(3)]
        slotk = [s.rearrange("p (k c) -> p k c", k=KD) for s in slot]
        wkv = slot[1][:, 0:KD * 272].rearrange("p (k c) -> p k c", k=KD)
        gA, bA = gb_in[:, 0, :], gb_in[:, 1, :]
        qT = xT[:, 0:4, :]
        kz = xT[:, 4:6, :]
        s0, s1 = ring[:, 0, :], ring[:, 1, :]
        NPREV = sum(n - 1 for _, n in SEQS)
        state = s0[:, 0:4 * NPREV * 256].rearrange("p (d g n c) -> p d g n c", d=2, g=2, n=NPREV)
        prob = s1[:, 0:2048].rearrange("p (b c) -> p b c", b=4)
        dec = s1[:, 2048:3072].rearrange("p (d h l) -> p d h l", d=2, h=HPG)
        msum = s1[:, 3072:3584].rearrange("p (h l) -> p h l", h=HPG)
        offm = s1[:, 3584:4096].rearrange("p (d c) -> p d c", d=2)
        xrows = late[:, KC * PADW:KC * PADW + 4 * CW]
        tri_r = over("tri_r", "late", NT * 768, [P, 2, P])
        a_r = [over(f"a_r{i}", "late", NT * 768 + 2 * P + i * NT * 16, [P, NT, 16]) for i in range(2)]
        probT = [xrows[:, 0:2048].rearrange("p (b c) -> p b c", b=4),
                 gb_in[:, :, :].rearrange("p a c -> p (a c)").rearrange("p (b c) -> p b c", b=4)]
        cbT = xrows[:, 2048:2304].rearrange("p (d l) -> p d l", d=2)
        yadd = xrows[:, 2304:2560]
        ysum = xrows[:, 2560:2816]
        ysq = xrows[:, 2816:3072]
        xsc = qksq[:, 0:512].rearrange("p (d c) -> p d c", d=2)
        rot = gb_in[:, 0, 0:512].rearrange("p (b c) -> p b c", b=2)
        mixf = mix[:, :, :].rearrange("p t c -> p (t c)")
        sig = mixf[:, 4 * D:5 * D].rearrange("p (b c) -> p b c", b=2)
        logitsT = gB[0:NE, 0:T]
        affw = [gB[0:NE, 0:T], bB[0:NE, 0:T]]
        xe = mixf[0:CAP, 5 * D:6 * D]
        kvf = kvd[:, :, :].rearrange("p t c -> p (t c)")
        ptok = kvf[:, 0:NT * PLE].rearrange("p (t c) -> p t c", t=NT)
        pT = kvf[:, 0:NT * PLE].rearrange("p (k c) -> p k c", k=2)
        wple = gb_in
        bple = [qksq[0:1, 0:512], dtw[0:1, 0:6, :].rearrange("p r c -> p (r c)")[:, 0:512]]
        xaf = xa[:, :, :].rearrange("p t c -> p (t c)")
        xeT = [over(f"xeT{i}", "xa", i * KD * CAP, [P, KD, CAP]) for i in range(2)]
        hidT = [over(f"hidT{i}", "xa", (2 + i) * KD * CAP, [P, KD, CAP]) for i in range(2)]
        hid = xaf[0:CAP, 4 * KD * CAP:4 * KD * CAP + D]
        ye = xaf[0:CAP, 4 * KD * CAP + D:4 * KD * CAP + 2 * D]
        CH = 2 * D
        raw = [late[:, j * CH:(j + 1) * CH] for j in range(NB)]
        where = [("ring", 4), ("ring", 8), ("xT", 0), ("xT", 4), ("ring", 0), ("mix", 0)]
        high = [over(f"high{j}", b, o * D, [P, CH]) for j, (b, o) in enumerate(where)]
        where[3] = ("gb_in", -2)
        low = [over(f"low{j}", b, (o + 2) * D, [P, CH]) for j, (b, o) in enumerate(where)]
        fin = xT[:, :, :].rearrange("p k c -> p (k c)").rearrange("p (t c) -> p t c", t=NT)

        s_const = sem("s_const")
        s_tab = sem("s_tab")
        s_param = sem("s_param")
        s_xin = [sem(f"s_xin{t}") for t in range(NT)]
        s_slot = [sem(f"s_slot{j}") for j in range(6)]
        s_ple_in = sem("s_ple_in")
        s_dve = sem("s_dve")
        s_act = sem("s_act")
        s_pool = sem("s_pool")
        s_prep = sem("s_prep")
        s_var = sem("s_var")
        s_std = sem("s_std")
        s_xa = sem("s_xa")
        s_tr = sem("s_tr")
        s_xT = sem("s_xT")
        s_cw = sem("s_cw")
        s_proj = sem("s_proj")
        s_projo = sem("s_projo")
        s_rr = sem("s_rr")
        s_rope = sem("s_rope")
        s_kz = sem("s_kz")
        s_conv = sem("s_conv")
        s_silu = sem("s_silu")
        s_qkT = sem("s_qkT")
        s_xB = sem("s_xB")
        s_dt1 = sem("s_dt1")
        s_dt2 = sem("s_dt2")
        s_a = sem("s_a")
        s_ar = sem("s_ar")
        s_cum = sem("s_cum")
        s_cums = sem("s_cums")
        s_ecum = sem("s_ecum")
        s_sc = sem("s_sc")
        s_max = sem("s_max")
        s_exp = sem("s_exp")
        s_rc = sem("s_rc")
        s_pn = sem("s_pn")
        s_pna = sem("s_pna")
        s_pt = sem("s_pt")
        s_pts = sem("s_pts")
        s_pv = sem("s_pv")
        s_ao = sem("s_ao")
        s_ws = sem("s_ws")
        s_st = sem("s_st")
        s_sts = sem("s_sts")
        s_dec = sem("s_dec")
        s_edec = sem("s_edec")
        s_off = sem("s_off")
        s_offm = sem("s_offm")
        s_t = sem("s_t")
        s_cb = sem("s_cb")
        s_cbs = sem("s_cbs")
        s_tfb = sem("s_tfb")
        s_m = sem("s_m")
        s_y = sem("s_y")
        s_yo = sem("s_yo")
        s_yz = sem("s_yz")
        s_gs = sem("s_gs")
        s_ssd = sem("s_ssd")
        s_mixT = sem("s_mixT")
        s_o = sem("s_o")
        s_res = sem("s_res")
        s_x1 = sem("s_x1")
        s_x1T = sem("s_x1T")
        s_rowst = sem("s_rowst")
        s_lg = sem("s_lg")
        s_lgT = sem("s_lgT")
        s_lge = sem("s_lge")
        s_lgd = sem("s_lgd")
        s_affT = sem("s_affT")
        s_top = sem("s_top")
        s_topT = sem("s_topT")
        s_idx = sem("s_idx")
        s_pT = sem("s_pT")
        s_pg = sem("s_pg")
        s_sig = sem("s_sig")
        s_base = sem("s_base")
        s_acc = [sem(f"s_acc{i}") for i in range(2)]
        s_wple = sem("s_wple")
        s_gath = sem("s_gath")
        s_idg = sem("s_idg")
        s_ids = sem("s_ids")
        s_xeT_p = sem("s_xeT_p")
        s_xeT = sem("s_xeT")
        s_raw = [sem(f"s_raw{j}") for j in range(NB)]
        s_high = sem("s_high")
        s_low = sem("s_low")
        s_used = sem("s_used")
        s_xeT_h = sem("s_xeT_h")
        s_hs = sem("s_hs")
        s_hid = sem("s_hid")
        s_hT_p = sem("s_hT_p")
        s_hT_h = sem("s_hT_h")
        s_hT = sem("s_hT")
        s_ye = sem("s_ye")
        s_scat = sem("s_scat")
        s_fin = [sem(f"s_fin_{t}") for t in range(NT)]
        s_ln2 = sem("s_ln2")
        s_bple = sem("s_bple")
        s_bn = sem("s_bn")
        s_mv = sem("s_mv")
        s_inv = sem("s_inv")
        s_ln_s = sem("s_ln_s")
        s_ln_z = sem("s_ln_z")
        s_ln_g = sem("s_ln_g")
        s_y2 = sem("s_y2")
        s_y2_last = sem("s_y2_last")
        s_out = sem("s_out")

        tok_groups = [(kind, t) for t in range(NT) for kind in ("q", "kv")]
        xbc_groups = [("xbc", m, s) for m in range(KC) for s in range(2)]
        z_groups = [("z", t) for t in range(NT)]
        groups = tok_groups + xbc_groups + z_groups
        gidx = {g: n for n, g in enumerate(groups)}
        COLS = {"q": (0, K0), "kv": (K0, 256), "z": (0, 512)}
        tr_units = [(s_xT, t + 1) for t in range(NT)] + [(s_cw, 1)] \
            + [(s_xB, t + 1) for t in range(NT)] + [(s_qkT, t + 1) for t in range(NT)]
        U_XB, U_QK = NT + 1, 2 * NT + 1
        att_units = [(t, 4 * i + j) for t in range(NT) for i in range(NKV) for j in range(4)]
        NU = len(att_units)
        NG = NU // 4
        seq_of = {t: (a, n) for a, n in SEQS for t in range(a, a + n)}
        ssd_units = [(t, g) for t in range(NT) for g in range(GROUPS)]
        assert len(ssd_units) == NG
        EARLY = 8
        ple_units = [(h, t) for h in range(2) for t in range(NT)]
        upd = []
        n0 = 0
        prev_at = {}
        for a, n in SEQS:
            for i in range(n - 1):
                prev_at[0, a + 1 + i] = n0 + i
                prev_at[1, a + n - 2 - i] = n0 + i
                for g in range(GROUPS):
                    upd.append((0, a + i, g, n0 + i, i == 0))
                    upd.append((1, a + n - 1 - i, g, n0 + i, i == 0))
            n0 += n - 1

        QC = D // (2 * P)
        FIRST, PER = 2 * QC, 3 * QC

        def buf(i):
            return i % NB

        def buf0(n):
            return (n + NB - FIRST % NB) % NB

        def seq(e, i):
            return PER * e + (FIRST - PER + i)

        def landed(e, i):
            before = [buf0(n) for n in range(FIRST)].count(buf(i))
            return 16 * (PER // NB) * (e - 1) + 16 * (before + 1 + i // NB)

        DT, ANEG, ACUM, EA, WDEC, CD, W1, W2 = range(8)

        def d16(r):
            return dtw[:, r, :].rearrange("p (t c) -> p t c", t=NT)

        block = ctx.enter_context(nc.Block())

        class Chain:

            def __init__(self, eng, s):
                self.eng, self.s, self.n = eng, s, 0

            def step(self, ins):
                self.n += 1
                ins.then_inc(self.s, 1)

            def settle(self):
                self.eng.wait_ge(self.s, self.n)

            def link(self, ins):
                self.step(ins)
                self.settle()

        @block.sync
        def _(sp):
            win = A["w_in"][0].rearrange("(k p) c -> p k c", p=P)
            wout = A["w_out"][0].rearrange("(k p) c -> p k c", p=P)
            wpg = A["w_ple_gate"][0].rearrange("(k p) c -> p k c", p=P)

            def xtile(name, i):
                return A[name][0][i * P:(i + 1) * P, :]

            def bc(ap):
                return ap.partition_broadcast(P)

            def load_x(t):
                src = xtile("x_prompt", t) if t < TP else xtile("x_sample", t - TP)
                sp.dma_start(xa[:, t, :], src).then_inc(s_xin[t], 16)

            load_x(0)
            sp.dma_start(cst[:, 0:P], consts[:, 0:P]).then_inc(s_const, 16)
            sp.dma_start(gA, bc(A["ln_in_g"])).then_inc(s_const, 16)
            sp.dma_start(bA, bc(A["ln_in_b"])).then_inc(s_const, 16)
            load_x(1)
            sp.dma_start(slotk[0], win[:, :, 0:K0]).then_inc(s_slot[0], 16)
            load_x(2)
            sp.dma_start(wkv[:, :, 0:256],
                         win[:, :, K0:Z0]).then_inc(s_slot[1], 16)
            sp.dma_start(wkv[:, :, 256:272],
                         win[:, :, DT0:IN_COLS]).then_inc(s_slot[1], 16)
            sp.dma_start(cst[:, P:], consts[:, P:]).then_inc(s_tab, 16)
            for t in range(3, NT):
                load_x(t)
            sp.dma_start(slotk[2], win[:, :, XBC0:XBC0 + 512]).then_inc(s_slot[2], 16)
            small2 = [(gB[:], bc(A["ln1_g"][0])), (bB[:], bc(A["ln1_b"][0])),
                      (ssdw[:], bc(A["ssd_norm_w"][0])),
                      (qkw[:, 0, :], bc(A["q_norm_w"][0])), (qkw[:, 1, :], bc(A["k_norm_w"][0])),
                      (hpar[:, 0, :], bc(A["dt_bias"][0].rearrange("d h -> (d h)"))),
                      (hpar[:, 1, :], bc(A["a_log"][0].rearrange("d h -> (d h)"))),
                      (hpar[:, 2, 0:NH], bc(A["d_skip"][0])),
                      (wr[:], A["w_router"][0].rearrange("(k p) e -> p k e", p=P)),
                      (cw_rows[0:TAPS, :], A["conv_w"][0]), (cw_rows[TAPS:TAPS + 1, :], A["conv_b"])]
            for dst, src in small2:
                sp.dma_start(dst, src).then_inc(s_param, 16)
            sp.wait_ge(s_proj, gidx["q", NT - 1] + 1)
            sp.dma_start(slotk[0], win[:, :, XBC0 + 512:DT0]).then_inc(s_slot[0], 16)
            sp.wait_ge(s_proj, gidx["kv", NT - 1] + 1)
            sp.dma_start(slotk[1], win[:, :, Z0:XBC0]).then_inc(s_slot[1], 16)
            sp.wait_ge(s_proj, gidx["xbc", 3, 1] + 1)

            def load_wout(j, h):
                c = slice(h * 512, (h + 1) * 512)
                for i in range(2):
                    rows = A["w_out"][0][i * 256:(i + 1) * 256, c].rearrange("(k p) c -> p k c", p=HD)
                    sp.dma_start(slotk[j][i * HD:(i + 1) * HD, 0:4, :], rows).then_inc(s_slot[j], 16)
                sp.dma_start(slotk[j][:, 4:8, :], wout[:, 4:8, c]).then_inc(s_slot[j], 16)

            load_wout(2, 0)
            sp.wait_ge(s_ao, NG)
            sp.wait_ge(s_yo, NG)
            load_wout(0, 1)
            pt = [(ptok[:, 0:TP, :], A["p_prompt"][0, 0]), (ptok[:, TP:NT, :], A["p_sample"][0, 0])]
            for dst, src in pt:
                sp.dma_start(dst, src.rearrange("(t p) c -> p t c", p=P)).then_inc(s_ple_in, 16)
            sp.dma_start(slotk[1], wpg[:, :, 0:512]).then_inc(s_slot[1], 16)
            sp.dma_start(wple[:], A["w_ple"][0].rearrange("(k p) c -> p k c", p=P)).then_inc(s_wple, 16)
            for h in range(2):
                sp.dma_start(bple[h], A["b_ple_gate"][:, h * 512:(h + 1) * 512]).then_inc(s_bple, 16)

            wg = A["w_e_gate"][0].rearrange("e (k p) f -> e p k f", p=P)
            wu = A["w_e_up"][0].rearrange("e (k p) f -> e p k f", p=P)
            wd = A["w_e_down"][0].rearrange("e (k p) f -> e p k f", p=P)

            def load(j, w, e, q):
                sp.dma_start(raw[j].rearrange("p (k c) -> p k c", k=2),
                             w[e, :, 2 * q:2 * q + 2, :]).then_inc(s_raw[j], 16)

            sp.wait_ge(s_gs, NG)
            for n in range(NB):
                load(buf0(n), (wg, wu)[n // QC], 0, n % QC)
            sp.wait_ge(s_o, NT)
            sp.dma_start(slotk[2], wpg[:, :, 512:D]).then_inc(s_slot[2], 16)
            for n in range(NB, FIRST):
                sp.wait_ge(s_low, n - NB + 1)
                load(buf0(n), (wg, wu)[n // QC], 0, n % QC)
            sp.wait_ge(s_top, 1)
            sp.dma_start(gB[:], bc(A["ln2_g"][0])).then_inc(s_ln2, 16)
            sp.dma_start(bB[:], bc(A["ln2_b"][0])).then_inc(s_ln2, 16)
            with sp.Fori(1, NE) as e:
                for i in range(PER):
                    sp.wait_ge(s_low, seq(e, i) - NB + 1)
                    load(buf(i), (wg, wu, wd)[i // QC], e if i < 2 * QC else e - 1, i % QC)
            for q in range(QC):
                sp.wait_ge(s_low, seq(NE, q) - NB + 1)
                load(buf(q), wd, NE - 1, q)
            sp.wait_ge(s_scat, 16 * NE)
            for t in range(NT):
                sp.dma_start(fin[:, t, :], acc_rows[t * P:(t + 1) * P, :]).then_inc(s_fin[t], 16)
            for t in range(NT):
                if t + 1 < NT:
                    sp.wait_ge(s_y2, t + 1)
                else:
                    sp.wait_ge(s_y2_last, 1)
                dst = out_prompt[0] if t < TP else out_sample[0]
                i = t if t < TP else t - TP
                sp.dma_start(dst[i * P:(i + 1) * P, :], fin[:, t, :]).then_inc(s_out, 16)
            sp.wait_ge(s_out, 16 * NT)
            sp.wait_ge(s_rowst, 16 * NT)
            for s in s_acc:
                sp.wait_ge(s, 16 * NT)

        @block.gpsimd
        def _(pool):
            ch = Chain(pool, s_pool)
            nc.gpsimd.memset(ones[:], 1.0)
            for c0, w in ((0, 2), (2 + TP * P, 2), (4 + T, 2)):
                last = nc.gpsimd.memset(u_pad[:, :, c0:c0 + w], 0.0)
            last.then_inc(s_prep, 1)
            pool.wait_ge(s_const, 16 * 3)
            pool.wait_ge(s_tab, 16)
            pool.wait_ge(s_xa, NT)
            for t in range(NT):
                pool.wait_ge(s_rr, t + 1)
                for src, h0, n, w in ((mix[:, t, 0:512], 0, NQ, 0), (kvd[:, t, 0:P], NQ, NKV, 1)):
                    v = src.rearrange("p (h c) -> p h c", c=HD)
                    rs = qks[:, t % 2, 2, h0:h0 + n].unsqueeze(2).broadcast_to([P, n, HD])
                    ch.link(nc.gpsimd.tensor_tensor(v, v, rs, ALU.mult))
                    wb = qkw[:, w, :].unsqueeze(1).broadcast_to([P, n, HD])
                    ch.link(nc.gpsimd.tensor_tensor(v, v, wb, ALU.mult))
                    halves = src.rearrange("p (h a i f) -> p i h a f", a=2, i=2, f=16)
                    x1, x2 = halves[:, 0], halves[:, 1]
                    c, sn = [rope[:, t, i].unsqueeze(1).broadcast_to([P, n, 2, 16]) for i in range(2)]
                    tmp = [rot[:, i, 0:n * 32].rearrange("p (h a f) -> p h a f", a=2, f=16) for i in range(2)]
                    ch.step(nc.gpsimd.tensor_tensor(tmp[0], x2, sn, ALU.mult))
                    ch.link(nc.gpsimd.tensor_tensor(tmp[1], x1, sn, ALU.mult))
                    ch.step(nc.gpsimd.tensor_tensor(x1, x1, c, ALU.mult))
                    ch.link(nc.gpsimd.tensor_tensor(x2, x2, c, ALU.mult))
                    ch.step(nc.gpsimd.tensor_tensor(x1, x1, tmp[0], ALU.subtract))
                    last = nc.gpsimd.tensor_tensor(x2, x2, tmp[1], ALU.add)
                    if w == 0:
                        ch.link(last)
                last.then_inc(s_rope, 1)
                pool.wait_ge(s_rope, t + 1)
            pool.wait_ge(s_cums, 2)
            pool.wait_ge(s_xB, NT)
            for n, (d, t, g, i, first) in enumerate(upd):
                if n >= 2:
                    pool.wait_ge(s_st, n - 1)
                o = xsc[:, n % 2, :].rearrange("p (h c) -> p h c", h=HPG)
                xin = xtok[:, t, g * 256:(g + 1) * 256].rearrange("p (h c) -> p h c", h=HPG)
                w = d16(WDEC)[:, t, d * NH + g * HPG:d * NH + (g + 1) * HPG]
                nc.gpsimd.tensor_tensor(o, xin, w.unsqueeze(2).broadcast_to([P, HPG, HD]),
                                        ALU.mult).then_inc(s_ws, 1)
            pool.wait_ge(s_proj, len(groups))
            nc.gpsimd.memset(kz, 0.0).then_inc(s_kz, 1)

            def heads(ap):
                return ap.rearrange("p (h c) -> p h c", h=HPG)

            def normalise(u):
                L = seq_of[att_units[u][0]][1] * P
                pool.wait_ge(s_rc, u + 1)
                nc.gpsimd.tensor_scalar(prob[:, u % 4, 0:L], prob[:, u % 4, 0:L], att[:, 2, u:u + 1], None,
                                        ALU.mult).then_inc(s_pn, 1)

            def ssd_sums(n):
                t, g = ssd_units[n]
                pool.wait_ge(s_tfb, n + 1)
                if n:
                    pool.wait_ge(s_y, n)
                nc.gpsimd.tensor_tensor(msum, dec[:, 0], dec[:, 1], ALU.add).then_inc(s_m, 1)
                if n:
                    pool.wait_ge(s_yo, n)
                pool.wait_ge(s_offm, n + 1)
                dsk = hpar[:, 2, g * HPG:(g + 1) * HPG].unsqueeze(2).broadcast_to([P, HPG, HD])
                ch.link(nc.gpsimd.tensor_tensor(heads(yadd), heads(xtok[:, t, g * 256:(g + 1) * 256]), dsk, ALU.mult))
                dirs = [d for d in range(2) if (d, t) in prev_at]
                for d in dirs:
                    last = nc.gpsimd.tensor_tensor(yadd, yadd, offm[:, d, :], ALU.add)
                    if d != dirs[-1]:
                        ch.link(last)
                last.then_inc(s_t, 1)

            def gate(n):
                t, g = ssd_units[n]
                pool.wait_ge(s_yo, n + 1)
                z = mix[:, t, 512 + g * 256:512 + (g + 1) * 256]
                nc.gpsimd.tensor_tensor(z, ysum, z, ALU.mult).then_inc(s_yz, 1)

            pool.wait_ge(s_param, 16 * 11)
            for i in range(NU + 1):
                if i % 2:
                    normalise(i - 1)
                if i % 4 == 2:
                    ssd_sums(i // 4)
                if i % 4 == 0 and i:
                    gate(i // 4 - 1)
            for t in range(NT):
                pool.wait_ge(s_x1, t + 1)
                pool.dma_start(x1_rows[t * P:(t + 1) * P, :], xa[:, t, :]).then_inc(s_rowst, 16)

            def gather():
                pool.indirect_dma_start(xe, None, x1_rows,
                                        bass.IndirectOffsetOnAxis(ap=idx_now[:, 0:1], axis=0)
                                        ).then_inc(s_gath, 16)

            for u, (h, t) in enumerate(ple_units):
                pool.wait_ge(s_base, u + 1)
                pool.dma_start(acc_rows[t * P:(t + 1) * P, h * 512:(h + 1) * 512],
                               sig[:, u % 2, :]).then_inc(s_acc[u % 2], 16)
                if u == 7:
                    pool.wait_ge(s_rowst, 16 * NT)
                    pool.wait_ge(s_idx, 2)
                    ch.link(nc.gpsimd.tensor_copy(idx_now[:, 0:1], idxT[:, 0:1]))
                    gather()
                if u == 2 * NT - 2:
                    pool.wait_ge(s_xeT_p, 1)
                    ch.link(nc.gpsimd.tensor_copy(idx_now[:, 0:1], idxT[:, 1:2]))
                    gather()
            for s in s_acc:
                pool.wait_ge(s, 16 * NT)

            def scatter():
                pool.indirect_dma_start(acc_rows, bass.IndirectOffsetOnAxis(ap=idx_now[:, 1:2], axis=0),
                                        ye, None, compute_op=ALU.add).then_inc(s_scat, 16)

            def pick(col, e):
                return nc.gpsimd.tensor_copy(idx_now[:, col:col + 1], idxT[:, bass.ds(e, 1)])

            pool.wait_ge(s_xeT_p, 2)
            ch.link(pick(0, 2))
            gather()
            with pool.Fori(1, NE - 2) as f:
                pool.wait_ge(s_xeT_p, f + 2)
                pick(0, f + 2).then_inc(s_idg, 1)
                pool.wait_ge(s_const, 16 * 3)
                pool.wait_ge(s_idg, f)
                gather()
                pool.wait_ge(s_ye, f)
                pick(1, f - 1).then_inc(s_ids, 1)
                pool.wait_ge(s_const, 16 * 3)
                pool.wait_ge(s_ids, f)
                scatter()
            for e in (NE - 3, NE - 2, NE - 1):
                pool.wait_ge(s_ye, e + 1)
                ch.link(pick(1, e))
                scatter()
            pool.wait_ge(s_scat, 16 * NE)
            for t in range(NT - 1):
                pool.wait_ge(s_ln_g, t + 1)
                nc.gpsimd.tensor_tensor(fin[:, t, :], fin[:, t, :], bB[:], ALU.add).then_inc(s_y2, 1)

        @block.scalar
        def _(act):
            ch = Chain(act, s_act)
            nvar = [0]

            def root():
                nvar[0] += 1
                act.wait_ge(s_var, nvar[0])

            def copy(o, i):
                return nc.scalar.activation(o, i, ACT.Copy)

            def x_std(t):
                root()
                nc.scalar.activation(sd[:, 0, t:t + 1], sd[:, 0, t:t + 1], ACT.Sqrt).then_inc(s_std, 1)

            def xT_out(t):
                act.wait_ge(s_tr, t + 1)
                b = 2 * (t % 2)
                for half in range(2):
                    last = copy(xT[:, 4 * half:4 * half + 4, t * P:(t + 1) * P],
                                ps[:, b + half, :].rearrange("p (k c) -> p k c", k=4))
                last.then_inc(s_xT, 1)

            x_std(0)
            xT_out(0)
            x_std(1)
            n = 0
            for g in groups:
                if g[0] == "q" and g[1] + 2 < NT:
                    x_std(g[1] + 2)
                act.wait_ge(s_proj, n + 1)
                bank = ps[:, 4 + n % 4, :]
                if g[0] == "q":
                    copy(mix[:, g[1], 0:512].rearrange("p (j i c) -> p i j c", i=2, j=4),
                         bank.rearrange("p (i j c) -> p i j c", i=2, j=4)).then_inc(s_projo, 1)
                    if g[1] + 1 < NT:
                        xT_out(g[1] + 1)
                elif g[0] == "kv":
                    copy(kvd[:, g[1], :], bank[:, 0:272]).then_inc(s_projo, 1)
                elif g[0] == "xbc":
                    a, w = SEQS[g[2]]
                    c0 = 2 + a * P + 2 * g[2]
                    copy(u_pad[:, g[1], c0:c0 + w * P], bank[:, 0:w * P]).then_inc(s_projo, 1)
                    if g[2] == 1 and g[1] < NT:
                        root()
                        nc.scalar.activation(qks[:, g[1] % 2, 1, :], qks[:, g[1] % 2, 0, :],
                                             ACT.Sqrt).then_inc(s_std, 1)
                    if g[1:] == (NT, 1):
                        act.wait_ge(s_dt1, 1)
                        nc.scalar.activation(dtw[:, W1, :], dtw[:, W1, :], ACT.Exp)
                        nc.scalar.activation(hpar[:, 1, :], hpar[:, 1, :], ACT.Exp).then_inc(s_dt2, 1)
                        act.wait_ge(s_dt1, 2)
                        nc.scalar.activation(dtw[:, ACUM, :], dtw[:, W2, :], ACT.Ln).then_inc(s_dt2, 1)
                else:
                    if g[1] == 0:
                        for m in range(KC):
                            act.wait_ge(s_conv, m + 1)
                            nc.scalar.activation(conv[:, m, :], conv[:, m, :], ACT.Silu).then_inc(s_silu, 1)
                        act.wait_ge(s_proj, n + 1)
                    nc.scalar.activation(mix[:, g[1], 512:D], ps[:, 4 + n % 2, :], ACT.Silu).then_inc(s_projo, 1)
                    if g[1] == 0:
                        act.wait_ge(s_cums, 1)
                        nc.scalar.activation(dtw[:, EA, :], dtw[:, ACUM, :], ACT.Exp)
                        nc.scalar.activation(dtw[:, WDEC, :], dtw[:, W1, :], ACT.Exp)
                        nc.scalar.activation(dtw[:, CD, :], dtw[:, CD, :], ACT.Exp).then_inc(s_ecum, 1)
                    elif g[1] <= 3:
                        for t in (2 * g[1] - 2, 2 * g[1] - 1):
                            u = U_XB + t
                            act.wait_ge(s_tr, u + 1)
                            b = 2 * (u % 2)
                            copy(xtok[:, t, :], ps[:, b, :])
                            copy(btok[:, t, :], ps[:, b + 1, 0:256]).then_inc(s_xB, 1)
                n += 1
            act.wait_ge(s_kz, 1)
            for t in range(NT):
                u = U_QK + t
                act.wait_ge(s_tr, u + 1)
                b = 2 * (u % 2)
                tc = slice(t * P, (t + 1) * P)
                copy(qT[:, :, tc], ps[:, b, :].rearrange("p (j c) -> p j c", j=4))
                for i in range(NKV):
                    last = copy(kz[i * HD:(i + 1) * HD, i, tc], ps[i * HD:(i + 1) * HD, b + 1, 0:P])
                last.then_inc(s_qkT, 1)

            def probabilities(u):
                L = seq_of[att_units[u][0]][1] * P
                act.wait_ge(s_max, u + 1)
                if u >= 4:
                    act.wait_ge(s_pt, u - 3)
                nc.scalar.activation(prob[:, u % 4, 0:L], ps[:, u % 3, 0:L], ACT.Exp,
                                     bias=att[:, 0, u:u + 1], scale=HD ** -0.5,
                                     accum_out=att[:, 1, u:u + 1]).then_inc(s_exp, 1)

            def decays(n, d):
                t, g = ssd_units[n]
                act.wait_ge(s_dec, n + 1)
                if n:
                    act.wait_ge(s_m, n)
                for h in range(HPG):
                    c = d * NH + g * HPG + h
                    last = nc.scalar.activation(dec[:, d, h], ps[:, 5 + d, h * P:(h + 1) * P],
                                                ACT.Relu, bias=d16(ACUM)[:, t, c:c + 1], scale=-1.0)
                ch.link(last)
                v = dec[:, d].rearrange("p h l -> p (h l)")
                nc.scalar.activation(v, v, ACT.Exp, scale=-1.0).then_inc(s_edec, 1)

            def squares(n):
                t, g = ssd_units[n]
                act.wait_ge(s_yz, n + 1)
                if n:
                    act.wait_ge(s_gs, n)
                nc.scalar.activation(ysq, mix[:, t, 512 + g * 256:512 + (g + 1) * 256], ACT.Square,
                                     accum_out=gss[:, 0, n:n + 1]).then_inc(s_gs, 1)

            def group_root(a, b):
                root()
                nc.scalar.activation(gss[:, 1, a:b], gss[:, 1, a:b], ACT.Sqrt).then_inc(s_std, 1)

            for i in range(NU + 1):
                if i < NU:
                    probabilities(i)
                if i % 2 == 0 and i:
                    u = i - 1
                    act.wait_ge(s_rc, u + 1)
                    v = prob[:, u % 4, 0:seq_of[att_units[u][0]][1] * P]
                    nc.scalar.activation(v, v, ACT.Copy, scale=att[:, 2, u:u + 1]).then_inc(s_pna, 1)
                if i < NU:
                    if i % 4 < 2:
                        decays(i // 4, i % 4)
                if i % 4 == 2 and i > 4:
                    squares(i // 4 - 1)
                if i == 4 * EARLY + 6:
                    group_root(0, EARLY)
            squares(NG - 1)
            group_root(EARLY, NG)

            def mix_turned(t):
                act.wait_ge(s_tr, 3 * NT + 1 + t + 1)
                copy(xT[:, 4:8, t * P:(t + 1) * P],
                     ps[:, t % 4, :].rearrange("p (k c) -> p k c", k=4)).then_inc(s_mixT, 1)

            for t in range(NT):
                mix_turned(t)
            act.wait_ge(s_tr, 4 * NT + 2)
            for b in range(3):
                last = copy(pT[:, :, 2 * b * P:2 * (b + 1) * P],
                            ps[:, b, :].rearrange("p (k c) -> p k c", k=2))
            last.then_inc(s_pT, 1)

            def sigmoid(u):
                act.wait_ge(s_pg, u + 1)
                if u >= 2:
                    act.wait_ge(s_acc[u % 2], 16 * (u // 2))
                nc.scalar.activation(sig[:, u % 2, :], ps[:, 2 * (u % 2), :], ACT.Sigmoid).then_inc(s_sig, 1)

            for t in range(NT):
                root()
                nc.scalar.activation(sd[:, 0, t:t + 1], sd[:, 0, t:t + 1], ACT.Sqrt).then_inc(s_std, 1)
                act.wait_ge(s_tr, 4 * NT + 2 + t + 1)
                b = 2 * (t % 2)
                for half in range(2):
                    last = copy(xT[:, 4 * half:4 * half + 4, t * P:(t + 1) * P],
                                ps[:, b + half, :].rearrange("p (k c) -> p k c", k=4))
                last.then_inc(s_x1T, 1)
            sigmoid(0)
            act.wait_ge(s_lg, 1)
            act.wait_ge(s_x1, NT)
            copy(logitsT[:, 0:512], ps[0:NE, 4, :])
            copy(logitsT[:, 512:T], ps[0:NE, 5, 0:T - 512]).then_inc(s_lgT, 1)
            sigmoid(1)
            act.wait_ge(s_lgd, 1)
            nc.scalar.activation(rt[:, 0, :], rt[:, 0, :], ACT.Exp).then_inc(s_lge, 1)
            def split(j, landings):
                act.wait_ge(s_raw[j], landings)
                copy(high[j], raw[j]).then_inc(s_high, 1)

            def split0(n):
                if n >= NB:
                    act.wait_ge(s_used, n - NB + 1)
                split(buf0(n), 16 * (n // NB + 1))

            def split_next(e, i):
                act.wait_ge(s_used, seq(e, i) - NB + 1)
                split(buf(i), landed(e, i))

            def high8(dst, done):
                for half in range(2):
                    last = copy(dst[0][:, 4 * half:4 * half + 4, :],
                                ps[:, 6 + half, 0:4 * CAP].rearrange("p (k c) -> p k c", k=4))
                last.then_inc(done, 1)

            def rows_high(e):
                act.wait_ge(s_xeT_p, e + 1)
                high8(xeT, s_xeT_h)

            def hid_high(e):
                act.wait_ge(s_hT_p, e + 1)
                high8(hidT, s_hT_h)

            def silu(e, first=False):
                act.wait_ge(s_used, (QC if first else seq(e, QC)))
                nc.scalar.activation(hid, ps[0:CAP, 0:2, :].rearrange("p b c -> p (b c)"),
                                     ACT.Silu).then_inc(s_hs, 1)

            for u in range(2, 2 * NT - 1):
                sigmoid(u)
                if u == NT + 1:
                    act.wait_ge(s_o, NT)
                    split0(0)
                if u == NT + 2:
                    split0(1)
                if u == NT + 3:
                    act.wait_ge(s_pg, NT)
                    split0(2)
            act.wait_ge(s_base, NT + 2)
            act.wait_ge(s_rowst, 16 * NT)
            rows_high(0)
            sigmoid(2 * NT - 1)
            act.wait_ge(s_pg, 2 * NT)
            split0(3)
            split0(4)
            split0(5)
            split0(6)
            act.wait_ge(s_base, 2 * NT)
            silu(0, first=True)
            split0(7)
            for i in range(3):
                split_next(1, i)
            rows_high(1)
            with act.Fori(1, NE - 1) as e:
                for i in range(3, 7):
                    split_next(e, i)
                hid_high(e - 1)
                silu(e)
                for i in range(7, 11):
                    split_next(e, i)
                rows_high(e + 1)
                split_next(e, 11)
                for i in range(3):
                    split_next(e + 1, i)
            for i in range(3, 7):
                split_next(NE - 1, i)
            hid_high(NE - 2)
            silu(NE - 1)
            for i in range(7, 11):
                split_next(NE - 1, i)
            act.wait_ge(s_hT_p, NE)
            high8(xeT, s_hT_h)
            split_next(NE - 1, 11)
            for q in range(QC):
                split_next(NE, q)
            for t in range(NT):
                root()
                nc.scalar.activation(sd[:, 0, t:t + 1], sd[:, 0, t:t + 1], ACT.Sqrt).then_inc(s_std, 1)
                act.wait_ge(s_ln_s, t + 1)
                nc.scalar.activation(fin[:, t, :], fin[:, t, :], ACT.Identity, bias=mv[:, t, 1:2],
                                     scale=sd[:, 1, t:t + 1]).then_inc(s_ln_z, 1)

        @block.vector
        def _(dve):
            ch = Chain(dve, s_dve)
            nroot = [0]

            def ln_stats(t, src, eps):
                for half in range(2):
                    ch.step(nc.vector.bn_stats(stats[:, t % 2, 6 * half:6 * half + 6],
                                               src[:, half * 512:(half + 1) * 512]))
                ch.settle()
                ch.link(nc.vector.bn_aggr(mv[:, t, :], stats[:, t % 2, :]))
                nc.vector.tensor_scalar(sd[:, 0, t:t + 1], mv[:, t, 1:2], eps, None, ALU.add).then_inc(s_var, 1)

            def ln_apply(t, x, o, g, b, done, landed=None):
                nroot[0] += 1
                dve.wait_ge(s_std, nroot[0])
                ch.link(nc.vector.reciprocal(sd[:, 1, t:t + 1], sd[:, 0, t:t + 1]))
                ch.link(nc.vector.tensor_scalar(o, x, mv[:, t, 0:1], sd[:, 1, t:t + 1], ALU.subtract, ALU.mult))
                if landed:
                    dve.wait_ge(*landed)
                ch.link(nc.vector.tensor_tensor(o, o, g[:], ALU.mult))
                nc.vector.tensor_tensor(o, o, b[:], ALU.add).then_inc(done, 1)

            for t in range(NT):
                dve.wait_ge(s_xin[t], 16)
                ln_stats(t, xa[:, t, :], LN_EPS)
                ln_apply(t, xa[:, t, :], xa[:, t, :], gA, bA, s_xa, landed=(s_const, 16 * 3))
            dve.wait_ge(s_tr, NT + 1)
            b = 2 * (NT % 2)
            nc.vector.tensor_copy(cw[:], ps[:, b, 0:KC * (TAPS + 1)].rearrange("p (m j) -> p m j", m=KC)
                                  ).then_inc(s_cw, 1)
            dve.wait_ge(s_cw, 1)

            def qk_rms(t):
                dve.wait_ge(s_projo, gidx["kv", t] + 1)
                q = mix[:, t, 0:512]
                k = kvd[:, t, 0:P]
                sq = qksq[:]
                ch.step(nc.vector.tensor_tensor(sq[:, 0:512], q, q, ALU.mult))
                ch.link(nc.vector.tensor_tensor(sq[:, 512:640], k, k, ALU.mult))
                if t >= 2:
                    dve.wait_ge(s_rope, t - 1)
                ch.link(nc.vector.tensor_reduce(qks[:, t % 2, 0, :], sq.rearrange("p (h c) -> p h c", c=HD), X, ALU.add))
                nc.vector.tensor_scalar(qks[:, t % 2, 0, :], qks[:, t % 2, 0, :], 1.0 / HD, NORM_EPS, ALU.mult,
                                        ALU.add).then_inc(s_var, 1)
                nroot[0] += 1
                dve.wait_ge(s_std, nroot[0])
                nc.vector.reciprocal(qks[:, t % 2, 2, :], qks[:, t % 2, 1, :]).then_inc(s_rr, 1)

            def conv_tile(m):
                dve.wait_ge(s_projo, gidx["xbc", m, 1] + 1)
                ch.link(nc.vector.tensor_scalar(conv[:, m, :], u_pad[:, m, 0:CW], cw[:, m, 0:1],
                                                cw[:, m, TAPS:TAPS + 1], ALU.mult, ALU.add))
                for j in range(1, TAPS):
                    ins = nc.vector.scalar_tensor_tensor(conv[:, m, :], u_pad[:, m, j:j + CW], cw[:, m, j:j + 1],
                                                         conv[:, m, :], ALU.mult, ALU.add)
                    if j == TAPS - 1:
                        ins.then_inc(s_conv, 1)
                    else:
                        ch.link(ins)

            dve.wait_ge(s_param, 16 * 11)
            dve.wait_ge(s_prep, 1)
            def dt_first():
                raw = kvd[:, :, 256:272]
                ch.link(nc.vector.tensor_tensor(d16(DT), raw, hpar[:, 0, :].unsqueeze(1).broadcast_to([P, NT, 16]),
                                                ALU.add))
                nc.vector.scalar_tensor_tensor(dtw[:, W1, :], dtw[:, DT, :], -1.0, dtw[:, DT, :], ALU.mult,
                                               ALU.min).then_inc(s_dt1, 1)
                dve.wait_ge(s_dt2, 1)
                nc.vector.tensor_scalar(dtw[:, W2, :], dtw[:, W1, :], 1.0, None, ALU.add).then_inc(s_dt1, 1)
                dve.wait_ge(s_dt1, 2)

            for m in range(KC):
                if m < NT:
                    qk_rms(m)
                if m == NT:
                    dt_first()
                if m:
                    conv_tile(m - 1)
            ch.link(nc.vector.tensor_scalar(dtw[:, EA, :], dtw[:, W2, :], 1.0, None, ALU.is_equal))
            dve.wait_ge(s_dt2, 2)
            ch.step(nc.vector.tensor_tensor(dtw[:, ACUM, :], dtw[:, ACUM, :], dtw[:, EA, :], ALU.add))
            ch.link(nc.vector.scalar_tensor_tensor(dtw[:, W2, :], dtw[:, W2, :], -1.0, dtw[:, EA, :], ALU.add, ALU.add))
            ch.link(nc.vector.reciprocal(dtw[:, W2, :], dtw[:, W2, :]))
            ch.link(nc.vector.tensor_tensor(dtw[:, W1, :], dtw[:, W1, :], dtw[:, ACUM, :], ALU.mult))
            ch.link(nc.vector.tensor_tensor(dtw[:, W1, :], dtw[:, W1, :], dtw[:, W2, :], ALU.mult))
            ch.link(nc.vector.scalar_tensor_tensor(dtw[:, DT, :], dtw[:, DT, :], 0.0, dtw[:, W1, :], ALU.max, ALU.add))
            nc.vector.scalar_tensor_tensor(d16(ANEG), d16(DT), -1.0,
                                           hpar[:, 1, :].unsqueeze(1).broadcast_to([P, NT, 16]), ALU.mult,
                                           ALU.mult).then_inc(s_a, 1)
            conv_tile(KC - 1)
            dve.wait_ge(s_tab, 16)
            dve.wait_ge(s_conv, KC)
            dve.wait_ge(s_a, 1)
            nc.vector.tensor_copy(tri_r, tri)
            ch.link(nc.vector.tensor_copy(a_r[0], d16(ANEG)))
            nc.vector.tensor_tensor(a_r[1], d16(ANEG), a_r[0], ALU.subtract).then_inc(s_ar, 1)
            dve.wait_ge(s_cum, 1)
            cum = ps[:, 6, 0:NT * 16].rearrange("p (d t h) -> p t d h", d=2, h=NH)
            tot = ps[:, 7, 0:NT * 16]
            a4 = dtw[:, ACUM, :].rearrange("p (t d h) -> p t d h", d=2, h=NH)
            ch.step(nc.vector.tensor_copy(dtw[:, CD, :], tot))
            ch.link(nc.vector.tensor_copy(a4, cum))
            nc.vector.tensor_tensor(dtw[:, W1, :], dtw[:, CD, :], dtw[:, ACUM, :], ALU.subtract).then_inc(s_cums, 1)
            dve.wait_ge(s_ecum, 1)
            nc.vector.tensor_tensor(dtw[:, WDEC, :], dtw[:, WDEC, :], dtw[:, DT, :], ALU.mult).then_inc(s_cums, 1)

            for n, (d, t, g, i, first) in enumerate(upd):
                dve.wait_ge(s_st, n + 1)
                new = state[:, d, g, i, :]
                prod = ps[:, 6 + n % 2, 0:256]
                if first:
                    nc.vector.tensor_copy(new, prod).then_inc(s_sts, 1)
                else:
                    dve.wait_ge(s_sts, n - 3)
                    o = new.rearrange("p (h c) -> p h c", h=HPG)
                    old = state[:, d, g, i - 1, :].rearrange("p (h c) -> p h c", h=HPG)
                    w = d16(CD)[:, t, d * NH + g * HPG:d * NH + (g + 1) * HPG]
                    ch.link(nc.vector.tensor_tensor(o, old, w.unsqueeze(2).broadcast_to([P, HPG, HD]), ALU.mult))
                    nc.vector.tensor_tensor(new, new, prod, ALU.add).then_inc(s_sts, 1)

            def row_max(u):
                L = seq_of[att_units[u][0]][1] * P
                dve.wait_ge(s_sc, u + 1)
                ch.link(nc.vector.reduce_max(att[:, 2, u:u + 1], ps[:, u % 3, 0:L], X))
                nc.vector.tensor_scalar(att[:, 0, u:u + 1], att[:, 2, u:u + 1], -(HD ** -0.5), None,
                                        ALU.mult).then_inc(s_max, 1)

            def pt_out(u):
                n = seq_of[att_units[u][0]][1]
                dve.wait_ge(s_pt, u + 1)
                if u >= 8:
                    dve.wait_ge(s_pv, u // 4 - 1)
                nc.vector.tensor_copy(probT[u // 4 % 2][:, 0:n, (u % 4) * P:(u % 4 + 1) * P],
                                      ps[:, 3, 0:n * P].rearrange("p (b c) -> p b c", c=P)).then_inc(s_pts, 1)

            def att_out(G):
                t, i = G // NKV, G % NKV
                dve.wait_ge(s_pv, G + 1)
                nc.vector.tensor_copy(mix[i * HD:(i + 1) * HD, t, 0:512],
                                      ps[i * HD:(i + 1) * HD, 4, :]).then_inc(s_ao, 1)

            def weights(n):
                t, g = ssd_units[n]
                dve.wait_ge(s_cb, n + 1)
                if n:
                    dve.wait_ge(s_tfb, n)
                nc.vector.tensor_tensor(cbT, ps[:, 7, 0:P].unsqueeze(1).broadcast_to([P, 2, P]), tri,
                                        ALU.mult).then_inc(s_cbs, 1)
                dve.wait_ge(s_cbs, n + 1)
                dve.wait_ge(s_edec, 2 * n + 2)
                for d in range(2):
                    for h in range(HPG):
                        c = d * NH + g * HPG + h
                        v = dec[:, d, h]
                        last = nc.vector.scalar_tensor_tensor(v, v, d16(DT)[:, t, c:c + 1], cbT[:, d, :],
                                                              ALU.mult, ALU.mult)
                last.then_inc(s_tfb, 1)
                dve.wait_ge(s_off, n + 1)
                if n:
                    dve.wait_ge(s_t, n)
                for d in range(2):
                    if (d, t) in prev_at:
                        c = d * NH + g * HPG
                        w = d16(EA)[:, t, c:c + HPG].unsqueeze(2).broadcast_to([P, HPG, HD])
                        last = nc.vector.tensor_tensor(
                            offm[:, d, :].rearrange("p (h c) -> p h c", h=HPG),
                            ps[:, 5, d * 256:(d + 1) * 256].rearrange("p (h c) -> p h c", h=HPG), w, ALU.mult)
                last.then_inc(s_offm, 1)

            def y_out(n):
                dve.wait_ge(s_y, n + 1)
                dve.wait_ge(s_t, n + 1)
                if n:
                    dve.wait_ge(s_yz, n)
                nc.vector.tensor_tensor(ysum, yadd, ps[:, 7, 0:256], ALU.add).then_inc(s_yo, 1)

            def group_var(a, b):
                dve.wait_ge(s_gs, b)
                nc.vector.tensor_scalar(gss[:, 1, a:b], gss[:, 0, a:b], 1.0 / 256, NORM_EPS, ALU.mult,
                                        ALU.add).then_inc(s_var, 1)

            def group_scale(a, b):
                nroot[0] += 1
                dve.wait_ge(s_std, nroot[0])
                ch.link(nc.vector.reciprocal(gss[:, 2, a:b], gss[:, 1, a:b]))

            def group_norm(n):
                t, g = ssd_units[n]
                y = mix[:, t, 512 + g * 256:512 + (g + 1) * 256]
                nc.vector.scalar_tensor_tensor(y, y, gss[:, 2, n:n + 1], ssdw[:, g * 256:(g + 1) * 256],
                                               ALU.mult, ALU.mult).then_inc(s_ssd, 1)

            for i in range(NU + 5):
                if i < NU:
                    row_max(i)
                if 1 <= i <= NU:
                    u = i - 1
                    dve.wait_ge(s_exp, u + 1)
                    nc.vector.reciprocal(att[:, 2, u:u + 1], att[:, 1, u:u + 1]).then_inc(s_rc, 1)
                if 3 <= i < NU + 3:
                    pt_out(i - 3)
                if i % 4 == 0 and i >= 8:
                    att_out(i // 4 - 2)
                if i % 4 == 0 and 4 <= i <= NU:
                    y_out(i // 4 - 1)
                if i % 4 == 2 and i < NU:
                    weights(i // 4)
                if i == 4 * EARLY + 5:
                    group_var(0, EARLY)
                if i == 4 * EARLY + 7:
                    group_scale(0, EARLY)
                if 4 * EARLY + 7 < i <= 5 * EARLY + 7:
                    group_norm(i - 4 * EARLY - 8)
            group_var(EARLY, NG)
            group_scale(EARLY, NG)
            for n in range(EARLY, NG):
                group_norm(n)

            for t in range(NT):
                dve.wait_ge(s_o, t + 1)
                b = 4 + 2 * (t % 2)
                nc.vector.scalar_tensor_tensor(xa[:, t, :], xa[:, t, :], ALPHA,
                                               ps[:, b:b + 2, :].rearrange("p b c -> p (b c)"),
                                               ALU.mult, ALU.add).then_inc(s_res, 1)
                dve.wait_ge(s_res, t + 1)
                ln_stats(t, xa[:, t, :], LN_EPS)
                ln_apply(t, xa[:, t, :], xa[:, t, :], gB, bB, s_x1)
            def base(u):
                h, t = ple_units[u]
                dve.wait_ge(s_sig, u + 1)
                b = sig[:, u % 2, :]
                ch.link(nc.vector.tensor_tensor(b, b, ps[:, 2 * (u % 2) + 1, :], ALU.mult))
                nc.vector.scalar_tensor_tensor(b, xa[:, t, h * 512:(h + 1) * 512], ALPHA, b, ALU.mult,
                                               ALU.add).then_inc(s_base, 1)

            base(0)
            base(1)
            dve.wait_ge(s_lg, 2)
            lg = ps[:, 6, 0:NT * NE].rearrange("p (t e) -> p t e", e=NE)
            r0 = rt[:, 0, :].rearrange("p (t e) -> p t e", e=NE)
            ch.link(nc.vector.reduce_max(rs6[:, 0, :], lg, X))
            nc.vector.tensor_tensor(r0, lg, rs6[:, 0, :].unsqueeze(2).broadcast_to([P, NT, NE]),
                                    ALU.subtract).then_inc(s_lgd, 1)
            dve.wait_ge(s_lge, 1)
            ch.link(nc.vector.reduce_sum(rs6[:, 1, :], r0, X))
            ch.link(nc.vector.reciprocal(rs6[:, 2, :], rs6[:, 1, :]))
            nc.vector.tensor_tensor(r0, r0, rs6[:, 2, :].unsqueeze(2).broadcast_to([P, NT, NE]),
                                    ALU.mult).then_inc(s_lgd, 1)
            dve.wait_ge(s_affT, 1)
            ch.link(nc.vector.tensor_copy(affw[0], ps[0:NE, 6:8, :].rearrange("p b c -> p (b c)")[:, 0:T]))
            rounds = 0
            for (a, n), c0, cap in ((SEQS[0], 0, CAPP), (SEQS[1], CAPP, CAPS)):
                lo, hi = a * P, (a + n) * P
                for k in range(cap // 8):
                    v = topv[:, c0 + 8 * k:c0 + 8 * k + 8]
                    cur, nxt = affw[k % 2][:, lo:hi], affw[(k + 1) % 2][:, lo:hi]
                    ch.link(nc.vector.max(v, cur))
                    ch.step(nc.vector.max_index(topi[:, c0 + 8 * k:c0 + 8 * k + 8], v, cur))
                    ch.link(nc.vector.match_replace(nxt, v, cur, -1.0))
                    rounds += 1
                    if rounds % 4 == 0:
                        base(1 + rounds // 4)
            ch.step(nc.vector.tensor_copy(topf[:, 0:CAPP], topi[:, 0:CAPP]))
            ch.link(nc.vector.tensor_copy(topf[:, CAPP:CAP], topi[:, CAPP:CAP]))
            nc.vector.tensor_scalar(topf[:, CAPP:CAP], topf[:, CAPP:CAP], float(TP * P), None, ALU.add).then_inc(s_top, 1)
            base(5)
            base(6)
            dve.wait_ge(s_topT, 1)
            nc.vector.tensor_copy(idxT[:], ps[0:CAP, 5, 0:NE]).then_inc(s_idx, 1)
            nc.vector.tensor_copy(gateT[:], ps[0:CAP, 5, NE:2 * NE]).then_inc(s_idx, 1)
            def split(j):
                nc.vector.tensor_tensor(low[j], raw[j], high[j], ALU.subtract).then_inc(s_low, 1)

            def split0(n):
                dve.wait_ge(s_high, n + 1)
                split(buf0(n))

            def split_next(e, i):
                dve.wait_ge(s_high, seq(e, i) + 1)
                split(buf(i))

            for u in range(7, 2 * NT - 1):
                base(u)
                if NT + 1 <= u <= NT + 3:
                    split0(u - NT - 1)

            def low8(dst, ready, n, done):
                dve.wait_ge(ready, n)
                for half in range(2):
                    k = slice(4 * half, 4 * half + 4)
                    last = nc.vector.tensor_tensor(
                        dst[1][:, k, :], ps[:, 6 + half, 0:4 * CAP].rearrange("p (k c) -> p k c", k=4),
                        dst[0][:, k, :], ALU.subtract)
                last.then_inc(done, 1)

            def rows_low(e):
                low8(xeT, s_xeT_h, e + 1, s_xeT)

            def hid_low(e):
                low8(hidT, s_hT_h, e + 1, s_hT)

            def hidden(e, first=False):
                dve.wait_ge(s_used, (2 * QC if first else seq(e, 2 * QC)))
                dve.wait_ge(s_hs, e + 1)
                nc.vector.tensor_tensor(hid, hid, ps[0:CAP, 2:4, :].rearrange("p b c -> p (b c)"),
                                        ALU.mult).then_inc(s_hid, 1)

            def ye_out(e, gate, first=False):
                if not first:
                    dve.wait_ge(s_scat, 16 * e)
                dve.wait_ge(s_used, seq(e + 2, 0) if not isinstance(e, int) or e < NE - 1 else seq(NE, QC))
                nc.vector.tensor_scalar(ye, ps[0:CAP, 4:6, :].rearrange("p b c -> p (b c)"), gate, None,
                                        ALU.mult).then_inc(s_ye, 1)

            dve.wait_ge(s_rowst, 16 * NT)
            dve.wait_ge(s_base, NT + 2)
            rows_low(0)
            base(2 * NT - 1)
            for n in range(3, FIRST):
                split0(n)
            dve.wait_ge(s_base, 2 * NT)
            split_next(1, 0)
            split_next(1, 1)
            rows_low(1)
            hidden(0, first=True)
            split_next(1, 2)
            for i in range(3, 7):
                split_next(1, i)
            hid_low(0)
            for i in range(7, 11):
                split_next(1, i)
            rows_low(2)
            hidden(1)
            split_next(1, 11)
            with dve.Fori(2, NE - 1) as e:
                for i in range(3):
                    split_next(e, i)
                ye_out(e - 2, gateT[:, bass.ds(e - 2, 1)])
                for i in range(3, 7):
                    split_next(e, i)
                hid_low(e - 1)
                for i in range(7, 11):
                    split_next(e, i)
                rows_low(e + 1)
                hidden(e)
                split_next(e, 11)
            for i in range(3):
                split_next(NE - 1, i)
            ye_out(NE - 3, gateT[:, NE - 3:NE - 2])
            for i in range(3, 7):
                split_next(NE - 1, i)
            hid_low(NE - 2)
            for i in range(7, 10):
                split_next(NE - 1, i)
            hidden(NE - 1)
            split_next(NE - 1, 10)
            low8(xeT, s_hT_h, NE, s_hT)
            split_next(NE - 1, 11)
            for q in range(3):
                split_next(NE, q)
            ye_out(NE - 2, gateT[:, NE - 2:NE - 1])
            split_next(NE, 3)
            ye_out(NE - 1, gateT[:, NE - 1:NE])

            def stats_half(t, half):
                dve.wait_ge(s_fin[t], 16)
                nc.vector.bn_stats(stats[:, t % 2, 6 * half:6 * half + 6],
                                   fin[:, t, half * 512:(half + 1) * 512]).then_inc(s_bn, 1)

            def moments(t):
                dve.wait_ge(s_bn, 2 * t + 2)
                nc.vector.bn_aggr(mv[:, t, :], stats[:, t % 2, :]).then_inc(s_mv, 1)

            def variance(t):
                dve.wait_ge(s_mv, t + 1)
                nc.vector.tensor_scalar(sd[:, 0, t:t + 1], mv[:, t, 1:2], LN_EPS, None, ALU.add).then_inc(s_var, 1)

            def inverse(t):
                nroot[0] += 1
                dve.wait_ge(s_std, nroot[0])
                nc.vector.reciprocal(sd[:, 1, t:t + 1], sd[:, 0, t:t + 1]).then_inc(s_inv, 1)

            def shift(t):
                dve.wait_ge(s_inv, t + 1)
                nc.vector.tensor_scalar(mv[:, t, 1:2], mv[:, t, 0:1], sd[:, 1, t:t + 1], -1.0, ALU.mult,
                                        ALU.mult).then_inc(s_ln_s, 1)

            def gain_half(t, half):
                dve.wait_ge(s_ln_z, t + 1)
                c = slice(half * 512, (half + 1) * 512)
                ins = nc.vector.tensor_tensor(fin[:, t, c], fin[:, t, c], gB[:, c], ALU.mult)
                if half:
                    ins.then_inc(s_ln_g, 1)

            dve.wait_ge(s_ln2, 32)
            stats_half(0, 0)
            stats_half(0, 1)
            moments(0)
            variance(0)
            stats_half(1, 0)
            inverse(0)
            stats_half(1, 1)
            shift(0)
            moments(1)
            variance(1)
            for t in range(NT):
                if t + 2 < NT:
                    stats_half(t + 2, 0)
                if t + 1 < NT:
                    inverse(t + 1)
                if t + 2 < NT:
                    stats_half(t + 2, 1)
                if t + 1 < NT:
                    shift(t + 1)
                gain_half(t, 0)
                if t + 2 < NT:
                    moments(t + 2)
                gain_half(t, 1)
                if t + 2 < NT:
                    variance(t + 2)
            dve.wait_ge(s_ln_g, NT)
            nc.vector.tensor_tensor(fin[:, NT - 1, :], fin[:, NT - 1, :], bB[:], ALU.add).then_inc(s_y2_last, 1)

        @block.tensor
        def _(pe):
            tr = [0]

            def unit(pairs, waits=()):
                n = tr[0]
                if n >= 2 and n < len(tr_units):
                    pe.wait_ge(*tr_units[n - 2])
                b = 2 * (n % 2)
                for half, lst in enumerate(pairs):
                    for col, src in lst:
                        k = src.shape[0]
                        w = 1
                        for s in src.shape[1:]:
                            w *= s
                        last = nc.tensor.transpose(ps[0:w, b + half, col:col + k], src, ident[0:k, 0:k])
                last.then_inc(s_tr, 1)
                tr[0] += 1

            def eight(src):
                return [[(j * P, src[:, (4 * half + j) * P:(4 * half + j + 1) * P]) for j in range(4)]
                        for half in range(2)]

            ng = [0]

            def group(g):
                n = ng[0]
                if n >= 4:
                    pe.wait_ge(s_projo, n - 1 if g[0] == "z" else n - 3)
                kind = g[0]
                bank = ps[:, 4 + (n % 2 if kind == "z" else n % 4), :]
                if kind == "xbc":
                    m, s = g[1], g[2]
                    a, w = SEQS[s]
                    wsl = slotk[2] if m < 4 else slotk[0]
                    for k in range(KD):
                        last = nc.tensor.matmul(bank[:, 0:w * P], wsl[:, k, (m % 4) * P:(m % 4 + 1) * P],
                                                xT[:, k, a * P:(a + w) * P], start=(k == 0), stop=(k == KD - 1))
                else:
                    t = g[1]
                    lhs = [xT[:, k, t * P:(t + 1) * P] for k in range(KD)]
                    if kind == "kv":
                        for k in range(KD):
                            last = nc.tensor.matmul(bank[:, 0:272], lhs[k], wkv[:, k, :], start=(k == 0),
                                                    stop=(k == KD - 1))
                    else:
                        w = slotk[0] if kind == "q" else slotk[1]
                        for k in range(KD):
                            last = nc.tensor.matmul(bank, lhs[k], w[:, k, :], start=(k == 0), stop=(k == KD - 1))
                last.then_inc(s_proj, 1)
                ng[0] += 1

            pe.wait_ge(s_const, 16 * 3)
            pe.wait_ge(s_xa, 1)
            unit(eight(xa[:, 0, :]))
            for t in range(NT):
                pe.wait_ge(s_xT, t + 1)
                if t == 0:
                    pe.wait_ge(s_slot[0], 16)
                group(("q", t))
                if t + 1 < NT:
                    pe.wait_ge(s_xa, t + 2)
                    unit(eight(xa[:, t + 1, :]))
                if t == 0:
                    pe.wait_ge(s_slot[1], 32)
                group(("kv", t))
            pe.wait_ge(s_param, 16 * 11)
            unit([[(m * (TAPS + 1), cw_rows[:, m * P:(m + 1) * P]) for m in range(KC)]])
            pe.wait_ge(s_slot[2], 16)
            for g in xbc_groups:
                if g == ("xbc", 4, 0):
                    pe.wait_ge(s_slot[0], 32)
                group(g)
            an = d16(ANEG)

            def cumulate():
                pe.wait_ge(s_a, 1)
                pe.wait_ge(s_projo, gidx["z", 0])
                pe.wait_ge(s_tab, 16)
                nc.tensor.matmul(ps[:, 6, 0:NT * NH], upto, an[:, :, 0:NH], start=True, stop=True)
                nc.tensor.matmul(ps[:, 6, NT * NH:2 * NT * NH], onward, an[:, :, NH:16], start=True, stop=True)
                pe.wait_ge(s_prep, 1)
                nc.tensor.matmul(ps[:, 7, 0:NT * 16], ones[:], dtw[:, ANEG, :], start=True,
                                 stop=True).then_inc(s_cum, 1)

            def x_token_major(t):
                c = conv_col(t)
                pe.wait_ge(s_silu, KC)
                unit([[(m * P, conv[:, m, c:c + P]) for m in range(4)],
                      [(m * P, conv[:, 4 + m, c:c + P]) for m in range(2)]])

            def chunk_state(n):
                d, t, g, i, first = upd[n]
                pe.wait_ge(s_ws, n + 1)
                pe.wait_ge(s_xB, NT)
                if n >= 2:
                    pe.wait_ge(s_sts, n - 1)
                else:
                    pe.wait_ge(s_cums, 1)
                nc.tensor.matmul(ps[:, 6 + n % 2, 0:256], btok[:, t, g * P:(g + 1) * P], xsc[:, n % 2, :],
                                 start=True, stop=True).then_inc(s_st, 1)

            pe.wait_ge(s_slot[1], 48)
            for t, g in enumerate(z_groups):
                group(g)
                if t == 0:
                    cumulate()
                elif t <= 3:
                    x_token_major(2 * t - 2)
                    x_token_major(2 * t - 1)
                else:
                    for n in range(len(upd) // 2):
                        chunk_state((t - 4) * len(upd) // 2 + n)
            for t in range(NT):
                pe.wait_ge(s_rope, t + 1)
                unit([[(j * P, mix[:, t, j * P:(j + 1) * P]) for j in range(4)], [(0, kvd[:, t, 0:P])]])

            def scores(u):
                t, h = att_units[u]
                a, n = seq_of[t]
                if u >= 3:
                    pe.wait_ge(s_exp, u - 2)
                nc.tensor.matmul(ps[:, u % 3, 0:n * P], qT[:, h % 4, t * P:(t + 1) * P],
                                 kz[:, h // 4, a * P:(a + n) * P], start=True, stop=True).then_inc(s_sc, 1)

            def turn(u):
                n = seq_of[att_units[u][0]][1]
                if u % 2:
                    pe.wait_ge(s_pna, u // 2 + 1)
                else:
                    pe.wait_ge(s_pn, u // 2 + 1)
                if u:
                    pe.wait_ge(s_pts, u)
                for b in range(n):
                    last = nc.tensor.transpose(ps[:, 3, b * P:(b + 1) * P], prob[:, u % 4, b * P:(b + 1) * P], ident)
                last.then_inc(s_pt, 1)

            def pv(G):
                a, n = seq_of[G // NKV]
                pe.wait_ge(s_pts, 4 * G + 4)
                if G:
                    pe.wait_ge(s_ao, G)
                for b in range(n):
                    last = nc.tensor.matmul(ps[:, 4, :], kvd[:, a + b, P:2 * P], probT[G % 2][:, b, :],
                                            start=(b == 0), stop=(b == n - 1))
                last.then_inc(s_pv, 1)

            def decay(n):
                t, g = ssd_units[n]
                if n:
                    pe.wait_ge(s_offm, n)
                    pe.wait_ge(s_edec, 2 * n)
                for d in range(2):
                    bank = ps[:, 5 + d, :]
                    for h in range(HPG):
                        c = d * NH + g * HPG + h
                        for i in range(2):
                            last = nc.tensor.matmul(bank[:, h * P:(h + 1) * P],
                                                    a_r[i][:, t, c:c + 1].broadcast_to([P, P]), tri_r[:, d, :],
                                                    start=(i == 0), stop=(i == 1))
                last.then_inc(s_dec, 1)

            def cb(n):
                t, g = ssd_units[n]
                cc = conv_col(t)
                if n:
                    pe.wait_ge(s_yo, n)
                nc.tensor.matmul(ps[:, 7, 0:P], conv[:, 4 + g, cc:cc + P],
                                 conv[:, 6 + g, cc:cc + P], start=True, stop=True).then_inc(s_cb, 1)

            def before(n):
                t, g = ssd_units[n]
                cc = conv_col(t)
                pe.wait_ge(s_edec, 2 * n + 2)
                for d in range(2):
                    if (d, t) in prev_at:
                        last = nc.tensor.matmul(ps[:, 5, d * 256:(d + 1) * 256], conv[:, 6 + g, cc:cc + P],
                                                state[:, d, g, prev_at[d, t], :], start=True, stop=True)
                last.then_inc(s_off, 1)

            def y(n):
                t, g = ssd_units[n]
                pe.wait_ge(s_m, n + 1)
                for h in range(HPG):
                    last = nc.tensor.matmul(ps[:, 7, h * HD:(h + 1) * HD], msum[:, h],
                                            xtok[:, t, (g * HPG + h) * HD:(g * HPG + h + 1) * HD],
                                            start=True, stop=True)
                last.then_inc(s_y, 1)

            pe.wait_ge(s_ar, 1)
            pe.wait_ge(s_qkT, NT)
            pe.wait_ge(s_projo, len(groups))
            pe.wait_ge(s_sts, len(upd))
            for i in range(NU + 4):
                if i < NU:
                    scores(i)
                if i % 4 == 0:
                    if i:
                        if i <= NU:
                            y(i // 4 - 1)
                    if i < NU:
                        decay(i // 4)
                if i % 4 == 2 and i < NU:
                    cb(i // 4)
                if 3 <= i < NU + 3:
                    turn(i - 3)
                if i % 4 == 3 and i < NU:
                    before(i // 4)
                if i >= 7 and i % 4 == 3:
                    pv((i - 7) // 4)

            assert tr[0] == 3 * NT + 1

            def mix_turn(t):
                pe.wait_ge(s_ssd, 2 * t + 2)
                if t >= 4:
                    pe.wait_ge(s_mixT, t - 3)
                for j in range(4):
                    last = nc.tensor.transpose(ps[:, t % 4, j * P:(j + 1) * P],
                                               mix[:, t, 512 + j * P:512 + (j + 1) * P], ident)
                last.then_inc(s_tr, 1)

            def out_proj(t, h):
                w, j, n = ((slotk[2], 2, 64), (slotk[0], 0, 80))[h]
                if t == 0:
                    pe.wait_ge(s_slot[j], n)
                if t >= 2 and h == 0:
                    pe.wait_ge(s_res, t - 1)
                for k in range(KD):
                    if k == 4:
                        pe.wait_ge(s_mixT, t + 1)
                    lhs = mix[:, t, k * P:(k + 1) * P] if k < 4 else xT[:, k, t * P:(t + 1) * P]
                    last = nc.tensor.matmul(ps[:, 4 + 2 * (t % 2) + h, :], lhs, w[:, k, :],
                                            start=(k == 0), stop=(k == KD - 1))
                if h == 1:
                    last.then_inc(s_o, 1)

            def x1_turn(t):
                pe.wait_ge(s_x1, t + 1)
                if t < 2:
                    pe.wait_ge(s_pT, 1)
                else:
                    pe.wait_ge(s_x1T, t - 1)
                b = 2 * (t % 2)
                for j in range(KD):
                    last = nc.tensor.transpose(ps[:, b + j // 4, (j % 4) * P:(j % 4 + 1) * P],
                                               xa[:, t, j * P:(j + 1) * P], ident)
                last.then_inc(s_tr, 1)

            def ple_unit(u):
                h, t = ple_units[u]
                if u == 0:
                    pe.wait_ge(s_x1T, NT - 1)
                    pe.wait_ge(s_slot[1], 64)
                    pe.wait_ge(s_bple, 32)
                    pe.wait_ge(s_wple, 16)
                if u >= 2:
                    pe.wait_ge(s_base, u - 1)
                if u == NT:
                    pe.wait_ge(s_slot[2], 80)
                w = slotk[1] if h == 0 else slotk[2]
                b = 2 * (u % 2)
                nc.tensor.matmul(ps[:, b, :], ones[0:1, :], bple[h], start=True, stop=False)
                for k in range(KD):
                    nc.tensor.matmul(ps[:, b, :], xT[:, k, t * P:(t + 1) * P], w[:, k, :],
                                     start=False, stop=(k == KD - 1))
                for k in range(2):
                    last = nc.tensor.matmul(ps[:, b + 1, :], pT[:, k, t * P:(t + 1) * P],
                                            wple[:, k, h * 512:(h + 1) * 512], start=(k == 0), stop=(k == 1))
                last.then_inc(s_pg, 1)

            pe.wait_ge(s_pts, NU)
            for t in range(4):
                mix_turn(t)
            pe.wait_ge(s_ao, NG)
            pe.wait_ge(s_yo, NG)
            out_proj(0, 0)
            out_proj(1, 0)
            mix_turn(4)
            mix_turn(5)
            out_proj(0, 1)
            out_proj(1, 1)
            pe.wait_ge(s_ple_in, 32)
            pe.wait_ge(s_mixT, NT)
            for b in range(3):
                for k in range(2):
                    for i in range(2):
                        last = nc.tensor.transpose(ps[:, b, k * 256 + i * P:k * 256 + (i + 1) * P],
                                                   ptok[:, 2 * b + i, k * P:(k + 1) * P], ident)
            last.then_inc(s_tr, 1)
            for t in range(2, NT):
                out_proj(t, 0)
                if t == 2:
                    x1_turn(0)
                out_proj(t, 1)
                x1_turn(t - 1)
            ple_unit(0)
            x1_turn(NT - 1)
            pe.wait_ge(s_x1T, NT)
            for b, c0, c1 in ((4, 0, 512), (5, 512, T)):
                for k in range(KD):
                    last = nc.tensor.matmul(ps[0:NE, b, 0:c1 - c0], wr[:, k, :], xT[:, k, c0:c1],
                                            start=(k == 0), stop=(k == KD - 1))
            last.then_inc(s_lg, 1)
            ple_unit(1)
            pe.wait_ge(s_lgT, 1)
            for t in range(NT):
                last = nc.tensor.transpose(ps[:, 6, t * NE:(t + 1) * NE], logitsT[:, t * P:(t + 1) * P],
                                           ident[0:NE, 0:NE])
            last.then_inc(s_lg, 1)
            ple_unit(2)
            pe.wait_ge(s_lgd, 2)
            for t in range(NT):
                last = nc.tensor.transpose(ps[0:NE, 6 + t // 4, (t % 4) * P:(t % 4 + 1) * P],
                                           rt[:, 0, t * NE:(t + 1) * NE], ident)
            last.then_inc(s_affT, 1)
            for u in range(3, 6):
                ple_unit(u)
            pe.wait_ge(s_top, 1)
            nc.tensor.transpose(ps[0:CAP, 5, 0:NE], topf[:], ident[0:NE, 0:NE])
            nc.tensor.transpose(ps[0:CAP, 5, NE:2 * NE], topv[:], ident[0:NE, 0:NE]).then_inc(s_topT, 1)
            for u in range(6, 2 * NT - 1):
                ple_unit(u)

            def turn8(src, done):
                for j in range(KD):
                    last = nc.tensor.transpose(ps[:, 6 + j // 4, (j % 4) * CAP:(j % 4 + 1) * CAP],
                                               src[:, j * P:(j + 1) * P], ident[0:CAP, 0:CAP])
                last.then_inc(done, 1)

            def rows_turn(e):
                pe.wait_ge(s_gath, 16 * (e + 1))
                turn8(xe, s_xeT_p)

            def hid_turn(e):
                pe.wait_ge(s_hid, e + 1)
                turn8(hid, s_hT_p)

            def chunk(lhs, bank, q, j, n):
                pe.wait_ge(s_low, n + 1)
                for i in range(2):
                    k = 2 * q + i
                    for h in range(2):
                        c = slice(i * D + h * 512, i * D + (h + 1) * 512)
                        o = ps[0:CAP, bank + h, :]
                        nc.tensor.matmul(o, lhs[0][:, k, :], high[j][:, c], start=(k == 0), stop=False)
                        nc.tensor.matmul(o, lhs[0][:, k, :], low[j][:, c], start=False, stop=False)
                        last = nc.tensor.matmul(o, lhs[1][:, k, :], high[j][:, c], start=False,
                                                stop=(k == KD - 1))
                last.then_inc(s_used, 1)

            def gate(e):
                pe.wait_ge(s_xeT, e + 1)
                pe.wait_ge(s_hs, e)
                for q in range(QC):
                    chunk(xeT, 0, q, buf(q), seq(e, q))

            def up(e):
                pe.wait_ge(s_hid, e)
                for q in range(QC):
                    chunk(xeT, 2, q, buf(QC + q), seq(e, QC + q))

            def down(e, first=False, mid=None):
                pe.wait_ge(s_hT, e + 1)
                if not first:
                    pe.wait_ge(s_ye, e)
                for q in range(QC):
                    if q == QC // 2 and mid:
                        mid()
                    chunk(hidT, 4, q, buf(2 * QC + q), seq(e + 1, 2 * QC + q))

            pe.wait_ge(s_idx, 2)
            rows_turn(0)
            ple_unit(2 * NT - 1)
            pe.wait_ge(s_base, 2 * NT - 1)
            pe.wait_ge(s_xeT, 1)
            for q in range(QC):
                chunk(xeT, 0, q, buf0(q), q)
            pe.wait_ge(s_base, 2 * NT)
            for q in range(QC):
                chunk(xeT, 2, q, buf0(QC + q), QC + q)
            rows_turn(1)
            gate(1)
            hid_turn(0)
            up(1)
            pe.wait_ge(s_hT, 1)
            rows_turn(2)
            down(0, first=True)
            with pe.Fori(2, NE - 1) as e:
                gate(e)
                hid_turn(e - 1)
                up(e)
                pe.wait_ge(s_hT, e)
                rows_turn(e + 1)
                down(e - 1)
            gate(NE - 1)
            hid_turn(NE - 2)
            up(NE - 1)
            down(NE - 2, mid=lambda: hid_turn(NE - 1))
            pe.wait_ge(s_hT, NE)
            pe.wait_ge(s_ye, NE - 1)
            for q in range(QC):
                chunk(xeT, 4, q, buf(q), seq(NE, q))


NAMES = ["x_prompt", "x_sample", "p_prompt", "p_sample", "ln_in_g", "ln_in_b", "w_in", "q_norm_w",
         "k_norm_w", "conv_w", "conv_b", "dt_bias", "a_log", "d_skip", "ssd_norm_w", "w_out", "ln1_g",
         "ln1_b", "w_router", "w_e_gate", "w_e_up", "w_e_down", "w_ple_gate", "b_ple_gate", "w_ple",
         "ln2_g", "ln2_b"]


def kernel(**inputs):
    import concourse.bacc as bacc
    from concourse.bass_utils import run_bass_kernel_spmd

    nc = bacc.Bacc("TRN2", target_bir_lowering=False, num_devices=1)
    arrays, A = {}, {}
    for name in NAMES:
        a = np.ascontiguousarray(inputs[name])
        arrays[f"in_{name}"] = a
        A[name] = nc.dram_tensor(f"in_{name}", a.shape, mybir.dt.from_np(a.dtype), kind="ExternalInput").ap()
    lengths = (inputs["x_prompt"].shape[1], inputs["x_sample"].shape[1])
    c = shape_constants(lengths)
    arrays["shape_constants"] = c
    consts = nc.dram_tensor("shape_constants", c.shape, F32, kind="ExternalInput").ap()
    outs = [nc.dram_tensor(f"out_{i}", (1, n, D), F32, kind="ExternalOutput").ap()
            for i, n in enumerate(lengths)]
    hymba_layer(nc, A, consts, *outs)
    r = run_bass_kernel_spmd(nc, [arrays], core_ids=[0])
    return tuple(r.results[0][f"out_{i}"] for i in range(2))
```
